# Optimizing a Trainium2 kernel written in Bass

```python
import math
import numpy as np
import jax
import jax.numpy as jnp
from jax import lax

D_MODEL = 1024
BATCH = 1
SEQ = 512
DEPTH = 1

DN_ALPHA = (2.0 * DEPTH) ** 0.25
DN_BETA = (8.0 * DEPTH) ** -0.25
LN_EPS = 1e-5
NEG = -1e30
BIG = 1e6

POOL_WINDOWS = (2, 4, 8, 16)
POOL_GROUP = D_MODEL // 8
POOL_WIDTH = POOL_GROUP * len(POOL_WINDOWS)

NSA_HEAD_DIM = 64
NSA_HEADS = D_MODEL // 128
NSA_KV_HEADS = 2
NSA_HPG = NSA_HEADS // NSA_KV_HEADS
NSA_WIDTH = NSA_HEADS * NSA_HEAD_DIM
NSA_KV_WIDTH = 3 * 2 * NSA_KV_HEADS * NSA_HEAD_DIM
CMP_LEN = 32
CMP_STRIDE = 16
CMP_HIDDEN = 2 * NSA_HEAD_DIM
SLC_LEN = 64
SLC_TOPN = 8
WIN_LEN = 512
Q_BLOCK = 128

REL_BUCKETS = 32
REL_MAX_DIST = 128

SSD_D_INNER = D_MODEL
SSD_HEAD_DIM = 64
SSD_HEADS = SSD_D_INNER // SSD_HEAD_DIM
SSD_GROUPS = 4
SSD_HPG = SSD_HEADS // SSD_GROUPS
SSD_STATE = 128
SSD_CONV = 4
SSD_CHUNK = 128
SSD_XBC = SSD_D_INNER + 2 * SSD_GROUPS * SSD_STATE
SSD_IN_WIDTH = SSD_D_INNER + SSD_XBC + SSD_HEADS

N_EXPERTS = 16
N_EXPERT_GROUPS = 4
EXPERTS_PER_GROUP = N_EXPERTS // N_EXPERT_GROUPS
TOP_K = 2
D_EXPERT = 512

IN_SPLITS = (POOL_WIDTH, NSA_WIDTH, NSA_KV_WIDTH, 3 * NSA_HEADS, SSD_IN_WIDTH, 3 * D_MODEL)
D_IN = POOL_WIDTH + NSA_WIDTH + NSA_KV_WIDTH + 3 * NSA_HEADS + SSD_IN_WIDTH + 3 * D_MODEL

kernel_name = 'hybrid_pool_nsa_ssd_moe_deepnorm'

def layer_norm(x, g, b):
    xf = x.astype(jnp.float32)
    mu = jnp.mean(xf, -1, keepdims=True)
    var = jnp.mean(jnp.square(xf - mu), -1, keepdims=True)
    return ((xf - mu) * lax.rsqrt(var + LN_EPS) * g + b).astype(x.dtype)

def rel_bucket(dist):
    n = jnp.maximum(dist, 0)
    max_exact = REL_BUCKETS // 2
    nf = jnp.maximum(n, 1).astype(jnp.float32)
    large = max_exact + (jnp.log(nf / max_exact) / math.log(REL_MAX_DIST / max_exact)
                         * (REL_BUCKETS - max_exact)).astype(jnp.int32)
    large = jnp.minimum(large, REL_BUCKETS - 1)
    return jnp.where(n < max_exact, n, large)

def masked_softmax(s, mask):
    p = jax.nn.softmax(jnp.where(mask, s.astype(jnp.float32), NEG), axis=-1)
    return p * mask

def pool_mixer(u, w_grp, scale):
    bsz, s, _ = u.shape
    uf = u.astype(jnp.float32)
    csum = jnp.concatenate([jnp.zeros_like(uf[:, :1]), jnp.cumsum(uf, axis=1)], axis=1)
    t = jnp.arange(s)
    outs = []
    for gi, w in enumerate(POOL_WINDOWS):
        sl = slice(gi * POOL_GROUP, (gi + 1) * POOL_GROUP)
        lo = jnp.maximum(t + 1 - w, 0)
        cnt = jnp.minimum(t + 1, w).astype(jnp.float32)
        mean = (csum[:, 1:, sl] - csum[:, lo, sl]) / cnt[None, :, None]
        outs.append(mean - uf[..., sl])
    r = jnp.stack(outs, axis=2).astype(u.dtype)
    y = jnp.einsum('bsgc,gcd->bsgd', r, w_grp).reshape(bsz, s, POOL_WIDTH)
    return y * scale

def nsa_mixer(q, kv, gate_logits, pe_k, w1_k, w2_k, pe_v, w1_v, w2_v, rel_bias):
    bsz, s, _ = q.shape
    G, hpg, dh = NSA_KV_HEADS, NSA_HPG, NSA_HEAD_DIM
    q = q.reshape(bsz, s, G, hpg, dh) * (dh ** -0.5)
    kv = kv.reshape(bsz, s, 3, 2, G, dh)
    k_cmp_tok, v_cmp_tok = kv[:, :, 0, 0], kv[:, :, 0, 1]
    k_slc, v_slc = kv[:, :, 1, 0], kv[:, :, 1, 1]
    k_win, v_win = kv[:, :, 2, 0], kv[:, :, 2, 1]
    gates = jax.nn.sigmoid(gate_logits.astype(jnp.float32)).reshape(bsz, s, 3, G, hpg).astype(q.dtype)
    tbl = rel_bias.astype(jnp.float32).reshape(REL_BUCKETS, G, hpg)

    n_cmp = (s - CMP_LEN) // CMP_STRIDE + 1
    cidx = np.arange(n_cmp)[:, None] * CMP_STRIDE + np.arange(CMP_LEN)[None, :]

    def compress(tok, pe, w1, w2):
        blk = tok[:, cidx] + pe[None, None, :, None, :]
        blk = blk.transpose(0, 1, 3, 2, 4).reshape(bsz, n_cmp, G, CMP_LEN * dh)
        return jax.nn.gelu(blk @ w1) @ w2

    k_c = compress(k_cmp_tok, pe_k, w1_k, w2_k)
    v_c = compress(v_cmp_tok, pe_v, w1_v, w2_v)
    cmp_end = jnp.arange(n_cmp) * CMP_STRIDE + CMP_LEN - 1

    n_slc = s // SLC_LEN
    n_top = min(SLC_TOPN, n_slc)
    c0 = np.arange(n_cmp) * CMP_STRIDE
    s0s = np.arange(n_slc) * SLC_LEN
    ov = np.clip(np.minimum(c0[:, None] + CMP_LEN, s0s[None, :] + SLC_LEN)
                 - np.maximum(c0[:, None], s0s[None, :]), 0, None) / CMP_LEN
    overlap = jnp.asarray(ov, dtype=jnp.float32)
    kb = k_slc.reshape(bsz, n_slc, SLC_LEN, G, dh).transpose(0, 3, 1, 2, 4)
    vb = v_slc.reshape(bsz, n_slc, SLC_LEN, G, dh).transpose(0, 3, 1, 2, 4)
    gather_blocks = jax.vmap(jax.vmap(lambda blocks, ids: blocks[ids]))

    pad = ((0, 0), (WIN_LEN, 0), (0, 0), (0, 0))
    k_wp = jnp.pad(k_win, pad)
    v_wp = jnp.pad(v_win, pad)
    span = WIN_LEN + Q_BLOCK
    jpos = jnp.arange(n_slc)

    def block(bi):
        st = bi * Q_BLOCK
        t = st + jnp.arange(Q_BLOCK)
        qb = lax.dynamic_slice_in_dim(q, st, Q_BLOCK, axis=1)
        gb = lax.dynamic_slice_in_dim(gates, st, Q_BLOCK, axis=1)
        dist_c = t[:, None] - cmp_end[None, :]
        sc = jnp.einsum('bqghd,bngd->bghqn', qb, k_c).astype(jnp.float32) \
            + tbl[rel_bucket(dist_c)].transpose(2, 3, 0, 1)
        p_c = masked_softmax(sc, dist_c >= 0)
        o_c = jnp.einsum('bghqn,bngd->bqghd', p_c.astype(v_c.dtype), v_c)
        imp = jnp.einsum('bghqn,nj->bgqj', p_c, overlap)
        jt = t // SLC_LEN
        valid = jpos[None, :] * SLC_LEN <= t[:, None]
        forced = (jpos[None, :] == 0) | (jpos[None, :] == jt[:, None]) | (jpos[None, :] == jt[:, None] - 1)
        imp = jnp.where(forced, BIG, jnp.where(valid, imp, -BIG))
        _, sel = lax.top_k(imp, n_top)
        k_sel = gather_blocks(kb, sel).reshape(bsz, G, Q_BLOCK, n_top * SLC_LEN, dh)
        v_sel = gather_blocks(vb, sel).reshape(bsz, G, Q_BLOCK, n_top * SLC_LEN, dh)
        kpos = (sel[..., None] * SLC_LEN + jnp.arange(SLC_LEN)).reshape(bsz, G, Q_BLOCK, n_top * SLC_LEN)
        dist_s = t[None, None, :, None] - kpos
        bias_s = jax.vmap(lambda tb, bk: tb[bk], in_axes=(1, 1), out_axes=1)(tbl, rel_bucket(dist_s))
        ss = jnp.einsum('bqghd,bgqkd->bghqk', qb, k_sel).astype(jnp.float32) + jnp.moveaxis(bias_s, -1, 2)
        p_s = masked_softmax(ss, (dist_s >= 0)[:, :, None])
        o_s = jnp.einsum('bghqk,bgqkd->bqghd', p_s.astype(v_sel.dtype), v_sel)
        kw = lax.dynamic_slice_in_dim(k_wp, st, span, axis=1)
        vw = lax.dynamic_slice_in_dim(v_wp, st, span, axis=1)
        kpos_w = st - WIN_LEN + jnp.arange(span)
        dist_w = t[:, None] - kpos_w[None, :]
        mask_w = (dist_w >= 0) & (dist_w < WIN_LEN) & (kpos_w[None, :] >= 0)
        sw = jnp.einsum('bqghd,bkgd->bghqk', qb, kw).astype(jnp.float32) \
            + tbl[rel_bucket(dist_w)].transpose(2, 3, 0, 1)
        p_w = masked_softmax(sw, mask_w)
        o_w = jnp.einsum('bghqk,bkgd->bqghd', p_w.astype(vw.dtype), vw)
        return (gb[:, :, 0, ..., None] * o_c + gb[:, :, 1, ..., None] * o_s
                + gb[:, :, 2, ..., None] * o_w)

    out = lax.map(block, jnp.arange(s // Q_BLOCK))
    return out.transpose(1, 0, 2, 3, 4, 5).reshape(bsz, s, NSA_WIDTH)

def ssd_mixer(zxbcdt, conv_w, conv_b, dt_bias, a_log, d_skip, norm_g):
    bsz, s, _ = zxbcdt.shape
    G, E, P, N, L = SSD_GROUPS, SSD_HPG, SSD_HEAD_DIM, SSD_STATE, SSD_CHUNK
    nc = s // L
    z = zxbcdt[..., :SSD_D_INNER]
    xbc = zxbcdt[..., SSD_D_INNER:SSD_D_INNER + SSD_XBC]
    dt = zxbcdt[..., SSD_D_INNER + SSD_XBC:]
    xbc = lax.conv_general_dilated(xbc, conv_w[:, None, :], window_strides=(1,),
                                   padding=[(SSD_CONV - 1, 0)],
                                   dimension_numbers=('NWC', 'WIO', 'NWC'),
                                   feature_group_count=SSD_XBC) + conv_b
    xbc = jax.nn.silu(xbc)
    xs = xbc[..., :SSD_D_INNER].reshape(bsz, s, G, E, P)
    Bc = xbc[..., SSD_D_INNER:SSD_D_INNER + G * N].reshape(bsz, nc, L, G, N)
    Cc = xbc[..., SSD_D_INNER + G * N:].reshape(bsz, nc, L, G, N)
    dt = jax.nn.softplus(dt.astype(jnp.float32) + dt_bias)
    A = -jnp.exp(a_log.astype(jnp.float32))
    a = (dt * A).reshape(bsz, nc, L, G, E)
    xdt = (xs * dt.reshape(bsz, s, G, E)[..., None]).reshape(bsz, nc, L, G, E, P)
    acs = jnp.cumsum(a, axis=2)
    acs_t = jnp.moveaxis(acs, 2, -1)
    tri = jnp.tril(jnp.ones((L, L), dtype=bool))
    seg = jnp.exp(jnp.where(tri, acs_t[..., :, None] - acs_t[..., None, :], -jnp.inf))
    cb = jnp.einsum('bclgn,bcsgn->bcgls', Cc, Bc)
    y_diag = jnp.einsum('bcgls,bcgels,bcsgep->bclgep', cb, seg, xdt)
    decay_in = jnp.exp(acs[:, :, -1:] - acs)
    states = jnp.einsum('bclgn,bclge,bclgep->bcgepn', Bc, decay_in, xdt)
    chunk_decay = jnp.exp(acs[:, :, -1])

    def step(h, inp):
        dec, st = inp
        return dec[..., None, None] * h + st, h

    _, h_in = lax.scan(step, jnp.zeros_like(states[:, 0]),
                       (jnp.moveaxis(chunk_decay, 1, 0), jnp.moveaxis(states, 1, 0)))
    h_in = jnp.moveaxis(h_in, 0, 1)
    y_off = jnp.einsum('bclgn,bcgepn,bclge->bclgep', Cc, h_in, jnp.exp(acs))
    y = (y_diag + y_off).reshape(bsz, s, G, E, P) + xs * d_skip.reshape(G, E)[..., None]
    y = y.reshape(bsz, s, SSD_D_INNER) * jax.nn.silu(z.astype(jnp.float32))
    yg = y.reshape(bsz, s, SSD_GROUPS, -1)
    yg = yg * lax.rsqrt(jnp.mean(yg * yg, -1, keepdims=True) + LN_EPS)
    return (yg.reshape(bsz, s, SSD_D_INNER) * norm_g).astype(zxbcdt.dtype)

def moe(x, router_w, router_b, w1, w3, w2):
    bsz, s, d = x.shape
    xt = x.reshape(-1, d)
    probs = jax.nn.softmax((xt @ router_w).astype(jnp.float32), axis=-1)
    sel_score = (probs + router_b).reshape(-1, N_EXPERT_GROUPS, EXPERTS_PER_GROUP)
    grp_score = jnp.sum(lax.top_k(sel_score, TOP_K)[0], axis=-1)
    grp = jnp.argmax(grp_score, axis=-1)
    in_grp = grp[:, None] == jnp.arange(N_EXPERT_GROUPS)[None, :]
    masked = jnp.where(in_grp[..., None], sel_score, -jnp.inf).reshape(-1, N_EXPERTS)
    _, idx = lax.top_k(masked, TOP_K)
    wsel = jnp.take_along_axis(probs, idx, axis=-1)
    wsel = wsel / jnp.sum(wsel, -1, keepdims=True)
    combine = jnp.sum(jax.nn.one_hot(idx, N_EXPERTS, dtype=jnp.float32) * wsel[..., None], axis=1)
    y = jnp.zeros(xt.shape, jnp.float32)
    for e in range(N_EXPERTS):
        h = jax.nn.silu(xt @ w1[e]) * (xt @ w3[e])
        y = y + combine[:, e:e + 1] * (h @ w2[e])
    return y.reshape(bsz, s, d).astype(x.dtype)

def setup_inputs(seed: int = 0) -> dict:
    key = jax.random.key(seed)
    ks = iter(jax.random.split(key, 40))

    def nrm(shape, scale):
        return scale * jax.random.normal(next(ks), shape, jnp.float32)

    Ld = DEPTH
    dt0 = jnp.exp(jax.random.uniform(next(ks), (Ld, SSD_HEADS), jnp.float32)
                  * (math.log(0.1) - math.log(0.001)) + math.log(0.001))
    return {
        'x': nrm((BATCH, SEQ, D_MODEL), 1.0),
        'ln0_g': 1.0 + nrm((D_MODEL,), 0.1),
        'ln0_b': nrm((D_MODEL,), 0.02),
        'w_in': nrm((Ld, D_MODEL, D_IN), D_MODEL ** -0.5),
        'pool_w': nrm((Ld, len(POOL_WINDOWS), POOL_GROUP, POOL_GROUP), POOL_GROUP ** -0.5),
        'pool_scale': 1.0 + nrm((Ld, POOL_WIDTH), 0.1),
        'cmp_k_pe': nrm((Ld, CMP_LEN, NSA_HEAD_DIM), 0.1),
        'cmp_k_w1': nrm((Ld, CMP_LEN * NSA_HEAD_DIM, CMP_HIDDEN), (CMP_LEN * NSA_HEAD_DIM) ** -0.5),
        'cmp_k_w2': nrm((Ld, CMP_HIDDEN, NSA_HEAD_DIM), CMP_HIDDEN ** -0.5),
        'cmp_v_pe': nrm((Ld, CMP_LEN, NSA_HEAD_DIM), 0.1),
        'cmp_v_w1': nrm((Ld, CMP_LEN * NSA_HEAD_DIM, CMP_HIDDEN), (CMP_LEN * NSA_HEAD_DIM) ** -0.5),
        'cmp_v_w2': nrm((Ld, CMP_HIDDEN, NSA_HEAD_DIM), CMP_HIDDEN ** -0.5),
        'rel_bias': nrm((REL_BUCKETS, NSA_HEADS), 0.3),
        'conv_w': nrm((Ld, SSD_CONV, SSD_XBC), SSD_CONV ** -0.5),
        'conv_b': nrm((Ld, SSD_XBC), 0.02),
        'dt_bias': dt0 + jnp.log(-jnp.expm1(-dt0)),
        'a_log': jnp.log(jax.random.uniform(next(ks), (Ld, SSD_HEADS), jnp.float32, 1.0, 16.0)),
        'd_skip': 1.0 + nrm((Ld, SSD_HEADS), 0.1),
        'ssd_norm_g': 1.0 + nrm((Ld, SSD_D_INNER), 0.1),
        'w_br_pool': nrm((Ld, POOL_WIDTH, D_MODEL), POOL_WIDTH ** -0.5),
        'w_br_nsa': nrm((Ld, NSA_WIDTH, D_MODEL), NSA_WIDTH ** -0.5),
        'w_br_ssd': nrm((Ld, SSD_D_INNER, D_MODEL), SSD_D_INNER ** -0.5),
        'w_out': nrm((Ld, D_MODEL, D_MODEL), DN_BETA * D_MODEL ** -0.5),
        'ln1_g': 1.0 + nrm((Ld, D_MODEL), 0.1),
        'ln1_b': nrm((Ld, D_MODEL), 0.02),
        'router_w': nrm((D_MODEL, N_EXPERTS), D_MODEL ** -0.5),
        'router_b': nrm((N_EXPERTS,), 0.01),
        'exp_w1': nrm((Ld, N_EXPERTS, D_MODEL, D_EXPERT), D_MODEL ** -0.5),
        'exp_w3': nrm((Ld, N_EXPERTS, D_MODEL, D_EXPERT), D_MODEL ** -0.5),
        'exp_w2': nrm((Ld, N_EXPERTS, D_EXPERT, D_MODEL), DN_BETA * D_EXPERT ** -0.5),
        'ln2_g': 1.0 + nrm((Ld, D_MODEL), 0.1),
        'ln2_b': nrm((Ld, D_MODEL), 0.02),
    }

def reference(x, ln0_g, ln0_b, w_in, pool_w, pool_scale, cmp_k_pe, cmp_k_w1, cmp_k_w2,
              cmp_v_pe, cmp_v_w1, cmp_v_w2, rel_bias, conv_w, conv_b, dt_bias, a_log, d_skip,
              ssd_norm_g, w_br_pool, w_br_nsa, w_br_ssd, w_out, ln1_g, ln1_b, router_w, router_b,
              exp_w1, exp_w3, exp_w2, ln2_g, ln2_b):
    split_points = np.cumsum(IN_SPLITS)[:-1].tolist()
    h = layer_norm(x, ln0_g, ln0_b)
    for i in range(DEPTH):
        proj = h @ w_in[i]
        u_pool, u_q, u_kv, u_ng, u_ssd, u_gate = jnp.split(proj, split_points, axis=-1)
        br_a = pool_mixer(u_pool, pool_w[i], pool_scale[i]) @ w_br_pool[i]
        br_b = nsa_mixer(u_q, u_kv, u_ng, cmp_k_pe[i], cmp_k_w1[i], cmp_k_w2[i],
                         cmp_v_pe[i], cmp_v_w1[i], cmp_v_w2[i], rel_bias) @ w_br_nsa[i]
        br_c = ssd_mixer(u_ssd, conv_w[i], conv_b[i], dt_bias[i], a_log[i], d_skip[i],
                         ssd_norm_g[i]) @ w_br_ssd[i]
        g_a, g_b, g_c = jnp.split(jax.nn.sigmoid(u_gate), 3, axis=-1)
        mix = (g_a * br_a + g_b * br_b + g_c * br_c) @ w_out[i]
        h = layer_norm(DN_ALPHA * h + mix, ln1_g[i], ln1_b[i])
        h = layer_norm(DN_ALPHA * h + moe(h, router_w, router_b, exp_w1[i], exp_w3[i], exp_w2[i]),
                       ln2_g[i], ln2_b[i])
    return h


_drawn_inputs = setup_inputs


def setup_inputs(seed=0):
    import zlib

    import numpy as np

    out = dict(_drawn_inputs(seed))
    spreads = {}
    factors = {'cmp_k_pe': 4.644, 'cmp_v_pe': 2.671, 'ln2_b': 2.908}
    for name, (base, spread) in spreads.items():
        noise = np.random.default_rng([zlib.crc32(name.encode()), seed]).standard_normal(out[name].shape)
        drawn = base * np.exp(spread * noise) if base else spread * noise
        out[name] = jnp.asarray(drawn.astype(out[name].dtype))
    for name, factor in factors.items():
        out[name] = (out[name] * factor).astype(out[name].dtype)
    return out
```

```python
import math
from contextlib import ExitStack

import numpy as np
import concourse.bass as bass
from concourse import mybir

F32 = mybir.dt.float32
ALU = mybir.AluOpType
ACT = mybir.ActivationFunctionType
AX = mybir.AxisListType

P = 128
T = 512
D = 1024
TB = T // P
KT = D // P
ALPHA = 2.0 ** 0.25
LN_EPS = 1e-5
NEG = -1e30

HEADS, KVG, HPG, DH = 8, 2, 4, 64
BUCKETS = 32
MAX_DIST = 128
CMP_LEN, CMP_STRIDE = 32, 16
NCMP = (T - CMP_LEN) // CMP_STRIDE + 1
WINDOWS = (2, 4, 8, 16)

SG, SE, SP, SN = 4, 4, 64, 128
SH = SG * SE
NE, DE = 16, 512
FT = DE // P

CM_PROJ = 28
BR_TILES = 5
SLOTS = 5
VD = 2 * P + SH + 3 * HEADS
REVN = T + P

C_LN0G, C_LN0B, C_LN1G, C_LN1B, C_PS, C_CW, C_CB, C_NG, C_PEK, C_PEV, C_END = (
    0, 8, 16, 24, 32, 36, 100, 116, 124, 140, 156)
K_ID, K_TRI, K_CAP, K_AID, K_ONE, K_ROW, K_LOW, K_INV, K_END = 0, 128, 256, 384, 512, 640, 641, 657, 721
R_DTB, R_ALOG, R_DSK, R_RB = 0, 16, 32, 48


def build_program(nc, x, w_cm, w_tm, w_vd, cols, rows, lnrows, fixed, onehot, table, pool_w, w1c_in, w2kv,
                  w_out, w_rt, e13, e2, out, bias_dram):
    with ExitStack() as ctx:
        def sb(name, shape):
            return ctx.enter_context(nc.sbuf_tensor(name, shape, F32))

        def sem(name):
            return ctx.enter_context(nc.semaphore(name))

        bank = [ctx.enter_context(nc.psum_tensor(f"bank{i}", [P, 512], F32)) for i in range(8)]

        r_h = sb("r_h", [P, 4096])
        r_ring = sb("r_ring", [P, SLOTS * D])
        r_big = sb("r_big", [P, 6 * 4096])
        r_qkv = sb("r_qkv", [P, 4096])
        r_tmp = sb("r_tmp", [P, 5632])
        r_o = sb("r_o", [P, 2048])
        r_oT = sb("r_oT", [P, 2048])
        r_pool = sb("r_pool", [P, 2048])
        colv = sb("colv", [P, C_END])
        fix = sb("fix", [P, K_END])
        rowv = sb("rowv", [P, 4 * SH])
        small = sb("small", [P, 1280])
        vbd = sb("vbd", [P, KVG, HPG, DH])
        kcT = sb("kcT", [P, NCMP])

        def view(region, off, *dims):
            v = region[:, off:off + int(np.prod(dims))]
            names = "abcde"[:len(dims)]
            if len(dims) == 1:
                return v
            return v.rearrange(f"p ({' '.join(names)}) -> p {' '.join(names)}",
                               **{n: d for n, d in zip(names[1:], dims[1:])})

        hT = view(r_h, 0, KT, T)
        ysum = view(r_h, 0, TB, D)
        ring = view(r_ring, 0, SLOTS, KT, P)
        h1T = view(r_ring, 0, KT, T)
        zs = view(r_big, 0, TB, D)
        ytok = view(r_big, 4096, TB, D)
        xsT = view(r_big, 8192, 8, T)
        yT = view(r_big, 12288, 8, T)
        bcT = view(r_big, 16384, 8, T)
        strips = view(r_big, 20480, HEADS, T)
        btok = view(r_big, 20480, TB, SG, SN)
        xin = view(r_big, 0, TB, D)
        xnorm = view(r_big, 4096, TB, D)
        wz = [view(r_big, 12288, KT, 512), view(r_big, 4096, KT, 512)]
        wvd = view(r_big, 8192, KT, VD)
        w1c = view(r_big, 16384, 2, 16, P)
        wo = view(r_big, 16384, 2, KT, 512)
        qT = view(r_qkv, 0, 4, T)
        kT = [view(r_qkv, 2048, T), view(r_qkv, 2560, T)]
        vtok = view(r_qkv, 3072, TB, 2, KVG, DH)
        mT = view(r_qkv, 0, KT, T)
        tok2 = view(r_o, 0, 2, KVG, T)
        oacc = view(r_o, 0, TB, HEADS, DH)
        oT = view(r_oT, 0, 4, T)
        pcs = view(r_oT, 0, TB, HEADS, 32)
        pct = view(r_oT, 1024, 2, 2, P)
        poolT = view(r_pool, 0, 4, T)

        ident, tri, cap, aident, ones = (fix[:, k:k + P] for k in (K_ID, K_TRI, K_CAP, K_AID, K_ONE))
        rowok = fix[:, K_ROW:K_ROW + 1]
        lower = fix[:, K_LOW:K_LOW + 16].rearrange("p (i j) -> p i j", i=4)
        invc = fix[:, K_INV:K_INV + 64].rearrange("p (g w) -> p g w", g=4)

        used = [0]

        def sm(*dims):
            n = int(np.prod(dims))
            used[0] += n
            assert used[0] <= 1280
            return view(small, used[0] - n, *dims)

        stats, mv, sdev, rstd = sm(TB, 2, 6), sm(TB, 2), sm(TB), sm(TB)
        dtx, dtm, dte, dt, dta = sm(TB, SH), sm(TB, SH), sm(TB, SH), sm(TB, SH), sm(TB, SH)
        acs, negacs, eacs, decin, cdec = sm(TB, SH), sm(TB, SH), sm(TB, SH), sm(TB, SH), sm(TB, SH)
        expa = sm(SH)
        ngate = sm(TB, 3, HEADS)
        nmax, psums = sm(2, TB, HEADS), sm(2, TB, HEADS)
        ogate = sm(3, TB, HEADS)
        cmax, csum = sm(TB, HEADS), sm(TB, HEADS)
        yss, yrt, yrs = sm(TB, SG), sm(TB, SG), sm(TB, SG)
        bvec = sm(2)
        comb = sm(TB, NE)

        onehot_sb, table_sb = r_tmp[0:BUCKETS + 1, 0:REVN], r_tmp[0:BUCKETS + 1, REVN:REVN + HEADS]
        bias_sb = r_tmp[0:HEADS, 700:700 + REVN]
        w2c = view(r_tmp, 1400, 2, DH)
        hidc = view(r_tmp, 1600, 2, KVG, NCMP)
        poolw = view(r_tmp, 1800, 4, P)
        praw = view(r_tmp, 2320, T + 16)
        pw = [view(r_tmp, 2320 + 528 * (i + 1), T + 16) for i in range(2)]
        pr = view(r_tmp, 3904, T)
        att_s = [view(r_tmp, 512 * i, 512) for i in range(3)]
        att_p = [view(r_tmp, 1536 + 512 * i, 512) for i in range(3)]
        att_pt = [view(r_tmp, 3072 + 512 * i, 4, P) for i in range(3)]
        osc = view(r_tmp, 4608, HEADS, DH)
        xdt = [view(r_tmp, 0, D), view(r_o, 0, D)]
        xdd = view(r_tmp, 1024, D)
        xsd = view(r_tmp, 2048, D)
        segd = [view(r_tmp, 3072 + 512 * i, SE, P) for i in range(2)]
        segm = [view(r_tmp, 4096 + 512 * i, SE, P) for i in range(2)]
        yoff = view(r_tmp, 5120, SE, SP)
        hst = view(r_o, 1024, SG, SE * SP)
        gsb = [view(r_tmp, 512 * i, 512) for i in range(3)]
        gm = [view(r_tmp, 1536 + 512 * i, 512) for i in range(3)]
        n1 = view(r_tmp, 0, TB, D)
        wrt = view(r_pool, 0, KT, NE)
        up = [view(r_tmp, 512 * i, 512) for i in range(2)]
        hid = view(r_o, 0, FT, T)
        lnr = view(r_tmp, 1024, 2, D)
        obuf = view(r_tmp, 3072, 2, D)
        ew13 = [view(r_big, 12288 * i, 2, KT, DE) for i in range(2)]
        ew2 = [view(r_big, 12288 * i + 8192, FT, D) for i in range(2)]

        def rv(k):
            return view(r_pool, 128 + k * 64, TB, NE)

        prob, score, lg = rv(0), rv(1), rv(2)
        sel, ssel, selp = rv(3), rv(4), rv(5)
        gt, ge = view(r_pool, 640, TB * 4, 4, 4), view(r_pool, 896, TB * 4, 4, 4)
        rank, gsc, grank, ing = (view(r_pool, 1152, TB * 4, 4), view(r_pool, 1216, TB, 4),
                                 view(r_pool, 1232, TB, 4), view(r_pool, 1248, TB, 4))
        lmax, lsum, wden = view(r_pool, 1264, TB), view(r_pool, 1268, TB), view(r_pool, 1272, TB)

        names = """ld_const ld_bias ld_cmp ld_vd ld_strip ld_poolw st_bias ld_wo ld_rt ld_ln st_out
            ln_stat ln_sd ln_rstd ln_norm ln_turned hT_act hT_dve
            proj_done act_freed dve_freed cmp_mm cmp_pe cmp_hid cmp2_mm cmp_kc cmp_vc bias_mm bias_rows zeroed
            vd_mm vd_used z_mm z_silu pool_in pool_out pool_mm pool_scaled conv_first conv_sum conv_done dv ac gp
            soft_abs soft_ln decay_a gates_e sc_mm sc_max p_done p_turned pt_copied o_mm o_read o_acc o_turned oT_copied
            cs_mm cs_sub cs_exp cs_turned cs_copied co_mm co_read gate_w
            acs_mm acs_neg acs_exp bt_turned bt_copied xt_turned xt_copied xdt_done xdd_done xsd_done
            seg_mm seg_cap seg_exp seg_done y_mm y_read st_mm st_new y_gated y_sq y_ms y_sd y_norm y_turned yT_done
            gate_mm gate_sig br_mm br_used m_add mT_done mix_mm mix_read rt_mm rt_max rt_exp comb_done
            res_mm res_done up_mm up_silu up_used hid_done dn_mm dn_used ln2_norm ln2_out""".split()
        S = {n: sem(n) for n in names}
        ld_x = [sem(f"ld_x{i}") for i in range(TB)]
        ld_z = [sem(f"ld_z{i}") for i in range(2)]
        ld_ring = [sem(f"ld_ring{i}") for i in range(SLOTS)]
        ld_e = [sem(f"ld_e{i}") for i in range(2)]
        st_ob = [sem(f"st_ob{i}") for i in range(2)]

        NCONST, DVE_TILES = 3, (0, 1)

        def release(i):
            if i < 2:
                return S["dve_freed"], i + 1
            if i < 12:
                return S["act_freed"], i - 1
            return S["conv_sum"], 3 * (i - 11)

        units = [(br, qb, h) for br in range(2) for qb in range(TB) for h in range(HEADS)]
        nvalid = [7 + 8 * qb for qb in range(TB)]
        groups = [(c, g) for c in range(TB) for g in range(SG)]
        block = ctx.enter_context(nc.Block())

        @block.sync
        def _(sp):
            for b in range(TB):
                sp.dma_start(xin[:, b, :], x[b * P:(b + 1) * P, :]).then_inc(ld_x[b], 16)
            sp.dma_start(fix[:, :], fixed).then_inc(S["ld_const"], 16)
            sp.dma_start(colv[:, :], cols).then_inc(S["ld_const"], 16)
            sp.dma_start(rowv[:, :], rows.partition_broadcast(P)).then_inc(S["ld_const"], 16)

            def load_tile(i):
                if i >= SLOTS:
                    sp.wait_ge(S["proj_done"], i - SLOTS + 1)
                sp.dma_start(ring[:, i % SLOTS, :, :], w_cm[i].rearrange("p (k n) -> p k n", k=KT)
                             ).then_inc(ld_ring[i % SLOTS], 16)

            for i in range(4):
                load_tile(i)
            sp.dma_start(w1c, w1c_in).then_inc(S["ld_cmp"], 16)
            sp.dma_start(w2c, w2kv).then_inc(S["ld_cmp"], 16)
            sp.dma_start(onehot_sb, onehot).then_inc(S["ld_bias"], 16)
            sp.dma_start(table_sb, table).then_inc(S["ld_bias"], 16)
            sp.dma_start(wvd, w_vd).then_inc(S["ld_vd"], 16)
            sp.dma_start(wz[0], w_tm[0]).then_inc(ld_z[0], 16)
            for i in range(4, 9):
                load_tile(i)
            sp.wait_ge(S["ln_turned"], KT)
            sp.dma_start(wz[1], w_tm[1]).then_inc(ld_z[1], 16)
            sp.dma_start(poolw, pool_w).then_inc(S["ld_poolw"], 16)
            for i in range(9, 12):
                load_tile(i)
            sp.wait_ge(S["bias_rows"], 2)
            skewed = bass.AP(bias_dram.tensor, 0, [[P * (REVN + 1), HEADS], [REVN + 1, P], [1, REVN]])
            sp.dma_start(skewed, bias_sb.unsqueeze(1).broadcast_to([HEADS, P, REVN])).then_inc(S["st_bias"], 16)
            sp.wait_ge(S["st_bias"], 16)
            strip_src = bass.AP(bias_dram.tensor, P - 1, [[REVN, P], [P * (REVN + 1), HEADS], [1, T]])
            sp.dma_start(strips, strip_src).then_inc(S["ld_strip"], 16)
            for i in range(12, CM_PROJ):
                load_tile(i)

            for s in range(BR_TILES):
                sp.wait_ge(S["proj_done"], CM_PROJ)
                sp.dma_start(ring[:, s, :, :], w_cm[CM_PROJ + s].rearrange("p (k n) -> p k n", k=KT)
                             ).then_inc(ld_ring[s], 16)
            sp.wait_ge(S["y_mm"], 16)
            for half in range(2):
                sp.dma_start(wo[:, half], w_out[half]).then_inc(S["ld_wo"], 16)
            with sp.Fori(1, KT) as j:
                for s in range(BR_TILES):
                    if s < 3:
                        sp.wait_ge(S["gate_mm"], j * 3 + (s - 2))
                    else:
                        sp.wait_ge(S["br_mm"], j * 3 + (s - 4))
                    src = w_cm[bass.ds(CM_PROJ + s + j * BR_TILES, 1), :, :].rearrange("a p (k n) -> (a p) k n", k=KT)
                    sp.dma_start(ring[:, s, :, :], src).then_inc(ld_ring[s], 16)
            sp.wait_ge(S["mT_done"], KT)
            sp.dma_start(wrt, w_rt).then_inc(S["ld_rt"], 16)

            def load_expert(e, slot):
                sp.dma_start(ew13[slot], e13[bass.ds(e, 1)].rearrange("a p m k f -> (a p) m k f")).then_inc(ld_e[slot], 16)
                sp.dma_start(ew2[slot], e2[bass.ds(e, 1)].rearrange("a p k n -> (a p) k n")).then_inc(ld_e[slot], 16)

            load_expert(0, 0)
            sp.wait_ge(S["mix_mm"], TB)
            load_expert(1, 1)
            with sp.Fori(1, NE // 2) as i:
                for slot in range(2):
                    sp.wait_ge(S["dn_mm"], (i * 2 + slot - 1) * 2 * TB)
                    load_expert(i * 2 + slot, slot)
            sp.wait_ge(S["up_mm"], 2 * FT * NE)
            sp.wait_ge(S["hid_done"], FT * NE)
            for i in range(2):
                sp.dma_start(lnr[:, i, :], lnrows[i:i + 1, :].partition_broadcast(P)).then_inc(S["ld_ln"], 16)
            for b in range(TB):
                sp.wait_ge(S["ln2_out"], b + 1)
                sp.dma_start(out[b * P:(b + 1) * P, :], obuf[:, b % 2, :]).then_inc(st_ob[b % 2], 16)
            for i in range(2):
                sp.wait_ge(st_ob[i], 16 * TB // 2)

        @block.tensor
        def _(pe):
            mm = nc.tensor.matmul
            tr = nc.tensor.transpose
            pe.wait_ge(S["ld_const"], 16 * NCONST)
            pe.wait_ge(S["ln_norm"], TB)
            for k in range(KT):
                for b in range(TB):
                    last = tr(bank[k][:, b * P:(b + 1) * P], xnorm[:, b, k * P:(k + 1) * P], ident)
                last.then_inc(S["ln_turned"], 1)

            def proj(i):
                pe.wait_ge(ld_ring[i % SLOTS], 16 * (i // SLOTS + 1))
                if i >= 2:
                    pe.wait_ge(*release(i - 2))
                for k in range(KT):
                    last = mm(bank[i % 2][:, :], ring[:, i % SLOTS, k, :], hT[:, k, :], start=(k == 0), stop=(k == KT - 1))
                last.then_inc(S["proj_done"], 1)

            pe.wait_ge(S["hT_act"], KT // 2)
            pe.wait_ge(S["hT_dve"], KT // 2)
            for i in range(8):
                proj(i)

            pe.wait_ge(S["ld_cmp"], 32)
            pe.wait_ge(S["dve_freed"], 2)
            for kv in range(2):
                for l in range(CMP_LEN // 2):
                    rhs = tok2[:, kv, :, 2 * l:2 * l + CMP_STRIDE * (NCMP - 1) + 1:CMP_STRIDE]
                    last = mm(bank[2 + kv][:, 0:KVG * NCMP].rearrange("p (g n) -> p g n", g=KVG), w1c[:, kv, l, :], rhs,
                              start=(l == 0), stop=(l == CMP_LEN // 2 - 1))
                for l in range(CMP_LEN // 2):
                    c = (C_PEK, C_PEV)[kv] + l
                    last = mm(bank[2 + kv][:, 64:65], w1c[:, kv, l, :], colv[:, c:c + 1],
                              start=(l == 0), stop=(l == CMP_LEN // 2 - 1))
                last.then_inc(S["cmp_mm"], 1)
            pe.wait_ge(S["ld_bias"], 32)
            for i in range(2):
                mm(bank[6 + i][0:HEADS, 0:REVN // 2], table_sb, onehot_sb[:, i * REVN // 2:(i + 1) * REVN // 2],
                   start=True, stop=True).then_inc(S["bias_mm"], 1)
            pe.wait_ge(S["cmp_hid"], 2)
            for g in range(KVG):
                mm(bank[4][g * DH:(g + 1) * DH, 0:NCMP], w2c[:, 0, :], hidc[:, 0, g, :], start=True, stop=True)
            for g in range(KVG):
                for h in range(HPG):
                    last = mm(bank[5][32 * h:32 * h + NCMP, g * DH:(g + 1) * DH], hidc[:, 1, g, :], w2c[:, 1, :],
                              start=True, stop=True)
            last.then_inc(S["cmp2_mm"], 1)
            pe.wait_ge(S["ld_vd"], 16)
            pe.wait_ge(S["cmp_kc"], 1)
            pe.wait_ge(S["cmp_vc"], HPG)
            for b in range(TB):
                for k in range(KT):
                    last = mm(bank[2 + b][:, 0:VD], hT[:, k, b * P:(b + 1) * P], wvd[:, k, :], start=(k == 0), stop=(k == KT - 1))
                last.then_inc(S["vd_mm"], 1)
            for i in range(8, CM_PROJ):
                proj(i)
            pe.wait_ge(S["bias_rows"], 2)
            for half in range(2):
                pe.wait_ge(ld_z[half], 16)
                for b in range(TB):
                    n = half * TB + b
                    if n >= 2:
                        pe.wait_ge(S["z_silu"], n - 1)
                    for k in range(KT):
                        last = mm(bank[6 + n % 2][:, :], hT[:, k, b * P:(b + 1) * P], wz[half][:, k, :],
                                  start=(k == 0), stop=(k == KT - 1))
                    last.then_inc(S["z_mm"], 1)
            pe.wait_ge(S["ld_poolw"], 16)
            for g in range(4):
                pe.wait_ge(S["pool_out"], g + 1)
                if g == 0:
                    pe.wait_ge(S["vd_used"], TB)
                mm(bank[2 + g][:, :], poolw[:, g, :], poolT[:, g, :], start=True, stop=True).then_inc(S["pool_mm"], 1)

            pe.wait_ge(S["pool_scaled"], 4)
            for qb in range(TB):
                nv = nvalid[qb]
                if qb == 0:
                    pe.wait_ge(S["act_freed"], 6)
                    pe.wait_ge(S["conv_sum"], 48)
                    pe.wait_ge(S["cmp_kc"], 1)
                if qb >= 2:
                    pe.wait_ge(S["cs_sub"], qb - 1)
                for h in range(HEADS):
                    g, i = divmod(h, HPG)
                    last = mm(bank[2 * (qb % 2) + g][:, 32 * h:32 * h + nv], qT[g * DH:(g + 1) * DH, i, qb * P:(qb + 1) * P],
                              kcT[g * DH:(g + 1) * DH, 0:nv], start=True, stop=True)
                last.then_inc(S["cs_mm"], 1)
                pe.wait_ge(S["cs_exp"], qb + 1)
                if qb >= 1:
                    pe.wait_ge(S["cs_copied"], qb)
                for g in range(KVG):
                    last = tr(bank[4][:, g * P:(g + 1) * P], pcs[:, qb, g * HPG:(g + 1) * HPG, :].rearrange("p h n -> p (h n)"), ident)
                last.then_inc(S["cs_turned"], 1)
                pe.wait_ge(S["cs_copied"], qb + 1)
                pe.wait_ge(S["cmp_vc"], HPG)
                if qb >= 1:
                    pe.wait_ge(S["co_read"], qb)
                for g in range(KVG):
                    last = mm(bank[5][:, g * 256:(g + 1) * 256], pct[:, qb % 2, g, :], vbd[:, g, :, :].rearrange("p h d -> p (h d)"),
                              start=True, stop=True)
                last.then_inc(S["co_mm"], 1)

            def scores(u):
                br, qb, h = units[u]
                g, i = divmod(h, HPG)
                n = (qb + 1) * P
                if u >= 3:
                    pe.wait_ge(S["sc_max"], u - 2)
                mm(bank[u % 3][:, 0:n], qT[g * DH:(g + 1) * DH, i, qb * P:(qb + 1) * P], kT[br][g * DH:(g + 1) * DH, 0:n],
                   start=True, stop=True).then_inc(S["sc_mm"], 1)

            def turn(u):
                br, qb, h = units[u]
                pe.wait_ge(S["p_done"], u + 1)
                if u >= 2:
                    pe.wait_ge(S["pt_copied"], u - 1)
                for kb in range(qb + 1):
                    last = tr(bank[3 + u % 2][:, kb * P:(kb + 1) * P], att_p[u % 3][:, kb * P:(kb + 1) * P], ident)
                last.then_inc(S["p_turned"], 1)

            def values(u):
                br, qb, h = units[u]
                n = br * TB + qb
                pe.wait_ge(S["pt_copied"], u + 1)
                if h == 0 and n >= 2:
                    pe.wait_ge(S["o_read"], n - 1)
                for kb in range(qb + 1):
                    last = mm(bank[5 + n % 2][:, h * DH:(h + 1) * DH], att_pt[u % 3][:, kb, :], vtok[:, kb, br, h // HPG, :],
                              start=(kb == 0), stop=(kb == qb))
                last.then_inc(S["o_mm"], 1)

            def turn_o(qb):
                pe.wait_ge(S["o_acc"], TB + qb + 1)
                if qb >= 1:
                    pe.wait_ge(S["oT_copied"], qb)
                for ct in range(4):
                    last = tr(bank[7][:, ct * P:(ct + 1) * P], oacc[:, qb, 2 * ct:2 * ct + 2, :].rearrange("p h d -> p (h d)"), ident)
                last.then_inc(S["o_turned"], 1)

            pe.wait_ge(S["cs_sub"], TB)
            pe.wait_ge(S["cs_copied"], TB)
            pe.wait_ge(S["co_read"], TB)
            NU = len(units)
            for u in range(NU + 3):
                if u < NU:
                    scores(u)
                if 2 <= u < NU + 2:
                    turn(u - 2)
                if u >= 3:
                    values(u - 3)
            for qb in range(TB):
                turn_o(qb)

            for c in range(TB):
                if c >= 2:
                    pe.wait_ge(S["bt_copied"], c - 1)
                if c == 0:
                    pe.wait_ge(S["conv_done"], 16)
                for g in range(SG):
                    last = tr(bank[c % 2][:, g * P:(g + 1) * P], bcT[:, g, c * P:(c + 1) * P], ident)
                last.then_inc(S["bt_turned"], 1)
            for n in range(2 * TB):
                c, half = divmod(n, 2)
                if n >= 2:
                    pe.wait_ge(S["xt_copied"], n - 1)
                else:
                    pe.wait_ge(S["sc_max"], NU)
                for i in range(4):
                    last = tr(bank[2 + n % 2][:, i * P:(i + 1) * P], xsT[:, half * 4 + i, c * P:(c + 1) * P], ident)
                last.then_inc(S["xt_turned"], 1)
            pe.wait_ge(S["decay_a"], 1)
            a_all = dta.rearrange("p c h -> p (c h)")
            mm(bank[4][:, 0:64], tri, a_all, start=True, stop=True)
            mm(bank[4][:, 64:128], ones, a_all, start=True, stop=True).then_inc(S["acs_mm"], 1)

            def seg(n):
                c, g = groups[n]
                if n >= 2:
                    pe.wait_ge(S["seg_cap"], 4 * (n - 1))
                    pe.wait_ge(S["seg_done"], n - 1)
                for e in range(SE):
                    h = g * SE + e
                    mm(bank[n % 2][:, e * P:(e + 1) * P], dta[:, c, h:h + 1].to_broadcast([P, P]), tri, start=True, stop=True)
                mm(bank[2 + n % 2][:, 0:P], bcT[:, g, c * P:(c + 1) * P], bcT[:, 4 + g, c * P:(c + 1) * P],
                   start=True, stop=True).then_inc(S["seg_mm"], 1)

            def y_and_state(n):
                c, g = groups[n]
                yb, stb = bank[4 + n % 2], bank[6 + n % 2]
                pe.wait_ge(S["seg_done"], n + 1)
                pe.wait_ge(S["xdt_done"], c + 1)
                if n >= 2:
                    pe.wait_ge(S["y_read"], n - 1)
                for e in range(SE):
                    h = g * SE + e
                    last = mm(yb[:, e * SP:(e + 1) * SP], segm[n % 2][:, e, :], xdt[c % 2][:, h * SP:(h + 1) * SP],
                              start=True, stop=True)
                if c > 0:
                    pe.wait_ge(S["st_new"], n - SG + 1)
                    last = mm(yb[:, 256:512], bcT[:, 4 + g, c * P:(c + 1) * P], hst[:, g, :], start=True, stop=True)
                last.then_inc(S["y_mm"], 1)
                if c < TB - 1:
                    pe.wait_ge(S["xdd_done"], c + 1)
                    if n >= 2:
                        pe.wait_ge(S["st_new"], n - 1)
                    mm(stb[:, 0:256], btok[:, c, g, :], xdd[:, g * 256:(g + 1) * 256], start=True, stop=True).then_inc(S["st_mm"], 1)

            pe.wait_ge(S["bt_copied"], TB)
            pe.wait_ge(S["xt_copied"], 2 * TB)
            pe.wait_ge(S["acs_neg"], 1)
            pe.wait_ge(S["oT_copied"], TB)
            seg(0)
            for n in range(16):
                if n + 1 < 16:
                    seg(n + 1)
                y_and_state(n)
            for c in range(TB):
                pe.wait_ge(S["y_norm"], c + 1)
                for half in range(2):
                    n = 2 * c + half
                    if n >= 2:
                        pe.wait_ge(S["yT_done"], n - 1)
                    else:
                        pe.wait_ge(S["st_new"], 12)
                    for i in range(4):
                        k = half * 4 + i
                        last = tr(bank[6 + n % 2][:, i * P:(i + 1) * P], ytok[:, c, k * P:(k + 1) * P], ident)
                    last.then_inc(S["y_turned"], 1)

            loads = [len([i for i in range(CM_PROJ) if i % SLOTS == s]) for s in range(SLOTS)]

            def branch(j, first):
                for s in range(3):
                    pe.wait_ge(ld_ring[s], (j + (loads[s] + 1)) * 16)
                    if not first:
                        pe.wait_ge(S["gate_sig"], j * 3)
                    for k in range(KT):
                        last = mm(bank[s][:, :], ring[:, s, k, :], hT[:, k, :], start=(k == 0), stop=(k == KT - 1))
                    last.then_inc(S["gate_mm"], 1)
                pe.wait_ge(ld_ring[3], (j + (loads[3] + 1)) * 16)
                if not first:
                    pe.wait_ge(S["br_used"], j * 3)
                for k in range(4):
                    last = mm(bank[3][:, :], ring[:, 3, k, :], poolT[:, k, :], start=(k == 0), stop=(k == 3))
                last.then_inc(S["br_mm"], 1)
                for k in range(4):
                    last = mm(bank[4][:, :], ring[:, 3, 4 + k, :], oT[:, k, :], start=(k == 0), stop=(k == 3))
                last.then_inc(S["br_mm"], 1)
                pe.wait_ge(ld_ring[4], (j + (loads[4] + 1)) * 16)
                for k in range(KT):
                    last = mm(bank[5][:, :], ring[:, 4, k, :], yT[:, k, :], start=(k == 0), stop=(k == KT - 1))
                last.then_inc(S["br_mm"], 1)

            pe.wait_ge(S["yT_done"], 2 * TB)
            pe.wait_ge(S["y_read"], 16)
            branch(0, True)
            with pe.Fori(1, KT) as j:
                branch(j, False)

            pe.wait_ge(S["ld_wo"], 32)
            pe.wait_ge(S["mT_done"], KT)
            for b in range(TB):
                if b >= 2:
                    pe.wait_ge(S["mix_read"], b - 1)
                for half in range(2):
                    acc = bank[(6, 0)[b % 2] + half]
                    for k in range(KT):
                        last = mm(acc[:, :], mT[:, k, b * P:(b + 1) * P], wo[:, half, k, :], start=(k == 0), stop=(k == KT - 1))
                        if k < 4:
                            mm(acc[:, k * P:(k + 1) * P], hT[:, half * 4 + k, b * P:(b + 1) * P], aident, start=False, stop=False)
                last.then_inc(S["mix_mm"], 1)
            pe.wait_ge(S["ln_norm"], 2 * TB)
            for k in range(KT):
                for b in range(TB):
                    last = tr(bank[k][:, b * P:(b + 1) * P], n1[:, b, k * P:(k + 1) * P], ident)
                last.then_inc(S["ln_turned"], 1)

            pe.wait_ge(S["hT_act"], KT)
            pe.wait_ge(S["hT_dve"], KT)
            pe.wait_ge(S["ld_rt"], 16)
            for b in range(TB):
                for k in range(KT):
                    last = mm(bank[0][:, b * NE:(b + 1) * NE], h1T[:, k, b * P:(b + 1) * P], wrt[:, k, :], start=(k == 0), stop=(k == KT - 1))
            last.then_inc(S["rt_mm"], 1)
            for n in range(2 * TB):
                b, half = divmod(n, 2)
                if n >= 2:
                    pe.wait_ge(S["res_done"], n - 1)
                for i in range(4):
                    last = mm(bank[6 + n % 2][:, i * P:(i + 1) * P], h1T[:, half * 4 + i, b * P:(b + 1) * P], aident, start=True, stop=True)
                last.then_inc(S["res_mm"], 1)

            def expert(i, slot, first):
                pe.wait_ge(ld_e[slot], (i + 1) * 32)
                for f in range(FT):
                    for m in range(2):
                        if not first or f >= 2:
                            pe.wait_ge(S["hid_done"], (i * 2 + slot) * FT + f - 1)
                        for k in range(KT):
                            last = mm(bank[2 * (f % 2) + m][:, :], ew13[slot][:, m, k, f * P:(f + 1) * P], h1T[:, k, :],
                                      start=(k == 0), stop=(k == KT - 1))
                        last.then_inc(S["up_mm"], 1)
                pe.wait_ge(S["hid_done"], (i * 2 + slot) * FT + FT)
                for n in range(2 * TB):
                    b, half = divmod(n, 2)
                    if not first or n >= 4:
                        pe.wait_ge(S["dn_used"], (i * 2 + slot) * 2 * TB + n - 3)
                    for k in range(FT):
                        last = mm(bank[4 + n % 4][:, :], hid[:, k, b * P:(b + 1) * P], ew2[slot][:, k, half * 512:(half + 1) * 512],
                                  start=(k == 0), stop=(k == FT - 1))
                    last.then_inc(S["dn_mm"], 1)

            pe.wait_ge(S["rt_max"], 1)
            pe.wait_ge(S["res_done"], 2 * TB)
            expert(0, 0, True)
            expert(0, 1, False)
            with pe.Fori(1, NE // 2) as i:
                expert(i, 0, False)
                expert(i, 1, False)

        @block.scalar
        def _(act):
            ac = nc.scalar.activation
            act.wait_ge(S["ln_stat"], 1)
            ac(sdev, mv[:, :, 1], ACT.Sqrt).then_inc(S["ln_sd"], 1)

            def turned_to(dst, base, g0, b0):
                for k in range(0, KT, 2):
                    act.wait_ge(S["ln_turned"], base + k + 1)
                    ac(dst[:, k, :], bank[k][:, :], ACT.Identity, scale=colv[:, g0 + k:g0 + k + 1],
                       bias=colv[:, b0 + k:b0 + k + 1]).then_inc(S["hT_act"], 1)

            act.wait_ge(S["ld_const"], 16 * NCONST)
            turned_to(hT, 0, C_LN0G, C_LN0B)
            for i in (2, 3):
                act.wait_ge(S["proj_done"], i + 1)
                ac(kT[i - 2], bank[i % 2][:, :], ACT.Copy).then_inc(S["act_freed"], 1)
            for i in range(4, 8):
                act.wait_ge(S["proj_done"], i + 1)
                ac(qT[:, i - 4, :], bank[i % 2][:, :], ACT.Copy, scale=DH ** -0.5).then_inc(S["act_freed"], 1)
            for kv in range(2):
                act.wait_ge(S["cmp_mm"], kv + 1)
                ac(bvec[:, kv:kv + 1], bank[2 + kv][:, 64:65], ACT.Copy).then_inc(S["cmp_pe"], 1)
            act.wait_ge(S["cmp_pe"], 2)
            for kv in range(2):
                ac(hidc[:, kv], bank[2 + kv][:, 0:KVG * NCMP].rearrange("p (g n) -> p g n", g=KVG), ACT.Gelu_apprx_tanh,
                   bias=bvec[:, kv:kv + 1]).then_inc(S["cmp_hid"], 1)
            act.wait_ge(S["cmp2_mm"], 1)
            ac(kcT[:, :], bank[4][:, 0:NCMP], ACT.Copy).then_inc(S["cmp_kc"], 1)
            for g in range(4):
                i = 8 + g
                act.wait_ge(S["proj_done"], i + 1)
                if g >= 1:
                    act.wait_ge(S["pool_out"], g)
                else:
                    act.wait_ge(S["zeroed"], 3)
                ac(praw[:, 16:], bank[i % 2][:, :], ACT.Copy).then_inc(S["act_freed"], 1)

            def conv_out(i):
                act.wait_ge(S["conv_sum"], 3 * (i + 1))
                dst = xsT[:, i, :] if i < 8 else bcT[:, i - 8, :]
                ac(dst, dst, ACT.Silu).then_inc(S["conv_done"], 1)

            for i in range(16):
                dst = xsT[:, i, :] if i < 8 else bcT[:, i - 8, :]
                if i == 0:
                    act.wait_ge(S["vd_mm"], TB)
                if i == 8:
                    act.wait_ge(S["cmp_mm"], 2)
                act.wait_ge(S["proj_done"], 12 + i + 1)
                ac(dst, bank[i % 2][:, :], ACT.Identity, scale=colv[:, C_CW + 48 + i:C_CW + 49 + i],
                   bias=colv[:, C_CB + i:C_CB + i + 1]).then_inc(S["conv_first"], 1)
                if i >= 1:
                    conv_out(i - 1)
            conv_out(15)
            for n in range(2 * TB):
                half, b = divmod(n, TB)
                act.wait_ge(S["z_mm"], n + 1)
                ac(zs[:, b, half * 512:(half + 1) * 512], bank[6 + n % 2][:, :], ACT.Silu).then_inc(S["z_silu"], 1)
            act.wait_ge(S["soft_abs"], 1)
            ac(dte, dtm, ACT.Exp, scale=-1.0).then_inc(S["ac"], 1)
            act.wait_ge(S["ac"], 1)
            ac(dte, dte, ACT.Ln, bias=1.0).then_inc(S["soft_ln"], 1)
            ac(expa, rowv[:, R_ALOG:R_ALOG + SH], ACT.Exp).then_inc(S["soft_ln"], 1)
            ac(ngate, ngate, ACT.Exp, scale=-1.0).then_inc(S["gates_e"], 1)

            for qb in range(TB):
                act.wait_ge(S["cs_sub"], qb + 1)
                v = pcs[:, qb, :, 0:nvalid[qb]]
                ac(v, v, ACT.Exp).then_inc(S["cs_exp"], 1)
            for u, (br, qb, h) in enumerate(units):
                n = (qb + 1) * P
                act.wait_ge(S["sc_max"], u + 1)
                if u >= 3:
                    act.wait_ge(S["p_turned"], u - 2)
                ac(att_p[u % 3][:, 0:n], att_s[u % 3][:, 0:n], ACT.Exp, scale=-1.0, bias=nmax[:, br, qb, h:h + 1],
                   accum_out=psums[:, br, qb, h:h + 1]).then_inc(S["p_done"], 1)
            for qb in range(TB):
                act.wait_ge(S["o_turned"], qb + 1)
                ac(oT[:, :, qb * P:(qb + 1) * P], bank[7][:, :].rearrange("p (a b) -> p a b", a=4), ACT.Copy).then_inc(S["oT_copied"], 1)
            for n in range(2 * TB):
                c, half = divmod(n, 2)
                act.wait_ge(S["xt_turned"], n + 1)
                ac(ytok[:, c, half * 512:(half + 1) * 512], bank[2 + n % 2][:, :], ACT.Copy).then_inc(S["xt_copied"], 1)
            act.wait_ge(S["acs_neg"], 3)
            for dst, src in ((eacs, acs), (decin, decin), (cdec, cdec)):
                ac(dst, src, ACT.Exp).then_inc(S["acs_exp"], 1)
            for n in range(16):
                act.wait_ge(S["seg_cap"], 4 * (n + 1))
                ac(segd[n % 2], segd[n % 2], ACT.Exp).then_inc(S["seg_exp"], 1)
            for c in range(TB):
                act.wait_ge(S["y_gated"], c + 1)
                for g in range(SG):
                    ac(r_qkv[:, 0:256], ytok[:, c, g * 256:(g + 1) * 256], ACT.Square, accum_out=yss[:, c, g:g + 1]).then_inc(S["y_sq"], 1)
                    act.wait_ge(S["y_sq"], c * SG + g + 1)
            act.wait_ge(S["y_ms"], 1)
            ac(yrt, yrt, ACT.Sqrt).then_inc(S["y_sd"], 1)
            for n in range(2 * TB):
                c, half = divmod(n, 2)
                act.wait_ge(S["y_turned"], n + 1)
                for i in range(4):
                    k = half * 4 + i
                    last = ac(yT[:, k, c * P:(c + 1) * P], bank[6 + n % 2][:, i * P:(i + 1) * P], ACT.Copy, scale=colv[:, C_NG + k:C_NG + k + 1])
                last.then_inc(S["yT_done"], 1)

            def sigmoids(j, first):
                for s in range(3):
                    act.wait_ge(S["gate_mm"], j * 3 + (s + 1))
                    if not first:
                        act.wait_ge(S["br_used"], j * 3)
                    ac(gsb[s], bank[s][:, :], ACT.Sigmoid).then_inc(S["gate_sig"], 1)

            sigmoids(0, True)
            with act.Fori(1, KT) as j:
                sigmoids(j, False)
            act.wait_ge(S["mT_done"], KT)
            for b in range(TB):
                act.wait_ge(S["mix_mm"], b + 1)
                for half in range(2):
                    last = ac(n1[:, b, half * 512:(half + 1) * 512], bank[(6, 0)[b % 2] + half][:, :], ACT.Copy)
                last.then_inc(S["mix_read"], 1)
            act.wait_ge(S["ln_stat"], 2)
            ac(sdev, mv[:, :, 1], ACT.Sqrt).then_inc(S["ln_sd"], 1)
            turned_to(h1T, KT, C_LN1G, C_LN1B)
            act.wait_ge(S["rt_max"], 1)
            ac(lg, lg, ACT.Exp).then_inc(S["rt_exp"], 1)

            def silus(i, slot, first):
                for f in range(FT):
                    act.wait_ge(S["up_mm"], (i * 2 + slot) * 2 * FT + (2 * f + 1))
                    if not first or f >= 2:
                        act.wait_ge(S["hid_done"], (i * 2 + slot) * FT + f - 1)
                    ac(up[f % 2], bank[2 * (f % 2)][:, :], ACT.Silu).then_inc(S["up_silu"], 1)

            silus(0, 0, True)
            silus(0, 1, False)
            with act.Fori(1, NE // 2) as i:
                silus(i, 0, False)
                silus(i, 1, False)
            act.wait_ge(S["ln_stat"], 3)
            ac(sdev, mv[:, :, 1], ACT.Sqrt).then_inc(S["ln_sd"], 1)

        @block.gpsimd
        def _(gp):
            g_ = nc.gpsimd
            g_.memset(praw[:, 0:16], 0.0).then_inc(S["zeroed"], 1)
            g_.memset(pw[0][:, 0:16], 0.0).then_inc(S["zeroed"], 1)
            g_.memset(pw[1][:, 0:16], 0.0).then_inc(S["zeroed"], 1)
            g_.memset(vbd[:, :, :, :], 0.0).then_inc(S["zeroed"], 1)
            g_.memset(pcs, 0.0).then_inc(S["zeroed"], 1)
            step = 0
            gp.wait_ge(S["zeroed"], 3)
            gp.wait_ge(S["ld_const"], 16 * NCONST)
            for g, w in enumerate(WINDOWS):
                gp.wait_ge(S["act_freed"], 6 + g + 1)
                src, span, flip = praw, 1, 0
                while span < w:
                    dst = pw[flip]
                    g_.tensor_tensor(dst[:, 16:], src[:, 16:], src[:, 16 - span:16 - span + T], ALU.add).then_inc(S["gp"], 1)
                    step += 1
                    gp.wait_ge(S["gp"], step)
                    src, span, flip = dst, span * 2, 1 - flip
                g_.tensor_scalar(pr[:, 16:], src[:, 32:], 1.0 / w, None, ALU.mult).then_inc(S["gp"], 1)
                g_.tensor_tensor(pr[:, 0:16], src[:, 16:32], invc[:, g, :], ALU.mult).then_inc(S["gp"], 1)
                step += 2
                gp.wait_ge(S["gp"], step)
                g_.tensor_tensor(poolT[:, g, :], pr, praw[:, 16:], ALU.subtract).then_inc(S["pool_out"], 1)
                gp.wait_ge(S["pool_out"], g + 1)
            for c in range(TB):
                gp.wait_ge(S["xdt_done"], c + 1)
                if c < TB - 1:
                    if c >= 1:
                        gp.wait_ge(S["st_mm"], SG * c)
                    g_.tensor_tensor(xdd.rearrange("p (h d) -> p h d", h=SH), xdt[c % 2].rearrange("p (h d) -> p h d", h=SH),
                                     decin[:, c, :].unsqueeze(2).broadcast_to([P, SH, SP]), ALU.mult).then_inc(S["xdd_done"], 1)
                if c >= 1:
                    gp.wait_ge(S["y_gated"], c)
                g_.tensor_tensor(xsd.rearrange("p (h d) -> p h d", h=SH), ytok[:, c, :].rearrange("p (h d) -> p h d", h=SH),
                                 rowv[:, R_DSK:R_DSK + SH].unsqueeze(2).broadcast_to([P, SH, SP]), ALU.mult).then_inc(S["xsd_done"], 1)

        @block.vector
        def _(dve):
            v = nc.vector
            chain = [0]

            def then(ins):
                chain[0] += 1
                ins.then_inc(S["dv"], 1)
                dve.wait_ge(S["dv"], chain[0])

            def stats_of(b, halves):
                for i, half in enumerate(halves):
                    last = v.bn_stats(stats[:, b, i, :], half)
                then(last)
                return v.bn_aggr(mv[:, b, :], stats[:, b].rearrange("p a s -> p (a s)"))

            def add_eps():
                then(v.tensor_scalar(rstd, mv[:, :, 1], LN_EPS, None, ALU.add))
                v.tensor_copy(mv[:, :, 1], rstd).then_inc(S["ln_stat"], 1)

            for b in range(TB):
                dve.wait_ge(ld_x[b], 16)
                then(stats_of(b, [xin[:, b, 0:512], xin[:, b, 512:1024]]))
            add_eps()
            dve.wait_ge(S["ln_sd"], 1)
            then(v.reciprocal(rstd, sdev))
            for b in range(TB):
                v.tensor_scalar(xnorm[:, b, :], xin[:, b, :], mv[:, b, 0:1], rstd[:, b:b + 1], ALU.subtract, ALU.mult).then_inc(S["ln_norm"], 1)

            def turned_to(dst, base, g0, b0):
                for k in range(1, KT, 2):
                    dve.wait_ge(S["ln_turned"], base + k + 1)
                    v.tensor_scalar(dst[:, k, :], bank[k][:, :], colv[:, g0 + k:g0 + k + 1], colv[:, b0 + k:b0 + k + 1],
                                    ALU.mult, ALU.add).then_inc(S["hT_dve"], 1)

            dve.wait_ge(S["ld_const"], 16 * NCONST)
            turned_to(hT, 0, C_LN0G, C_LN0B)
            for kv in range(2):
                dve.wait_ge(S["proj_done"], kv + 1)
                for g in range(KVG):
                    rows_g = bank[kv][g * DH:(g + 1) * DH, :]
                    v.tensor_copy(tok2[0:DH, kv, g, :], rows_g)
                    last = v.tensor_copy(tok2[DH:P, kv, g, 0:T - 1], rows_g[:, 1:T])
                last.then_inc(S["dve_freed"], 1)
            for i in range(2):
                dve.wait_ge(S["bias_mm"], i + 1)
                v.tensor_copy(bias_sb[:, i * REVN // 2:(i + 1) * REVN // 2], bank[6 + i][0:HEADS, 0:REVN // 2]).then_inc(S["bias_rows"], 1)
            dve.wait_ge(S["cmp2_mm"], 1)
            dve.wait_ge(S["zeroed"], 4)
            for h in range(HPG):
                rows_h = slice(32 * h, 32 * h + NCMP)
                v.tensor_copy(vbd[rows_h, :, h, :], bank[5][rows_h, 0:KVG * DH].rearrange("p (g d) -> p g d", g=KVG)).then_inc(S["cmp_vc"], 1)
            for b in range(TB):
                dve.wait_ge(S["vd_mm"], b + 1)
                v.tensor_copy(vtok[:, b].rearrange("p r g d -> p (r g d)"), bank[2 + b][:, 0:2 * P])
                v.tensor_tensor(dtx[:, b, :], bank[2 + b][:, 2 * P:2 * P + SH], rowv[:, R_DTB:R_DTB + SH], ALU.add)
                v.tensor_copy(ngate[:, b].rearrange("p r h -> p (r h)"), bank[2 + b][:, 2 * P + SH:VD]).then_inc(S["vd_used"], 1)
            for i in range(16):
                dst = xsT[:, i, :] if i < 8 else bcT[:, i - 8, :]
                dve.wait_ge(S["conv_first"], i + 1)
                for n, back in enumerate((1, 2, 3)):
                    tap = C_CW + (3 - back) * 16 + i
                    if n:
                        dve.wait_ge(S["conv_sum"], 3 * i + n)
                    v.scalar_tensor_tensor(out=dst[:, back:], in0=bank[i % 2][:, 0:T - back], scalar=colv[:, tap:tap + 1],
                                           in1=dst[:, back:], op0=ALU.mult, op1=ALU.add).then_inc(S["conv_sum"], 1)
            for g in range(4):
                dve.wait_ge(S["pool_mm"], g + 1)
                v.tensor_scalar(poolT[:, g, :], bank[2 + g][:, :], colv[:, C_PS + g:C_PS + g + 1], None, ALU.mult).then_inc(S["pool_scaled"], 1)
            v.scalar_tensor_tensor(out=dtm, in0=dtx, scalar=-1.0, in1=dtx, op0=ALU.mult, op1=ALU.max).then_inc(S["soft_abs"], 1)
            dve.wait_ge(S["soft_ln"], 2)
            then(v.scalar_tensor_tensor(out=dt, in0=dtx, scalar=0.0, in1=dte, op0=ALU.max, op1=ALU.add))
            v.scalar_tensor_tensor(out=dta, in0=dt, scalar=-1.0, in1=expa.unsqueeze(1).broadcast_to([P, TB, SH]),
                                   op0=ALU.mult, op1=ALU.mult).then_inc(S["decay_a"], 1)
            dve.wait_ge(S["gates_e"], 1)
            then(v.tensor_scalar(ngate, ngate, 1.0, None, ALU.add))
            then(v.reciprocal(ngate, ngate))

            dve.wait_ge(S["ld_strip"], 16)
            dve.wait_ge(S["zeroed"], 5)
            for qb in range(TB):
                nv = nvalid[qb]
                z0 = T - P - qb * P + CMP_LEN - 1
                dve.wait_ge(S["cs_mm"], qb + 1)
                s3 = pcs[:, qb, :, 0:nv]
                for g in range(KVG):
                    hs = slice(g * HPG, (g + 1) * HPG)
                    last = v.tensor_tensor(s3[:, hs, :], bank[2 * (qb % 2) + g][:, 0:256].rearrange("p (h n) -> p h n", h=HEADS)[:, hs, 0:nv],
                                           strips[:, hs, z0:z0 + CMP_STRIDE * (nv - 1) + 1:CMP_STRIDE], ALU.add)
                then(last)
                then(v.tensor_reduce(cmax[:, qb, :], s3, AX.X, ALU.max))
                v.tensor_tensor(s3, s3, cmax[:, qb, :].unsqueeze(2).broadcast_to([P, HEADS, nv]), ALU.subtract).then_inc(S["cs_sub"], 1)
                dve.wait_ge(S["cs_exp"], qb + 1)
                then(v.tensor_reduce(csum[:, qb, :], s3, AX.X, ALU.add))
                then(v.reciprocal(csum[:, qb, :], csum[:, qb, :]))
                gate = ngate[:, qb, 0, :]
                if qb == 0:
                    then(v.tensor_scalar(gate, gate, rowok, None, ALU.mult))
                then(v.tensor_tensor(ogate[:, 0, qb, :], gate, csum[:, qb, :], ALU.mult))
                dve.wait_ge(S["cs_turned"], qb + 1)
                if qb >= 2:
                    dve.wait_ge(S["co_mm"], qb - 1)
                v.tensor_copy(pct[:, qb % 2].rearrange("p g n -> p (g n)"), bank[4][:, 0:256]).then_inc(S["cs_copied"], 1)
                dve.wait_ge(S["co_mm"], qb + 1)
                v.tensor_tensor(oacc[:, qb], bank[5][:, :].rearrange("p (h d) -> p h d", h=HEADS),
                                ogate[:, 0, qb, :].unsqueeze(2).broadcast_to([P, HEADS, DH]), ALU.mult).then_inc(S["co_read"], 1)

            NU = len(units)
            for u in range(NU + 3):
                if u < NU:
                    br, qb, h = units[u]
                    n = (qb + 1) * P
                    dve.wait_ge(S["sc_mm"], u + 1)
                    if u >= 3:
                        dve.wait_ge(S["p_done"], u - 2)
                    v.tensor_tensor_reduce(out=att_s[u % 3][:, 0:n], in0=bank[u % 3][:, 0:n], in1=strips[:, h, T - n:T],
                                           scale=-1.0, scalar=3e38, op0=ALU.add, op1=ALU.min,
                                           accum_out=nmax[:, br, qb, h:h + 1]).then_inc(S["sc_max"], 1)
                if 2 <= u < NU + 2:
                    w = u - 2
                    nb = units[w][1] + 1
                    dve.wait_ge(S["p_turned"], w + 1)
                    if w >= 3:
                        dve.wait_ge(S["o_mm"], w - 2)
                    v.tensor_copy(att_pt[w % 3][:, 0:nb, :].rearrange("p a b -> p (a b)"), bank[3 + w % 2][:, 0:nb * P]).then_inc(S["pt_copied"], 1)
                if u >= 3 and units[u - 3][2] == HEADS - 1:
                    br, qb, _h = units[u - 3]
                    n = br * TB + qb
                    dve.wait_ge(S["p_done"], u - 2)
                    then(v.reciprocal(psums[:, br, qb, :], psums[:, br, qb, :]))
                    then(v.tensor_tensor(ogate[:, 1 + br, qb, :], psums[:, br, qb, :], ngate[:, qb, 1 + br, :], ALU.mult))
                    dve.wait_ge(S["o_mm"], u - 2)
                    v.tensor_tensor(osc, bank[5 + n % 2][:, :].rearrange("p (h d) -> p h d", h=HEADS),
                                    ogate[:, 1 + br, qb, :].unsqueeze(2).broadcast_to([P, HEADS, DH]), ALU.mult).then_inc(S["o_read"], 1)
                    dve.wait_ge(S["o_read"], n + 1)
                    v.tensor_tensor(oacc[:, qb], oacc[:, qb], osc, ALU.add).then_inc(S["o_acc"], 1)

            for c in range(TB):
                dve.wait_ge(S["bt_turned"], c + 1)
                v.tensor_copy(btok[:, c].rearrange("p g n -> p (g n)"), bank[c % 2][:, :]).then_inc(S["bt_copied"], 1)
            dve.wait_ge(S["acs_mm"], 1)
            flat = lambda a: a.rearrange("p c h -> p (c h)")
            then(v.tensor_copy(flat(acs), bank[4][:, 0:64]))
            v.tensor_scalar(negacs, acs, -1.0, None, ALU.mult).then_inc(S["acs_neg"], 1)
            v.tensor_tensor(flat(decin), bank[4][:, 64:128], flat(acs), ALU.subtract).then_inc(S["acs_neg"], 1)
            v.tensor_copy(flat(cdec), bank[4][:, 64:128]).then_inc(S["acs_neg"], 1)

            def caps(n):
                c, g = groups[n]
                dve.wait_ge(S["seg_mm"], n + 1)
                for e in range(SE):
                    v.scalar_tensor_tensor(out=segd[n % 2][:, e, :], in0=bank[n % 2][:, e * P:(e + 1) * P],
                                           scalar=negacs[:, c, g * SE + e:g * SE + e + 1], in1=cap,
                                           op0=ALU.add, op1=ALU.min).then_inc(S["seg_cap"], 1)

            def weigh(n):
                dve.wait_ge(S["seg_exp"], n + 1)
                if n >= 2:
                    dve.wait_ge(S["y_mm"], n - 1)
                v.tensor_tensor(segm[n % 2], segd[n % 2], bank[2 + n % 2][:, 0:P].unsqueeze(1).broadcast_to([P, SE, P]),
                                ALU.mult).then_inc(S["seg_done"], 1)

            def heads_of(a, g):
                return a[:, g * SE:(g + 1) * SE].unsqueeze(2).broadcast_to([P, SE, SP])

            dve.wait_ge(S["o_turned"], TB)
            dve.wait_ge(S["acs_exp"], 3)
            dve.wait_ge(S["acs_neg"], 3)
            dve.wait_ge(S["z_silu"], 2 * TB)
            caps(0)
            weigh(0)
            for n, (c, g) in enumerate(groups):
                if g == 0:
                    dve.wait_ge(S["xt_copied"], 2 * (c + 1))
                    if c >= 2:
                        dve.wait_ge(S["xdd_done"], c - 1)
                    v.tensor_tensor(xdt[c % 2].rearrange("p (h d) -> p h d", h=SH), ytok[:, c, :].rearrange("p (h d) -> p h d", h=SH),
                                    dt[:, c, :].unsqueeze(2).broadcast_to([P, SH, SP]), ALU.mult).then_inc(S["xdt_done"], 1)
                if n + 1 < 16:
                    caps(n + 1)
                dve.wait_ge(S["y_mm"], n + 1)
                yb = bank[4 + n % 2]
                h4 = lambda a: a.rearrange("p (h d) -> p h d", h=SE)
                dve.wait_ge(S["xsd_done"], c + 1)
                dst = h4(ytok[:, c, g * 256:(g + 1) * 256])
                x4 = h4(xsd[:, g * 256:(g + 1) * 256])
                if c > 0:
                    then(v.tensor_tensor(yoff, h4(yb[:, 256:512]), heads_of(eacs[:, c, :], g), ALU.mult))
                    then(v.tensor_tensor(yoff, yoff, x4, ALU.add))
                    v.tensor_tensor(dst, h4(yb[:, 0:256]), yoff, ALU.add).then_inc(S["y_read"], 1)
                else:
                    v.tensor_tensor(dst, h4(yb[:, 0:256]), x4, ALU.add).then_inc(S["y_read"], 1)
                if c < TB - 1:
                    stb = bank[6 + n % 2]
                    hg = h4(hst[:, g, :])
                    dve.wait_ge(S["st_mm"], n + 1)
                    if c == 0:
                        v.tensor_copy(hst[:, g, :], stb[:, 0:256]).then_inc(S["st_new"], 1)
                    else:
                        then(v.tensor_tensor(hg, hg, heads_of(cdec[:, c, :], g), ALU.mult))
                        v.tensor_tensor(hg, h4(stb[:, 0:256]), hg, ALU.add).then_inc(S["st_new"], 1)
                if n + 1 < 16:
                    weigh(n + 1)
                if g == SG - 1:
                    dve.wait_ge(S["y_read"], n + 1)
                    v.tensor_tensor(ytok[:, c, :], ytok[:, c, :], zs[:, c, :], ALU.mult).then_inc(S["y_gated"], 1)
            dve.wait_ge(S["y_sq"], 16)
            v.tensor_scalar(yrt, yss, 1.0 / 256, LN_EPS, ALU.mult, ALU.add).then_inc(S["y_ms"], 1)
            dve.wait_ge(S["y_sd"], 1)
            then(v.reciprocal(yrs, yrt))
            for c in range(TB):
                y4 = ytok[:, c, :].rearrange("p (g d) -> p g d", g=SG)
                v.tensor_tensor(y4, y4, yrs[:, c, :].unsqueeze(2).broadcast_to([P, SG, 256]), ALU.mult).then_inc(S["y_norm"], 1)

            def gated(j, first):
                if not first:
                    dve.wait_ge(S["mT_done"], j)
                for s in range(3):
                    dve.wait_ge(S["gate_sig"], j * 3 + (s + 1))
                    dve.wait_ge(S["br_mm"], j * 3 + (s + 1))
                    v.tensor_tensor(gm[s], gsb[s], bank[3 + s][:, :], ALU.mult).then_inc(S["br_used"], 1)
                dve.wait_ge(S["br_used"], j * 3 + 3)
                v.tensor_tensor(gm[0], gm[0], gm[1], ALU.add).then_inc(S["m_add"], 1)
                dve.wait_ge(S["m_add"], j + 1)
                dst = mT[:, 0, :] if first else mT[:, bass.ds(j, 1), :].rearrange("p a t -> p (a t)")
                v.tensor_tensor(dst, gm[0], gm[2], ALU.add).then_inc(S["mT_done"], 1)

            gated(0, True)
            with dve.Fori(1, KT) as j:
                gated(j, False)
            for b in range(TB):
                dve.wait_ge(S["mix_read"], b + 1)
                then(stats_of(b, [n1[:, b, 0:512], n1[:, b, 512:1024]]))
            add_eps()
            dve.wait_ge(S["ln_sd"], 2)
            then(v.reciprocal(rstd, sdev))
            for b in range(TB):
                v.tensor_scalar(n1[:, b, :], n1[:, b, :], mv[:, b, 0:1], rstd[:, b:b + 1], ALU.subtract, ALU.mult).then_inc(S["ln_norm"], 1)
            turned_to(h1T, KT, C_LN1G, C_LN1B)

            b16 = lambda a: a.unsqueeze(2).broadcast_to([P, TB, NE])
            dve.wait_ge(S["rt_mm"], 1)
            lg_in = bank[0][:, 0:TB * NE].rearrange("p (b e) -> p b e", b=TB)
            then(v.tensor_reduce(lmax, lg_in, AX.X, ALU.max))
            v.tensor_tensor(lg, lg_in, b16(lmax), ALU.subtract).then_inc(S["rt_max"], 1)
            dve.wait_ge(S["rt_exp"], 1)
            then(v.tensor_reduce(lsum, lg, AX.X, ALU.add))
            then(v.reciprocal(lsum, lsum))
            then(v.tensor_tensor(prob, lg, b16(lsum), ALU.mult))
            then(v.tensor_tensor(score, prob, rowv[:, R_RB:R_RB + NE].unsqueeze(1).broadcast_to([P, TB, NE]), ALU.add))

            def ranks(dst, vals, n):
                other = vals.unsqueeze(2).broadcast_to([P, n, 4, 4])
                own = vals.unsqueeze(3).broadcast_to([P, n, 4, 4])
                low = lower.unsqueeze(1).broadcast_to([P, n, 4, 4])
                a, b = gt[:, 0:n], ge[:, 0:n]
                then(v.tensor_tensor(a, other, own, ALU.is_gt))
                then(v.tensor_tensor(b, other, own, ALU.is_equal))
                then(v.tensor_tensor(b, b, low, ALU.mult))
                then(v.tensor_tensor(a, a, b, ALU.add))
                then(v.tensor_reduce(dst, a, AX.X, ALU.add))

            by4 = lambda a: a.rearrange("p b (g i) -> p (b g) i", g=4)
            ranks(rank, by4(score), 4 * TB)
            then(v.tensor_scalar(by4(sel), rank, 1.5, None, ALU.is_lt))
            then(v.tensor_tensor(ssel, sel, score, ALU.mult))
            then(v.tensor_reduce(gsc.rearrange("p b g -> p (b g)"), by4(ssel), AX.X, ALU.add))
            ranks(grank, gsc, TB)
            then(v.tensor_scalar(ing, grank, 0.5, None, ALU.is_lt))
            then(v.tensor_tensor(by4(sel), by4(sel), ing.rearrange("p b g -> p (b g)").unsqueeze(2).broadcast_to([P, 4 * TB, 4]), ALU.mult))
            then(v.tensor_tensor(selp, sel, prob, ALU.mult))
            then(v.tensor_reduce(wden, selp, AX.X, ALU.add))
            then(v.reciprocal(wden, wden))
            then(v.tensor_tensor(comb, selp, b16(wden), ALU.mult))

            for n in range(2 * TB):
                b, half = divmod(n, 2)
                dve.wait_ge(S["res_mm"], n + 1)
                v.tensor_copy(ysum[:, b, half * 512:(half + 1) * 512], bank[6 + n % 2][:, :]).then_inc(S["res_done"], 1)

            def expert(i, slot, first):
                for f in range(FT):
                    dve.wait_ge(S["up_silu"], (i * 2 + slot) * FT + (f + 1))
                    dve.wait_ge(S["up_mm"], (i * 2 + slot) * 2 * FT + (2 * f + 2))
                    if not first:
                        dve.wait_ge(S["dn_mm"], (i * 2 + slot) * 2 * TB)
                    v.tensor_tensor(hid[:, f, :], up[f % 2], bank[2 * (f % 2) + 1][:, :], ALU.mult).then_inc(S["hid_done"], 1)
                for n in range(2 * TB):
                    b, half = divmod(n, 2)
                    dve.wait_ge(S["dn_mm"], (i * 2 + slot) * 2 * TB + (n + 1))
                    if not first:
                        dve.wait_ge(S["dn_used"], (i * 2 + slot) * 2 * TB)
                    y = ysum[:, b, half * 512:(half + 1) * 512]
                    w = comb[:, b, slot:slot + 1] if isinstance(i, int) else comb[:, b, bass.ds(i * 2 + slot, 1)]
                    v.scalar_tensor_tensor(out=y, in0=bank[4 + n % 4][:, :], scalar=w, in1=y, op0=ALU.mult, op1=ALU.add
                                           ).then_inc(S["dn_used"], 1)

            dve.wait_ge(S["res_done"], 2 * TB)
            expert(0, 0, True)
            expert(0, 1, False)
            with dve.Fori(1, NE // 2) as i:
                expert(i, 0, False)
                expert(i, 1, False)

            dve.wait_ge(S["dn_used"], NE * 2 * TB)
            for b in range(TB):
                then(stats_of(b, [ysum[:, b, 0:512], ysum[:, b, 512:1024]]))
            add_eps()
            dve.wait_ge(S["ln_sd"], 3)
            then(v.reciprocal(rstd, sdev))
            dve.wait_ge(S["ld_ln"], 32)
            for b in range(TB):
                y, o = ysum[:, b, :], obuf[:, b % 2, :]
                then(v.tensor_scalar(y, y, mv[:, b, 0:1], rstd[:, b:b + 1], ALU.subtract, ALU.mult))
                then(v.tensor_tensor(y, y, lnr[:, 0, :], ALU.mult))
                if b >= 2:
                    dve.wait_ge(st_ob[b % 2], 16)
                v.tensor_tensor(o, y, lnr[:, 1, :], ALU.add).then_inc(S["ln2_out"], 1)


def shape_constants():
    fixed = np.zeros((P, K_END), np.float32)
    fixed[:, K_ID:K_ID + P] = np.eye(P)
    s, l = np.arange(P)[:, None], np.arange(P)[None, :]
    fixed[:, K_TRI:K_TRI + P] = s <= l
    fixed[:, K_CAP:K_CAP + P] = np.where(s <= l, -NEG, NEG)
    fixed[:, K_AID:K_AID + P] = np.eye(P) * ALPHA
    fixed[:, K_ONE:K_ONE + P] = 1.0
    fixed[:, K_ROW] = np.arange(P) >= CMP_LEN - 1
    fixed[:, K_LOW:K_LOW + 16] = (np.arange(4)[None, :] < np.arange(4)[:, None]).reshape(-1)
    for g, w in enumerate(WINDOWS):
        fixed[:, K_INV + 16 * g:K_INV + 16 * (g + 1)] = 1.0 / np.minimum(np.arange(16) + 1, w)
    dist = T - 1 - np.arange(REVN)
    n = np.maximum(dist, 0)
    exact = BUCKETS // 2
    nf = np.maximum(n, 1).astype(np.float32)
    large = exact + (np.log(nf / np.float32(exact)) / np.float32(math.log(MAX_DIST / exact)) * np.float32(BUCKETS - exact)).astype(np.int32)
    bucket = np.where(n < exact, n, np.minimum(large, BUCKETS - 1))
    onehot = np.zeros((BUCKETS + 1, REVN), np.float32)
    onehot[np.where(dist < 0, BUCKETS, bucket), np.arange(REVN)] = 1.0
    return fixed, onehot


def kernel(**inputs):
    import concourse.bacc as bacc
    from concourse.bass_utils import run_bass_kernel_spmd

    a = {k: np.asarray(v) for k, v in inputs.items()}
    w_in = a["w_in"][0]
    c_pool, c_q, c_kv = 0, 512, 1024
    c_ng = c_kv + 768
    c_ssd = c_ng + 24
    c_gate = c_ssd + 3088

    def lhs(w):
        return w.reshape(KT, P, P).transpose(1, 0, 2).reshape(P, D)

    cols128 = lambda c: w_in[:, c:c + P]
    tiles = [cols128(c_kv), cols128(c_kv + P), cols128(c_kv + 2 * P), cols128(c_kv + 4 * P)]
    for i in range(HPG):
        tiles.append(np.concatenate([w_in[:, c_q + i * DH:c_q + (i + 1) * DH],
                                     w_in[:, c_q + (HPG + i) * DH:c_q + (HPG + i + 1) * DH]], axis=1))
    tiles += [cols128(c_pool + i * P) for i in range(4)]
    tiles += [cols128(c_ssd + D + i * P) for i in range(16)]
    assert len(tiles) == CM_PROJ
    for j in range(KT):
        sl = slice(j * P, (j + 1) * P)
        tiles += [cols128(c_gate + b * D + j * P) for b in range(3)]
        tiles.append(np.concatenate([a["w_br_pool"][0][:, sl], a["w_br_nsa"][0][:, sl]], axis=0))
        tiles.append(a["w_br_ssd"][0][:, sl])
    w_cm = np.stack([lhs(w) for w in tiles])

    def rhs(w):
        return w.reshape(-1, P, w.shape[1]).transpose(1, 0, 2)

    w_tm = np.stack([rhs(w_in[:, c_ssd + h * 512:c_ssd + (h + 1) * 512]) for h in range(2)])
    w_vd = rhs(np.concatenate([cols128(c_kv + 3 * P), cols128(c_kv + 5 * P), w_in[:, c_ssd + 3072:c_ssd + 3088],
                               w_in[:, c_ng:c_ng + 24]], axis=1))
    percol = lambda u: u.reshape(-1, P).T
    cols = np.concatenate([
        percol(a["ln0_g"]), percol(a["ln0_b"]), percol(a["ln1_g"][0]), percol(a["ln1_b"][0]), percol(a["pool_scale"][0]),
        percol(a["conv_w"][0].reshape(-1)), percol(a["conv_b"][0]), percol(a["ssd_norm_g"][0]),
        percol(a["cmp_k_pe"][0].reshape(-1)), percol(a["cmp_v_pe"][0].reshape(-1))], axis=1)
    rows = np.concatenate([a["dt_bias"][0], a["a_log"][0], a["d_skip"][0], a["router_b"]])[None]
    fixed, onehot = shape_constants()
    table = np.concatenate([a["rel_bias"], np.full((1, HEADS), NEG, np.float32)], axis=0)
    e13 = np.stack([a["exp_w1"][0], a["exp_w3"][0]], axis=1).reshape(NE, 2, KT, P, DE).transpose(0, 3, 1, 2, 4)
    arrays = {
        "x": a["x"][0], "w_cm": w_cm, "w_tm": w_tm, "w_vd": w_vd, "cols": cols, "rows": rows,
        "lnrows": np.stack([a["ln2_g"][0], a["ln2_b"][0]]), "fixed": fixed, "onehot": onehot, "table": table,
        "pool_w": a["pool_w"][0].transpose(1, 0, 2),
        "w1c_in": np.stack([rhs(a["cmp_k_w1"][0]), rhs(a["cmp_v_w1"][0])], axis=1),
        "w2kv": np.stack([a["cmp_k_w2"][0], a["cmp_v_w2"][0]], axis=1),
        "w_out": np.stack([rhs(a["w_out"][0][:, h * 512:(h + 1) * 512]) for h in range(2)]),
        "w_rt": rhs(a["router_w"]),
        "e13": e13, "e2": a["exp_w2"][0].reshape(NE, FT, P, D).transpose(0, 2, 1, 3),
    }
    nc = bacc.Bacc("TRN2", target_bir_lowering=False, num_devices=1)
    handles = {}
    for name in arrays:
        arrays[name] = np.ascontiguousarray(arrays[name])
        handles[name] = nc.dram_tensor(f"in_{name}", arrays[name].shape, F32, kind="ExternalInput").ap()
    out = nc.dram_tensor("out", (T, D), F32, kind="ExternalOutput").ap()
    bias_dram = nc.dram_tensor("bias_rows", (HEADS, P * (REVN + 1)), F32, kind="Internal").ap()
    build_program(nc, out=out, bias_dram=bias_dram, **handles)
    r = run_bass_kernel_spmd(nc, [{f"in_{k}": v for k, v in arrays.items()}], core_ids=[0])
    return r.results[0]["out"].reshape(1, T, D)
```

```python
import math
from contextlib import ExitStack

import numpy as np
import concourse.bass as bass
from concourse import mybir

F32 = mybir.dt.float32
ALU = mybir.AluOpType
ACT = mybir.ActivationFunctionType
AX = mybir.AxisListType

P = 128
T = 512
D = 1024
TB = T // P
KT = D // P
ALPHA = 2.0 ** 0.25
LN_EPS = 1e-5
NEG = -1e30

HEADS, KVG, HPG, DH = 8, 2, 4, 64
BUCKETS = 32
MAX_DIST = 128
CMP_LEN, CMP_STRIDE = 32, 16
NCMP = (T - CMP_LEN) // CMP_STRIDE + 1
WINDOWS = (2, 4, 8, 16)

SG, SE, SP, SN = 4, 4, 64, 128
SH = SG * SE
NE, DE = 16, 512
FT = DE // P
SPARE = (2 * T - NE) // P

CM_PROJ = 28
EARLY = 3
CM_EARLY = CM_PROJ + 3 * EARLY
CM_LOOP = CM_EARLY + 2 * EARLY
BR_TILES = 5
SLOTS = 5
VD = 2 * P + SH + 3 * HEADS
REVN = T + P

C_LN0G, C_LN0B, C_LN1G, C_LN1B, C_PS, C_CW, C_CB, C_NG, C_PEK, C_PEV, C_END = (
    0, 8, 16, 24, 32, 36, 100, 116, 124, 140, 156)
K_ID, K_TRI, K_CAP, K_AID, K_ONE, K_ROW, K_LOW, K_INV, K_EID, K_EOFF, K_THR, K_SPI, K_LOW16, K_END = (
    0, 128, 256, 384, 512, 640, 641, 657, 721, 737, 753, 756, 763, 1019)
R_DTB, R_ALOG, R_DSK, R_RB = 0, 16, 32, 48


def build_program(nc, x, w_cm, w_tm, w_vd, cols, rows, lnrows, fixed, onehot, table, pool_w, w1c_in, w2kv,
                  w_out, w_rt, e13, e2, out, bias_dram, xs_dram, ys_dram):
    with ExitStack() as ctx:
        def sb(name, shape):
            return ctx.enter_context(nc.sbuf_tensor(name, shape, F32))

        def sem(name):
            return ctx.enter_context(nc.semaphore(name))

        bank = [ctx.enter_context(nc.psum_tensor(f"bank{i}", [P, 512], F32)) for i in range(8)]

        r_mid = sb("r_mid", [P, 4096 + SLOTS * D + 4096])
        r_h, r_ring, r_qkv = (r_mid[:, a:b] for a, b in ((0, 4096), (4096, 9216), (9216, 13312)))
        r_big = sb("r_big", [P, 6 * 4096])
        r_tmp = sb("r_tmp", [P, 5632])
        r_late = sb("r_late", [P, 6144])
        r_o, r_oT, r_pool = (r_late[:, i * 2048:(i + 1) * 2048] for i in range(3))
        colv = sb("colv", [P, C_END])
        fix = sb("fix", [P, K_END])
        rowv = sb("rowv", [P, 4 * SH])
        small = sb("small", [P, 1280])
        vbd = sb("vbd", [P, KVG, HPG, DH])
        kcT = sb("kcT", [P, NCMP])

        def view(region, off, *dims):
            v = region[:, off:off + int(np.prod(dims))]
            names = "abcde"[:len(dims)]
            if len(dims) == 1:
                return v
            return v.rearrange(f"p ({' '.join(names)}) -> p {' '.join(names)}",
                               **{n: d for n, d in zip(names[1:], dims[1:])})

        hT = view(r_h, 0, KT, T)
        ring = view(r_ring, 0, SLOTS, KT, P)
        h1T = view(r_ring, 0, KT, T)
        zs = view(r_big, 0, TB, D)
        ytok = view(r_big, 4096, TB, D)
        xsT = view(r_big, 8192, 8, T)
        yT = view(r_big, 12288, 8, T)
        bcT = view(r_big, 16384, 8, T)
        strips = view(r_big, 20480, HEADS, T)
        btok = view(r_big, 20480, TB, SG, SN)
        xin = view(r_big, 0, TB, D)
        xnorm = view(r_big, 4096, TB, D)
        wz = [view(r_big, 12288, KT, 512), view(r_big, 4096, KT, 512)]
        wvd = view(r_big, 8192, KT, VD)
        w1c = view(r_big, 16384, 2, 16, P)
        wo = view(r_big, 16384, 2, KT, 512)
        qT = view(r_qkv, 0, 4, T)
        kT = [view(r_qkv, 2048, T), view(r_qkv, 2560, T)]
        vtok = view(r_qkv, 3072, TB, 2, KVG, DH)
        mT = view(r_qkv, 0, KT, T)
        early = [view(r_big, 22528 + 512 * m, T) for m in range(4)] + [view(r_qkv, 512 * m, T) for m in range(EARLY, KT)]
        tok2 = view(r_o, 0, 2, KVG, T)
        oacc = view(r_o, 0, TB, HEADS, DH)
        oT = view(r_oT, 0, 4, T)
        pcs = view(r_oT, 0, TB, HEADS, 32)
        pct = view(r_oT, 1024, 2, 2, P)
        poolT = view(r_pool, 0, 4, T)
        blocks = view(r_pool, 0, 2, CMP_LEN // 2, KVG, NCMP)

        ident, tri, cap, aident, ones = (fix[:, k:k + P] for k in (K_ID, K_TRI, K_CAP, K_AID, K_ONE))
        rowok = fix[:, K_ROW:K_ROW + 1]
        eid = fix[:, K_EID:K_EID + NE]
        eoff = fix[:, K_EOFF:K_EOFF + NE]
        thr = fix[:, K_THR:K_THR + 3]
        spare_i = fix[:, K_SPI:K_SPI + SPARE]
        lower16 = fix[:, K_LOW16:K_LOW16 + NE * NE].rearrange("p (i j) -> p i j", i=NE)
        lower = fix[:, K_LOW:K_LOW + 16].rearrange("p (i j) -> p i j", i=4)
        invc = fix[:, K_INV:K_INV + 64].rearrange("p (g w) -> p g w", g=4)

        used = [0]

        def sm(*dims):
            n = int(np.prod(dims))
            used[0] += n
            assert used[0] <= 1280
            return view(small, used[0] - n, *dims)

        stats, mv, sdev, rstd = sm(TB, 2, 6), sm(TB, 2), sm(TB), sm(TB)
        dtx, dtm, dte, dt, dta = sm(TB, SH), sm(TB, SH), sm(TB, SH), sm(TB, SH), sm(TB, SH)
        acs, negacs, eacs, decin, cdec = sm(TB, SH), sm(TB, SH), sm(TB, SH), sm(TB, SH), sm(TB, SH)
        expa = sm(SH)
        ngate = sm(TB, 3, HEADS)
        nmax, psums = sm(2, TB, HEADS), sm(2, TB, HEADS)
        ogate = sm(3, TB, HEADS)
        cmax, csum = sm(TB, HEADS), sm(TB, HEADS)
        yss, yrt, yrs = sm(TB, SG), sm(TB, SG), sm(TB, SG)
        slot_wt = sm(TB, 2)
        slot_no = sm(TB, 2).bitcast(mybir.dt.uint32)
        spare_info = sm(SPARE + 1).bitcast(mybir.dt.int32)

        onehot_sb, table_sb = r_tmp[0:BUCKETS + 1, 0:REVN], r_tmp[0:BUCKETS + 1, REVN:REVN + HEADS]
        bias_sb = r_tmp[0:HEADS, 700:700 + REVN]
        w2c = view(r_tmp, 1400, 2, DH)
        hidc = view(r_tmp, 1600, 2, KVG, NCMP)
        poolw = view(r_tmp, 1800, 4, P)
        praw = view(r_tmp, 2320, T + 16)
        pw = [view(r_tmp, 2320 + 528 * (i + 1), T + 16) for i in range(2)]
        pr = view(r_tmp, 3904, T)
        att_s = [view(r_tmp, 512 * i, 512) for i in range(3)]
        att_p = [view(r_tmp, 1536 + 512 * i, 512) for i in range(3)]
        att_pt = [view(r_tmp, 3072 + 512 * i, 4, P) for i in range(3)]
        osc = view(r_tmp, 4608, HEADS, DH)
        xdt = [view(r_tmp, 0, D), view(r_o, 0, D)]
        xdd = view(r_tmp, 1024, D)
        xsd = view(r_tmp, 2048, D)
        segd = [view(r_tmp, 3072 + 512 * i, SE, P) for i in range(2)]
        segm = [view(r_tmp, 4096 + 512 * i, SE, P) for i in range(2)]
        yoff = view(r_tmp, 5120, SE, SP)
        hst = view(r_o, 1024, SG, SE * SP)
        gsb = [view(r_tmp, 512 * i, 512) for i in range(3)]
        gm = [view(r_tmp, 1536 + 512 * i, 512) for i in range(3)]
        n1 = view(r_tmp, 0, TB, D)
        wrt = view(r_pool, 0, KT, NE)
        lnr = view(r_late, 0, 2, D)
        ew13 = [view(r, o, 2, KT, DE) for r, o in ((r_big, 0), (r_big, 12288), (r_mid, 0))]
        ew2 = [view(r, o + 8192, FT, D) for r, o in ((r_big, 0), (r_big, 12288), (r_mid, 0))]
        xg = [view(r_late, i * D, D) for i in range(3)]
        xgT = view(r_late, 3 * D, KT, P)
        eout = view(r_late, 4 * D, D)
        upv, hidv, hidT = view(r_tmp, 4096, DE), view(r_tmp, 4608, DE), view(r_tmp, 5120, FT, P)
        by_token = view(r_big, 0, TB, 2, D)
        obuf = view(r_mid, 0, TB, D)
        zeros = view(r_oT, 1536, 512)
        zrow = zeros.unsqueeze(1).broadcast_to([P, 2, 512])

        def rv(k, *dims):
            return view(r_pool, 128 + k * 64, *(dims or (TB, NE)))

        prob, score, lg, sel, ssel, comb, pos, over, slot1 = (rv(k) for k in range(9))
        gt, ge = view(r_pool, 704, TB * 4, 4, 4), view(r_pool, 960, TB * 4, 4, 4)
        big16 = view(r_pool, 704, NE, NE)
        rank, gsc, grank, ing = (view(r_pool, 1216, TB * 4, 4), view(r_pool, 1280, TB, 4),
                                 view(r_pool, 1296, TB, 4), view(r_pool, 1312, TB, 4))
        lmax, lsum, wden = view(r_pool, 1328, TB), view(r_pool, 1332, TB), view(r_pool, 1336, TB)
        slot_a, slot_b = view(r_pool, 1340, TB), view(r_pool, 1344, TB)
        cnt, spn, spx = view(r_pool, 1348, NE), view(r_pool, 1364, NE), view(r_pool, 1380, NE)
        slotf, spf = view(r_pool, 1396, TB, 2), view(r_pool, 1404, SPARE + 1)
        thr_gt = view(r_pool, 1412, NE, 3)
        sp_le = view(r_pool, 1460, SPARE, NE)

        names = """ld_const ld_bias ld_cmp ld_vd ld_strip ld_poolw st_bias ld_wo ld_rt ld_ln st_out
            ln_stat ln_sd ln_rstd ln_norm ln_turned hT_act hT_dve
            proj_done act_freed dve_freed cmp_in cmp_mm cmp_hid cmp2_mm cmp_kc cmp_vc bias_mm bias_rows zeroed
            vd_mm vd_used z_mm z_silu pool_in pool_out pool_mm pool_scaled conv_first conv_sum conv_done dv ac gp
            soft_abs soft_ln decay_a gates_e sc_mm sc_max p_done p_turned pt_copied o_mm o_read o_acc o_turned oT_copied
            cs_mm cs_sub cs_exp cs_turned cs_copied co_mm co_read gate_w
            acs_mm acs_neg acs_exp bt_turned bt_copied xt_turned xt_copied xdt_done xdd_done xsd_done
            seg_mm seg_cap seg_exp seg_done y_mm y_read early_out st_mm st_new y_gated y_sq y_ms y_sd y_norm y_turned yT_done
            gate_mm gate_sig br_mm br_used m_add mT_done mix_mm mix_read rt_mm rt_max rt_exp comb_done
            zero_tile zeroed_x zeroed_y sel_done pos_mm slots_done ld_ln1 tok_dve tok_gp st_h x_turned xT_act xT_dve
            up_mm up_silu hid_done h_turned hidT_done dn_mm out_act out_dve st_y back_a ln2_out""".split()
        S = {n: sem(n) for n in names}
        ld_x = [sem(f"ld_x{i}") for i in range(TB)]
        ld_z = [sem(f"ld_z{i}") for i in range(2)]
        ld_ring = [sem(f"ld_ring{i}") for i in range(SLOTS)]
        ld_w13 = [sem(f"ld_w13_{i}") for i in range(3)]
        ld_w2 = [sem(f"ld_w2_{i}") for i in range(3)]
        ld_xg = [sem(f"ld_xg{i}") for i in range(3)]
        ld_back = [sem(f"ld_back{i}") for i in range(TB)]

        NCONST = 3
        CMP_AT = 15

        def release(i):
            if i < 2:
                return S["dve_freed"], i + 1
            if i < 12:
                return S["act_freed"], i - 1
            return S["conv_sum"], 3 * (i - 11)

        units = [(br, qb, h) for br in range(2) for qb in range(TB) for h in range(HEADS)]
        nvalid = [7 + 8 * qb for qb in range(TB)]
        groups = [(c, g) for c in range(TB) for g in range(SG)]
        block = ctx.enter_context(nc.Block())

        @block.sync
        def _(sp):
            for b in range(TB):
                sp.dma_start(xin[:, b, :], x[b * P:(b + 1) * P, :]).then_inc(ld_x[b], 16)
            sp.dma_start(fix[:, :], fixed).then_inc(S["ld_const"], 16)
            sp.dma_start(colv[:, :], cols).then_inc(S["ld_const"], 16)
            sp.dma_start(rowv[:, :], rows.partition_broadcast(P)).then_inc(S["ld_const"], 16)

            def load_tile(i):
                if i >= SLOTS:
                    sp.wait_ge(S["proj_done"], i - SLOTS + 1)
                sp.dma_start(ring[:, i % SLOTS, :, :], w_cm[i].rearrange("p (k n) -> p k n", k=KT)
                             ).then_inc(ld_ring[i % SLOTS], 16)

            for i in range(4):
                load_tile(i)
            sp.dma_start(w1c, w1c_in).then_inc(S["ld_cmp"], 16)
            sp.dma_start(w2c, w2kv).then_inc(S["ld_cmp"], 16)
            sp.dma_start(onehot_sb, onehot).then_inc(S["ld_bias"], 16)
            sp.dma_start(table_sb, table).then_inc(S["ld_bias"], 16)
            for i in range(4, 8):
                load_tile(i)
            sp.dma_start(wvd, w_vd).then_inc(S["ld_vd"], 16)
            load_tile(8)
            sp.dma_start(poolw, pool_w).then_inc(S["ld_poolw"], 16)
            for i in range(9, 12):
                load_tile(i)
            sp.wait_ge(S["bias_rows"], 2)
            skewed = bass.AP(bias_dram.tensor, 0, [[P * (REVN + 1), HEADS], [REVN + 1, P], [1, REVN]])
            sp.dma_start(skewed, bias_sb.unsqueeze(1).broadcast_to([HEADS, P, REVN])).then_inc(S["st_bias"], 16)
            sp.wait_ge(S["st_bias"], 16)
            strip_src = bass.AP(bias_dram.tensor, P - 1, [[REVN, P], [P * (REVN + 1), HEADS], [1, T]])
            sp.dma_start(strips, strip_src).then_inc(S["ld_strip"], 16)
            for i in range(12, CM_PROJ):
                load_tile(i)
                if i == 12:
                    sp.wait_ge(S["zero_tile"], 1)
                for n in range(2 * (i - 12), 2 * (i - 11)):
                    if n < NE + SPARE:
                        sp.dma_start(xs_dram[n * P:(n + 1) * P, :].rearrange("p (a n) -> p a n", a=2), zrow).then_inc(S["zeroed_x"], 16)
                    elif n < NE + 2 * SPARE:
                        m = n - SPARE
                        sp.dma_start(ys_dram[m * P:(m + 1) * P, :].rearrange("p (a n) -> p a n", a=2), zrow).then_inc(S["zeroed_y"], 16)
                if i in (14, 20):
                    sp.dma_start(wz[i // 20], w_tm[i // 20]).then_inc(ld_z[i // 20], 16)

            for i in range(CM_PROJ, CM_EARLY):
                load_tile(i)

            def load_slot(s, tile):
                src = w_cm[bass.ds(tile, 1), :, :].rearrange("a p (k n) -> (a p) k n", k=KT)
                sp.dma_start(ring[:, s, :, :], src).then_inc(ld_ring[s], 16)

            sp.wait_ge(S["proj_done"], CM_EARLY)
            for s in (3, 4):
                load_slot(s, CM_EARLY + s - 3)
            for s in range(3):
                load_slot(s, CM_LOOP + s)
            sp.wait_ge(S["y_mm"], 16)
            sp.dma_start(wo[:, 0], w_out[0]).then_inc(S["ld_wo"], 16)
            for j in range(1, EARLY + 1):
                for s in (3, 4):
                    sp.wait_ge(S["br_mm"], j * 3 + (s - 4))
                    load_slot(s, (CM_EARLY + 2 * j if j < EARLY else CM_LOOP + 3) + s - 3)
            sp.wait_ge(S["gate_sig"], 3 * EARLY)
            sp.dma_start(wo[:, 1], w_out[1]).then_inc(S["ld_wo"], 16)
            with sp.Fori(EARLY + 1, KT) as j:
                for s in range(BR_TILES):
                    if s < 3:
                        sp.wait_ge(S["gate_mm"], j * 3 + (s - 2 - 3 * EARLY))
                    else:
                        sp.wait_ge(S["br_mm"], j * 3 + (s - 4))
                    load_slot(s, CM_LOOP + s - BR_TILES * EARLY + j * BR_TILES)

            def load_expert(e, slot):
                src13, src2 = e13[bass.ds(e, 1)], e2[bass.ds(e, 1)]
                sp.dma_start(ew13[slot], src13.rearrange("a p m k f -> (a p) m k f")).then_inc(ld_w13[slot], 16)
                return src2

            def load_w2(src2, slot):
                sp.dma_start(ew2[slot], src2.rearrange("a p k n -> (a p) k n")).then_inc(ld_w2[slot], 16)

            def load_tokens(tile, buf):
                sp.dma_start(xg[buf], xs_dram[bass.ds(tile * P, P), :]).then_inc(ld_xg[buf], 16)

            sp.wait_ge(S["y_turned"], 2 * TB)
            load_w2(load_expert(0, 0), 0)
            sp.wait_ge(S["mT_done"], KT)
            sp.dma_start(wrt, w_rt).then_inc(S["ld_rt"], 16)
            for i in range(2):
                sp.dma_start(lnr[:, i, :], lnrows[i:i + 1, :].partition_broadcast(P)).then_inc(S["ld_ln1"], 16)
            sp.wait_ge(S["mix_mm"], TB)
            load_w2(load_expert(1, 1), 1)
            sp.wait_ge(S["rt_mm"], 1)
            load_w2(load_expert(2, 2), 2)
            sp.wait_ge(S["st_h"], 16 * 2 * TB)
            for e in range(3):
                load_tokens(e, e)

            def refill(e, slot):
                sp.wait_ge(S["x_turned"], e * 2 - 4)
                load_tokens(e, slot)
                sp.wait_ge(S["up_mm"], e * 2 - 4)
                src2 = load_expert(e, slot)
                sp.wait_ge(S["dn_mm"], e * 2 - 4)
                load_w2(src2, slot)

            refill(3, 0)
            with sp.Fori(1, (NE - 1) // 3) as i:
                for d in (1, 2, 3):
                    refill(i * 3 + d, d % 3)
            n_spare = sp.value_load(spare_info[0:1, SPARE:SPARE + 1], min_val=0, max_val=SPARE)
            with sp.Fori(0, SPARE) as i:
                with sp.If(i < n_spare):
                    e = sp.value_load(spare_info[0:1, bass.ds(i, 1)], min_val=0, max_val=NE - 1)
                    sp.wait_ge(S["dn_mm"], (i + NE) * 2)
                    load_tokens(i + NE, 0)
                    load_w2(load_expert(e, 0), 0)
            sp.wait_ge(S["back_a"], 1)
            for i in range(2):
                sp.dma_start(lnr[:, i, :], lnrows[2 + i:3 + i, :].partition_broadcast(P)).then_inc(S["ld_ln"], 16)
            for b in range(TB):
                sp.wait_ge(S["ln2_out"], b + 1)
                sp.dma_start(out[b * P:(b + 1) * P, :], obuf[:, b, :]).then_inc(S["st_out"], 16)
            sp.wait_ge(S["st_out"], 16 * TB)

        @block.tensor
        def _(pe):
            mm = nc.tensor.matmul
            tr = nc.tensor.transpose
            pe.wait_ge(S["ld_const"], 16 * NCONST)
            pe.wait_ge(S["ln_norm"], TB)
            for k in range(KT):
                for b in range(TB):
                    last = tr(bank[k][:, b * P:(b + 1) * P], xnorm[:, b, k * P:(k + 1) * P], ident)
                last.then_inc(S["ln_turned"], 1)

            def proj(i):
                pe.wait_ge(ld_ring[i % SLOTS], 16 * (i // SLOTS + 1))
                if i >= 2:
                    pe.wait_ge(*release(i - 2))
                for k in range(KT):
                    last = mm(bank[i % 2][:, :], ring[:, i % SLOTS, k, :], hT[:, k, :], start=(k == 0), stop=(k == KT - 1))
                last.then_inc(S["proj_done"], 1)

            pe.wait_ge(S["hT_act"], KT // 2)
            pe.wait_ge(S["hT_dve"], KT // 2)
            for i in range(8):
                proj(i)

            pe.wait_ge(S["ld_cmp"], 32)
            for kv in range(2):
                pe.wait_ge(S["cmp_in"], 2 * kv + 2)
                for l in range(CMP_LEN // 2):
                    last = mm(bank[2 + kv][:, 0:KVG * NCMP], w1c[:, kv, l, :], blocks[:, kv, l, :, :].rearrange("p g n -> p (g n)"),
                              start=(l == 0), stop=(l == CMP_LEN // 2 - 1))
                last.then_inc(S["cmp_mm"], 1)
            pe.wait_ge(S["ld_bias"], 32)
            for i in range(2):
                mm(bank[6 + i][0:HEADS, 0:REVN // 2], table_sb, onehot_sb[:, i * REVN // 2:(i + 1) * REVN // 2],
                   start=True, stop=True).then_inc(S["bias_mm"], 1)
            pe.wait_ge(S["cmp_hid"], 2)
            for g in range(KVG):
                mm(bank[4][g * DH:(g + 1) * DH, 0:NCMP], w2c[:, 0, :], hidc[:, 0, g, :], start=True, stop=True)
            for g in range(KVG):
                for h in range(HPG):
                    last = mm(bank[5][32 * h:32 * h + NCMP, g * DH:(g + 1) * DH], hidc[:, 1, g, :], w2c[:, 1, :],
                              start=True, stop=True)
            last.then_inc(S["cmp2_mm"], 1)
            pe.wait_ge(S["ld_vd"], 16)
            pe.wait_ge(S["cmp_kc"], 1)
            pe.wait_ge(S["cmp_vc"], HPG)
            for b in range(TB):
                for k in range(KT):
                    last = mm(bank[2 + b][:, 0:VD], hT[:, k, b * P:(b + 1) * P], wvd[:, k, :], start=(k == 0), stop=(k == KT - 1))
                last.then_inc(S["vd_mm"], 1)

            def cmp_scores(qb):
                if qb == 0:
                    pe.wait_ge(S["act_freed"], 6)
                    pe.wait_ge(S["cmp_kc"], 1)
                    pe.wait_ge(S["vd_used"], TB)
                else:
                    pe.wait_ge(S["cs_sub"], qb)
                nv = nvalid[qb]
                for h in range(HEADS):
                    g, i = divmod(h, HPG)
                    last = mm(bank[2 + g][:, 32 * h:32 * h + nv], qT[g * DH:(g + 1) * DH, i, qb * P:(qb + 1) * P],
                              kcT[g * DH:(g + 1) * DH, 0:nv], start=True, stop=True)
                last.then_inc(S["cs_mm"], 1)

            def cmp_turn(qb):
                pe.wait_ge(S["cs_exp"], qb + 1)
                if qb >= 1:
                    pe.wait_ge(S["cs_copied"], qb)
                for g in range(KVG):
                    last = tr(bank[4][:, g * P:(g + 1) * P], pcs[:, qb, g * HPG:(g + 1) * HPG, :].rearrange("p h n -> p (h n)"), ident)
                last.then_inc(S["cs_turned"], 1)

            def cmp_values(qb):
                pe.wait_ge(S["cs_copied"], qb + 1)
                pe.wait_ge(S["cmp_vc"], HPG)
                if qb >= 1:
                    pe.wait_ge(S["co_read"], qb)
                for g in range(KVG):
                    last = mm(bank[5][:, g * 256:(g + 1) * 256], pct[:, qb % 2, g, :], vbd[:, g, :, :].rearrange("p h d -> p (h d)"),
                              start=True, stop=True)
                last.then_inc(S["co_mm"], 1)

            for i in range(8, CM_PROJ):
                proj(i)
                qb, part = divmod(i - CMP_AT, 3)
                if 0 <= qb < TB:
                    (cmp_scores, cmp_turn, cmp_values)[part](qb)
            pe.wait_ge(S["ld_poolw"], 16)
            pe.wait_ge(S["co_read"], TB)
            for g in range(4):
                pe.wait_ge(S["pool_out"], g + 1)
                mm(bank[2 + g][:, :], poolw[:, g, :], poolT[:, g, :], start=True, stop=True).then_inc(S["pool_mm"], 1)

            def scores(u):
                br, qb, h = units[u]
                g, i = divmod(h, HPG)
                n = (qb + 1) * P
                if u >= 3:
                    pe.wait_ge(S["sc_max"], u - 2)
                mm(bank[u % 3][:, 0:n], qT[g * DH:(g + 1) * DH, i, qb * P:(qb + 1) * P], kT[br][g * DH:(g + 1) * DH, 0:n],
                   start=True, stop=True).then_inc(S["sc_mm"], 1)

            def turn(u):
                br, qb, h = units[u]
                pe.wait_ge(S["p_done"], u + 1)
                if u >= 2:
                    pe.wait_ge(S["pt_copied"], u - 1)
                for kb in range(qb + 1):
                    last = tr(bank[3 + u % 2][:, kb * P:(kb + 1) * P], att_p[u % 3][:, kb * P:(kb + 1) * P], ident)
                last.then_inc(S["p_turned"], 1)

            def values(u):
                br, qb, h = units[u]
                n = br * TB + qb
                pe.wait_ge(S["pt_copied"], u + 1)
                if h == 0 and n >= 2:
                    pe.wait_ge(S["o_read"], n - 1)
                for kb in range(qb + 1):
                    last = mm(bank[5 + n % 2][:, h * DH:(h + 1) * DH], att_pt[u % 3][:, kb, :], vtok[:, kb, br, h // HPG, :],
                              start=(kb == 0), stop=(kb == qb))
                last.then_inc(S["o_mm"], 1)

            def turn_o(qb):
                pe.wait_ge(S["o_acc"], TB + qb + 1)
                if qb >= 1:
                    pe.wait_ge(S["oT_copied"], qb)
                for ct in range(4):
                    last = tr(bank[7][:, ct * P:(ct + 1) * P], oacc[:, qb, 2 * ct:2 * ct + 2, :].rearrange("p h d -> p (h d)"), ident)
                last.then_inc(S["o_turned"], 1)

            def z_product(m):
                n, k = divmod(m, KT)
                half, b = divmod(n, TB)
                if k == 0:
                    if b == 0:
                        pe.wait_ge(ld_z[half], 16)
                    if n == 0:
                        pe.wait_ge(S["bias_rows"], 2)
                    else:
                        pe.wait_ge(S["z_silu"], n)
                last = mm(bank[7][:, :], hT[:, k, b * P:(b + 1) * P], wz[half][:, k, :], start=(k == 0), stop=(k == KT - 1))
                if k == KT - 1:
                    last.then_inc(S["z_mm"], 1)

            pe.wait_ge(S["conv_sum"], 48)
            pe.wait_ge(S["pool_scaled"], 4)
            NU = len(units)
            for u in range(NU + 3):
                if u < NU:
                    scores(u)
                if 2 <= u < NU + 2:
                    turn(u - 2)
                if u >= 3:
                    values(u - 3)
                if u < NU:
                    z_product(u)
            pe.wait_ge(S["z_silu"], 2 * TB)
            for qb in range(TB):
                turn_o(qb)

            for c in range(TB):
                if c >= 2:
                    pe.wait_ge(S["bt_copied"], c - 1)
                if c == 0:
                    pe.wait_ge(S["conv_done"], 16)
                for g in range(SG):
                    last = tr(bank[c % 2][:, g * P:(g + 1) * P], bcT[:, g, c * P:(c + 1) * P], ident)
                last.then_inc(S["bt_turned"], 1)
            for n in range(2 * TB):
                c, half = divmod(n, 2)
                if n >= 2:
                    pe.wait_ge(S["xt_copied"], n - 1)
                else:
                    pe.wait_ge(S["sc_max"], NU)
                for i in range(4):
                    last = tr(bank[2 + n % 2][:, i * P:(i + 1) * P], xsT[:, half * 4 + i, c * P:(c + 1) * P], ident)
                last.then_inc(S["xt_turned"], 1)
            pe.wait_ge(S["decay_a"], 1)
            a_all = dta.rearrange("p c h -> p (c h)")
            mm(bank[4][:, 0:64], tri, a_all, start=True, stop=True)
            mm(bank[4][:, 64:128], ones, a_all, start=True, stop=True).then_inc(S["acs_mm"], 1)

            def seg(n):
                c, g = groups[n]
                if n >= 2:
                    pe.wait_ge(S["seg_cap"], 4 * (n - 1))
                    pe.wait_ge(S["seg_done"], n - 1)
                for e in range(SE):
                    h = g * SE + e
                    mm(bank[n % 2][:, e * P:(e + 1) * P], dta[:, c, h:h + 1].to_broadcast([P, P]), tri, start=True, stop=True)
                if n >= 2 and n - 2 < (TB - 1) * SG:
                    pe.wait_ge(S["st_new"], n - 1)
                mm(bank[2 + n % 2][:, 0:P], bcT[:, g, c * P:(c + 1) * P], bcT[:, 4 + g, c * P:(c + 1) * P],
                   start=True, stop=True).then_inc(S["seg_mm"], 1)

            def y_and_state(n):
                c, g = groups[n]
                yb, stb = bank[4 + n % 2], bank[2 + n % 2][:, P:P + 256]
                pe.wait_ge(S["seg_done"], n + 1)
                pe.wait_ge(S["xdt_done"], c + 1)
                if n >= 2:
                    pe.wait_ge(S["y_read"], n - 1)
                for e in range(SE):
                    h = g * SE + e
                    last = mm(yb[:, e * SP:(e + 1) * SP], segm[n % 2][:, e, :], xdt[c % 2][:, h * SP:(h + 1) * SP],
                              start=True, stop=True)
                if c > 0:
                    pe.wait_ge(S["st_new"], n - SG + 1)
                    last = mm(yb[:, 256:512], bcT[:, 4 + g, c * P:(c + 1) * P], hst[:, g, :], start=True, stop=True)
                last.then_inc(S["y_mm"], 1)
                if c < TB - 1:
                    pe.wait_ge(S["xdd_done"], c + 1)
                    if n >= 2:
                        pe.wait_ge(S["st_new"], n - 1)
                    mm(stb, btok[:, c, g, :], xdd[:, g * 256:(g + 1) * 256], start=True, stop=True).then_inc(S["st_mm"], 1)

            pe.wait_ge(S["bt_copied"], TB)
            pe.wait_ge(S["xt_copied"], 2 * TB)
            pe.wait_ge(S["acs_neg"], 1)
            pe.wait_ge(S["oT_copied"], TB)

            def early_gates(first, last):
                for m in range(first, min(last, 3 * EARLY * KT)):
                    i, k = divmod(m, KT)
                    if k == 0:
                        t = CM_PROJ + i
                        pe.wait_ge(ld_ring[t % SLOTS], 16 * (t // SLOTS + 1))
                        if i >= 2:
                            pe.wait_ge(S["early_out"], i - 1)
                    last_mm = mm(bank[6 + i % 2][:, :], ring[:, (CM_PROJ + i) % SLOTS, k, :], hT[:, k, :], start=(k == 0), stop=(k == KT - 1))
                    if k == KT - 1:
                        last_mm.then_inc(S["proj_done"], 1)

            seg(0)
            for n in range(16):
                if n + 1 < 16:
                    seg(n + 1)
                early_gates(5 * n, 5 * n + 5)
                y_and_state(n)
            for c in range(TB):
                pe.wait_ge(S["y_norm"], c + 1)
                for half in range(2):
                    n = 2 * c + half
                    if n >= 2:
                        pe.wait_ge(S["yT_done"], n - 1)
                    else:
                        pe.wait_ge(S["early_out"], 3 * EARLY)
                    for i in range(4):
                        k = half * 4 + i
                        last = tr(bank[6 + n % 2][:, i * P:(i + 1) * P], ytok[:, c, k * P:(k + 1) * P], ident)
                    last.then_inc(S["y_turned"], 1)

            loads = [len([i for i in range(CM_EARLY) if i % SLOTS == s]) for s in range(SLOTS)]

            def branch(j, first, gates):
                if gates:
                    for s in range(3):
                        pe.wait_ge(ld_ring[s], (j + (loads[s] + 1 - EARLY)) * 16)
                        pe.wait_ge(S["gate_sig"], j * 3)
                        for k in range(KT):
                            last = mm(bank[s][:, :], ring[:, s, k, :], hT[:, k, :], start=(k == 0), stop=(k == KT - 1))
                        last.then_inc(S["gate_mm"], 1)
                pe.wait_ge(ld_ring[3], (j + (loads[3] + 1)) * 16)
                if not first:
                    pe.wait_ge(S["br_used"], j * 3)
                for k in range(4):
                    last = mm(bank[3][:, :], ring[:, 3, k, :], poolT[:, k, :], start=(k == 0), stop=(k == 3))
                last.then_inc(S["br_mm"], 1)
                for k in range(4):
                    last = mm(bank[4][:, :], ring[:, 3, 4 + k, :], oT[:, k, :], start=(k == 0), stop=(k == 3))
                last.then_inc(S["br_mm"], 1)
                pe.wait_ge(ld_ring[4], (j + (loads[4] + 1)) * 16)
                for k in range(KT):
                    last = mm(bank[5][:, :], ring[:, 4, k, :], yT[:, k, :], start=(k == 0), stop=(k == KT - 1))
                last.then_inc(S["br_mm"], 1)

            pe.wait_ge(S["yT_done"], 2 * TB)
            pe.wait_ge(S["y_read"], 16)
            for j in range(EARLY):
                branch(j, j == 0, False)
            with pe.Fori(EARLY, KT) as j:
                branch(j, False, True)

            pe.wait_ge(S["ld_wo"], 32)
            pe.wait_ge(S["mT_done"], KT)
            for b in range(TB):
                if b >= 2:
                    pe.wait_ge(S["mix_read"], b - 1)
                for half in range(2):
                    acc = bank[(6, 0)[b % 2] + half]
                    for k in range(KT):
                        last = mm(acc[:, :], mT[:, k, b * P:(b + 1) * P], wo[:, half, k, :], start=(k == 0), stop=(k == KT - 1))
                        if k < 4:
                            mm(acc[:, k * P:(k + 1) * P], hT[:, half * 4 + k, b * P:(b + 1) * P], aident, start=False, stop=False)
                last.then_inc(S["mix_mm"], 1)
            pe.wait_ge(S["ln_norm"], 2 * TB)
            for k in range(KT):
                for b in range(TB):
                    last = tr(bank[k][:, b * P:(b + 1) * P], n1[:, b, k * P:(k + 1) * P], ident)
                last.then_inc(S["ln_turned"], 1)

            pe.wait_ge(S["hT_act"], KT)
            pe.wait_ge(S["hT_dve"], KT)
            pe.wait_ge(S["ld_rt"], 16)
            for b in range(TB):
                for k in range(KT):
                    last = mm(bank[0][:, b * NE:(b + 1) * NE], h1T[:, k, b * P:(b + 1) * P], wrt[:, k, :], start=(k == 0), stop=(k == KT - 1))
            last.then_inc(S["rt_mm"], 1)
            pe.wait_ge(S["sel_done"], 1)
            for b in range(TB):
                for c in range(b + 1):
                    mm(bank[1][:, b * NE:(b + 1) * NE], tri if c == b else ones, sel[:, c, :], start=(c == 0), stop=(c == b))
            for c in range(TB):
                last = mm(bank[1][:, 64:64 + NE], ones, sel[:, c, :], start=(c == 0), stop=(c == TB - 1))
            last.then_inc(S["pos_mm"], 1)

            def turn_tokens(k, buf, load, first=False):
                pe.wait_ge(ld_xg[buf], load * 16)
                if not first:
                    pe.wait_ge(S["xT_act"], k)
                    pe.wait_ge(S["xT_dve"], k)
                for c in range(KT):
                    last = tr(bank[2 + c // 4][:, (c % 4) * P:(c % 4 + 1) * P], xg[buf][:, c * P:(c + 1) * P], ident)
                    if c % 4 == 3:
                        last.then_inc(S["x_turned"], 1)

            def up_products(k, slot, load, first=False):
                pe.wait_ge(S["xT_act"], k + 1)
                pe.wait_ge(S["xT_dve"], k + 1)
                pe.wait_ge(ld_w13[slot], load * 16)
                if not first:
                    pe.wait_ge(S["hid_done"], k)
                for m in range(2):
                    for c in range(KT):
                        last = mm(bank[m][:, :], xgT[:, c, :], ew13[slot][:, m, c, :], start=(c == 0), stop=(c == KT - 1))
                    last.then_inc(S["up_mm"], 1)

            def turn_hidden(k, first=False):
                pe.wait_ge(S["hid_done"], k + 1)
                if not first:
                    pe.wait_ge(S["hidT_done"], k)
                for f in range(FT):
                    last = tr(bank[4][:, f * P:(f + 1) * P], hidv[:, f * P:(f + 1) * P], ident)
                last.then_inc(S["h_turned"], 1)

            def down_products(k, slot, load, first=False):
                pe.wait_ge(S["hidT_done"], k + 1)
                pe.wait_ge(ld_w2[slot], load * 16)
                if not first:
                    pe.wait_ge(S["out_act"], k)
                    pe.wait_ge(S["out_dve"], k)
                for half in range(2):
                    for f in range(FT):
                        last = mm(bank[5 + half][:, :], hidT[:, f, :], ew2[slot][:, f, half * 512:(half + 1) * 512],
                                  start=(f == 0), stop=(f == FT - 1))
                    last.then_inc(S["dn_mm"], 1)

            def step(e, slot, load, load_next, load_prev, first=False, second=False, last=False):
                if not first:
                    turn_hidden(e - 1, first=second)
                up_products(e, slot, load, first=first)
                if not last:
                    turn_tokens(e + 1, (slot + 1) % 3, load_next)
                if not first:
                    down_products(e - 1, (slot + 2) % 3, load_prev, first=second)

            turn_tokens(0, 0, 1, first=True)
            step(0, 0, 1, 1, 0, first=True)
            step(1, 1, 1, 1, 1, second=True)
            step(2, 2, 1, 2, 1)
            step(3, 0, 2, 2, 1)
            with pe.Fori(1, (NE - 1) // 3 - 1) as i:
                step(i * 3 + 1, 1, i + 1, i + 1, i + 1)
                step(i * 3 + 2, 2, i + 1, i + 2, i + 1)
                step(i * 3 + 3, 0, i + 2, i + 2, i + 1)
            n = (NE - 1) // 3 - 1
            step(n * 3 + 1, 1, n + 1, n + 1, n + 1)
            step(n * 3 + 2, 2, n + 1, n + 2, n + 1)
            step(n * 3 + 3, 0, n + 2, n + 2, n + 1, last=True)
            turn_hidden(NE - 1)
            down_products(NE - 1, 0, n + 2)
            n_spare = pe.value_load(spare_info[0:1, SPARE:SPARE + 1], min_val=0, max_val=SPARE)
            with pe.Fori(0, SPARE) as i:
                with pe.If(i < n_spare):
                    turn_tokens(i + NE, 0, i + n + 3)
                    up_products(i + NE, 0, i + n + 3)
                    turn_hidden(i + NE)
                    down_products(i + NE, 0, i + n + 3)

        @block.scalar
        def _(act):
            ac = nc.scalar.activation
            act.wait_ge(S["ln_stat"], 1)
            ac(sdev, mv[:, :, 1], ACT.Sqrt).then_inc(S["ln_sd"], 1)

            def turned_to(dst, base, g0, b0):
                for k in range(0, KT, 2):
                    act.wait_ge(S["ln_turned"], base + k + 1)
                    ac(dst[:, k, :], bank[k][:, :], ACT.Identity, scale=colv[:, g0 + k:g0 + k + 1],
                       bias=colv[:, b0 + k:b0 + k + 1]).then_inc(S["hT_act"], 1)

            act.wait_ge(S["ld_const"], 16 * NCONST)
            turned_to(hT, 0, C_LN0G, C_LN0B)
            for i in (2, 3):
                act.wait_ge(S["proj_done"], i + 1)
                ac(kT[i - 2], bank[i % 2][:, :], ACT.Copy).then_inc(S["act_freed"], 1)
            for i in range(4, 8):
                act.wait_ge(S["proj_done"], i + 1)
                ac(qT[:, i - 4, :], bank[i % 2][:, :], ACT.Copy, scale=DH ** -0.5).then_inc(S["act_freed"], 1)
            for kv in range(2):
                act.wait_ge(S["cmp_mm"], kv + 1)
                ac(hidc[:, kv], bank[2 + kv][:, 0:KVG * NCMP].rearrange("p (g n) -> p g n", g=KVG),
                   ACT.Gelu_apprx_tanh).then_inc(S["cmp_hid"], 1)
            act.wait_ge(S["cmp2_mm"], 1)
            ac(kcT[:, :], bank[4][:, 0:NCMP], ACT.Copy).then_inc(S["cmp_kc"], 1)
            for g in range(4):
                i = 8 + g
                act.wait_ge(S["proj_done"], i + 1)
                if g >= 1:
                    act.wait_ge(S["pool_out"], g)
                else:
                    act.wait_ge(S["zeroed"], 3)
                ac(praw[:, 16:], bank[i % 2][:, :], ACT.Copy).then_inc(S["act_freed"], 1)

            def conv_out(i):
                act.wait_ge(S["conv_sum"], 3 * (i + 1))
                dst = xsT[:, i, :] if i < 8 else bcT[:, i - 8, :]
                ac(dst, dst, ACT.Silu).then_inc(S["conv_done"], 1)

            act.wait_ge(S["soft_abs"], 1)
            ac(dte, dtm, ACT.Exp, scale=-1.0).then_inc(S["ac"], 1)
            act.wait_ge(S["ac"], 1)
            ac(dte, dte, ACT.Ln, bias=1.0).then_inc(S["soft_ln"], 1)
            ac(expa, rowv[:, R_ALOG:R_ALOG + SH], ACT.Exp).then_inc(S["soft_ln"], 1)
            ac(ngate, ngate, ACT.Exp, scale=-1.0).then_inc(S["gates_e"], 1)

            for i in range(16):
                dst = xsT[:, i, :] if i < 8 else bcT[:, i - 8, :]
                qb, part = divmod(12 + i - CMP_AT, 3)
                if 0 <= qb < TB and part == 1:
                    act.wait_ge(S["cs_sub"], qb + 1)
                    v = pcs[:, qb, :, 0:nvalid[qb]]
                    ac(v, v, ACT.Exp).then_inc(S["cs_exp"], 1)
                if i == 0:
                    act.wait_ge(S["vd_mm"], TB)
                if i == 8:
                    act.wait_ge(S["cmp_mm"], 2)
                act.wait_ge(S["proj_done"], 12 + i + 1)
                ac(dst, bank[i % 2][:, :], ACT.Identity, scale=colv[:, C_CW + 48 + i:C_CW + 49 + i],
                   bias=colv[:, C_CB + i:C_CB + i + 1]).then_inc(S["conv_first"], 1)
                if i >= 1:
                    conv_out(i - 1)
            conv_out(15)
            for u, (br, qb, h) in enumerate(units):
                n = (qb + 1) * P
                act.wait_ge(S["sc_max"], u + 1)
                if u >= 3:
                    act.wait_ge(S["p_turned"], u - 2)
                ac(att_p[u % 3][:, 0:n], att_s[u % 3][:, 0:n], ACT.Exp, scale=-1.0, bias=nmax[:, br, qb, h:h + 1],
                   accum_out=psums[:, br, qb, h:h + 1]).then_inc(S["p_done"], 1)
                if u % KT == KT - 1:
                    half, b = divmod(u // KT, TB)
                    act.wait_ge(S["z_mm"], u // KT + 1)
                    ac(zs[:, b, half * 512:(half + 1) * 512], bank[7][:, :], ACT.Silu).then_inc(S["z_silu"], 1)
            act.wait_ge(S["zeroed_x"], 16 * (NE + SPARE))
            act.wait_ge(S["zeroed_y"], 16 * SPARE)
            for qb in range(TB):
                act.wait_ge(S["o_turned"], qb + 1)
                ac(oT[:, :, qb * P:(qb + 1) * P], bank[7][:, :].rearrange("p (a b) -> p a b", a=4), ACT.Copy).then_inc(S["oT_copied"], 1)
            for n in range(2 * TB):
                c, half = divmod(n, 2)
                act.wait_ge(S["xt_turned"], n + 1)
                ac(ytok[:, c, half * 512:(half + 1) * 512], bank[2 + n % 2][:, :], ACT.Copy).then_inc(S["xt_copied"], 1)
            act.wait_ge(S["acs_neg"], 3)
            for dst, src in ((eacs, acs), (decin, decin), (cdec, cdec)):
                ac(dst, src, ACT.Exp).then_inc(S["acs_exp"], 1)
            early_read = 0
            for n in range(16):
                act.wait_ge(S["seg_cap"], 4 * (n + 1))
                ac(segd[n % 2], segd[n % 2], ACT.Exp).then_inc(S["seg_exp"], 1)
                while early_read < 3 * EARLY and KT * (early_read + 1) <= 5 * n:
                    act.wait_ge(S["proj_done"], CM_PROJ + early_read + 1)
                    ac(early[early_read], bank[6 + early_read % 2][:, :], ACT.Copy).then_inc(S["early_out"], 1)
                    early_read += 1
            for c in range(TB):
                act.wait_ge(S["y_gated"], c + 1)
                for g in range(SG):
                    ac(r_qkv[:, 0:256], ytok[:, c, g * 256:(g + 1) * 256], ACT.Square, accum_out=yss[:, c, g:g + 1]).then_inc(S["y_sq"], 1)
                    act.wait_ge(S["y_sq"], c * SG + g + 1)
            act.wait_ge(S["y_ms"], 1)
            ac(yrt, yrt, ACT.Sqrt).then_inc(S["y_sd"], 1)
            for n in range(2 * TB):
                c, half = divmod(n, 2)
                act.wait_ge(S["y_turned"], n + 1)
                for i in range(4):
                    k = half * 4 + i
                    last = ac(yT[:, k, c * P:(c + 1) * P], bank[6 + n % 2][:, i * P:(i + 1) * P], ACT.Copy, scale=colv[:, C_NG + k:C_NG + k + 1])
                last.then_inc(S["yT_done"], 1)

            act.wait_ge(S["early_out"], 3 * EARLY)
            for j in range(EARLY):
                for s in range(3):
                    if j > 0:
                        act.wait_ge(S["br_used"], j * 3)
                    else:
                        act.wait_ge(S["y_norm"], TB)
                    ac(gsb[s], early[j * 3 + s], ACT.Sigmoid).then_inc(S["gate_sig"], 1)
            with act.Fori(EARLY, KT) as j:
                for s in range(3):
                    act.wait_ge(S["gate_mm"], j * 3 + (s + 1 - 3 * EARLY))
                    act.wait_ge(S["br_used"], j * 3)
                    ac(gsb[s], bank[s][:, :], ACT.Sigmoid).then_inc(S["gate_sig"], 1)
            act.wait_ge(S["mT_done"], KT)
            for b in range(TB):
                act.wait_ge(S["mix_mm"], b + 1)
                for half in range(2):
                    last = ac(n1[:, b, half * 512:(half + 1) * 512], bank[(6, 0)[b % 2] + half][:, :], ACT.Copy)
                last.then_inc(S["mix_read"], 1)
            act.wait_ge(S["ln_stat"], 2)
            ac(sdev, mv[:, :, 1], ACT.Sqrt).then_inc(S["ln_sd"], 1)
            turned_to(h1T, KT, C_LN1G, C_LN1B)
            act.wait_ge(S["rt_max"], 1)
            ac(lg, lg, ACT.Exp).then_inc(S["rt_exp"], 1)

            def tokens_out(k, first=False):
                act.wait_ge(S["x_turned"], k * 2 + 1)
                if not first:
                    act.wait_ge(S["up_mm"], k * 2)
                ac(xgT[:, 0:4, :].rearrange("p k t -> p (k t)"), bank[2][:, :], ACT.Copy).then_inc(S["xT_act"], 1)

            def silu(k, first=False):
                act.wait_ge(S["up_mm"], k * 2 + 1)
                if not first:
                    act.wait_ge(S["hid_done"], k)
                ac(upv, bank[0][:, :], ACT.Silu).then_inc(S["up_silu"], 1)

            def out_half(k, first=False):
                act.wait_ge(S["dn_mm"], k * 2 + 1)
                if not first:
                    act.wait_ge(S["st_y"], k * 16)
                ac(eout[:, 0:512], bank[5][:, :], ACT.Copy).then_inc(S["out_act"], 1)

            def step(e):
                silu(e)
                tokens_out(e + 1)
                out_half(e - 1)

            tokens_out(0, first=True)
            silu(0, first=True)
            tokens_out(1)
            silu(1)
            tokens_out(2)
            out_half(0, first=True)
            with act.Fori(2, NE - 1) as e:
                step(e)
            silu(NE - 1)
            out_half(NE - 2)
            out_half(NE - 1)
            n_spare = act.value_load(spare_info[0:1, SPARE:SPARE + 1], min_val=0, max_val=SPARE)
            with act.Fori(0, SPARE) as i:
                with act.If(i < n_spare):
                    tokens_out(i + NE)
                    silu(i + NE)
                    out_half(i + NE)
            act.wait_ge(S["ln_stat"], 3)
            ac(sdev, mv[:, :, 1], ACT.Sqrt).then_inc(S["ln_sd"], 1)

        @block.gpsimd
        def _(gp):
            g_ = nc.gpsimd
            g_.memset(praw[:, 0:16], 0.0).then_inc(S["zeroed"], 1)
            g_.memset(pw[0][:, 0:16], 0.0).then_inc(S["zeroed"], 1)
            g_.memset(pw[1][:, 0:16], 0.0).then_inc(S["zeroed"], 1)
            g_.memset(vbd[:, :, :, :], 0.0).then_inc(S["zeroed"], 1)
            g_.memset(zeros, 0.0).then_inc(S["zero_tile"], 1)
            g_.memset(pcs, 0.0).then_inc(S["zeroed"], 1)
            step = 0
            gp.wait_ge(S["zeroed"], 3)
            gp.wait_ge(S["ld_const"], 16 * NCONST)
            for g, w in enumerate(WINDOWS):
                gp.wait_ge(S["act_freed"], 6 + g + 1)
                src, span, flip = praw, 1, 0
                while span < w:
                    dst = pw[flip]
                    g_.tensor_tensor(dst[:, 16:], src[:, 16:], src[:, 16 - span:16 - span + T], ALU.add).then_inc(S["gp"], 1)
                    step += 1
                    gp.wait_ge(S["gp"], step)
                    src, span, flip = dst, span * 2, 1 - flip
                g_.tensor_scalar(pr[:, 16:], src[:, 32:], 1.0 / w, None, ALU.mult).then_inc(S["gp"], 1)
                g_.tensor_tensor(pr[:, 0:16], src[:, 16:32], invc[:, g, :], ALU.mult).then_inc(S["gp"], 1)
                step += 2
                gp.wait_ge(S["gp"], step)
                g_.tensor_tensor(poolT[:, g, :], pr, praw[:, 16:], ALU.subtract).then_inc(S["pool_out"], 1)
                gp.wait_ge(S["pool_out"], g + 1)
            for c in range(TB):
                gp.wait_ge(S["xdt_done"], c + 1)
                if c < TB - 1:
                    if c >= 1:
                        gp.wait_ge(S["st_mm"], SG * c)
                    g_.tensor_tensor(xdd.rearrange("p (h d) -> p h d", h=SH), xdt[c % 2].rearrange("p (h d) -> p h d", h=SH),
                                     decin[:, c, :].unsqueeze(2).broadcast_to([P, SH, SP]), ALU.mult).then_inc(S["xdd_done"], 1)
                if c >= 1:
                    gp.wait_ge(S["y_gated"], c)
                g_.tensor_tensor(xsd.rearrange("p (h d) -> p h d", h=SH), ytok[:, c, :].rearrange("p (h d) -> p h d", h=SH),
                                 rowv[:, R_DSK:R_DSK + SH].unsqueeze(2).broadcast_to([P, SH, SP]), ALU.mult).then_inc(S["xsd_done"], 1)

            gp.wait_ge(S["ld_ln1"], 32)
            gp.wait_ge(S["ln_turned"], 2 * KT)
            for b in (2, 3):
                g_.tensor_tensor(n1[:, b, :], n1[:, b, :], lnr[:, 0, :], ALU.mult).then_inc(S["tok_gp"], 1)
                gp.wait_ge(S["tok_gp"], (b - 2) * 2 + 1)
                g_.tensor_tensor(n1[:, b, :], n1[:, b, :], lnr[:, 1, :], ALU.add).then_inc(S["tok_gp"], 1)
            gp.wait_ge(S["tok_gp"], 4)
            gp.wait_ge(S["tok_dve"], 2)
            gp.wait_ge(S["slots_done"], 1)
            gp.wait_ge(S["zeroed_x"], 16 * (NE + SPARE))
            for b in range(TB):
                for k in range(2):
                    g_.indirect_dma_start(xs_dram, bass.IndirectOffsetOnAxis(ap=slot_no[:, b, k:k + 1], axis=0),
                                          n1[:, b, :], None).then_inc(S["st_h"], 16)

            def store(k):
                gp.wait_ge(S["out_act"], k + 1)
                gp.wait_ge(S["out_dve"], k + 1)
                g_.dma_start(ys_dram[bass.ds(k * P, P), :], eout).then_inc(S["st_y"], 16)
                gp.wait_ge(S["st_y"], k * 16 + 16)

            with gp.Fori(0, NE) as k:
                store(k)
            n_spare = gp.value_load(spare_info[0:1, SPARE:SPARE + 1], min_val=0, max_val=SPARE)
            with gp.Fori(0, SPARE) as i:
                with gp.If(i < n_spare):
                    store(i + NE)
            gp.wait_ge(S["zeroed_y"], 16 * SPARE)
            gp.sem_inc(S["back_a"], 1)
            for b in range(TB):
                for k in range(2):
                    g_.indirect_dma_start(by_token[:, b, k, :], None, ys_dram,
                                          bass.IndirectOffsetOnAxis(ap=slot_no[:, b, k:k + 1], axis=0)).then_inc(ld_back[b], 16)

        @block.vector
        def _(dve):
            v = nc.vector
            chain = [0]

            def then(ins):
                chain[0] += 1
                ins.then_inc(S["dv"], 1)
                dve.wait_ge(S["dv"], chain[0])

            def stats_of(b, halves):
                for i, half in enumerate(halves):
                    last = v.bn_stats(stats[:, b, i, :], half)
                then(last)
                return v.bn_aggr(mv[:, b, :], stats[:, b].rearrange("p a s -> p (a s)"))

            def add_eps():
                then(v.tensor_scalar(rstd, mv[:, :, 1], LN_EPS, None, ALU.add))
                v.tensor_copy(mv[:, :, 1], rstd).then_inc(S["ln_stat"], 1)

            for b in range(TB):
                dve.wait_ge(ld_x[b], 16)
                then(stats_of(b, [xin[:, b, 0:512], xin[:, b, 512:1024]]))
            add_eps()
            dve.wait_ge(S["ln_sd"], 1)
            then(v.reciprocal(rstd, sdev))
            for b in range(TB):
                v.tensor_scalar(xnorm[:, b, :], xin[:, b, :], mv[:, b, 0:1], rstd[:, b:b + 1], ALU.subtract, ALU.mult).then_inc(S["ln_norm"], 1)

            def turned_to(dst, base, g0, b0):
                for k in range(1, KT, 2):
                    dve.wait_ge(S["ln_turned"], base + k + 1)
                    v.tensor_scalar(dst[:, k, :], bank[k][:, :], colv[:, g0 + k:g0 + k + 1], colv[:, b0 + k:b0 + k + 1],
                                    ALU.mult, ALU.add).then_inc(S["hT_dve"], 1)

            dve.wait_ge(S["ld_const"], 16 * NCONST)
            turned_to(hT, 0, C_LN0G, C_LN0B)
            for kv in range(2):
                dve.wait_ge(S["proj_done"], kv + 1)
                for g in range(KVG):
                    rows_g = bank[kv][g * DH:(g + 1) * DH, :]
                    v.tensor_copy(tok2[0:DH, kv, g, :], rows_g)
                    last = v.tensor_copy(tok2[DH:P, kv, g, 0:T - 1], rows_g[:, 1:T])
                last.then_inc(S["dve_freed"], 1)
                dve.wait_ge(S["dve_freed"], kv + 1)
                rows16 = tok2[:, kv].rearrange("p g (n m) -> p g n m", m=CMP_STRIDE)
                for half in range(2):
                    c = (C_PEK, C_PEV)[kv] + half * 8
                    v.tensor_tensor(blocks[:, kv, half * 8:half * 8 + 8].rearrange("p l g n -> p g n l"),
                                    rows16[:, :, half:half + NCMP, 0:CMP_STRIDE:2],
                                    colv[:, c:c + 8].unsqueeze(1).unsqueeze(1).broadcast_to([P, KVG, NCMP, 8]),
                                    ALU.add).then_inc(S["cmp_in"], 1)
            for i in range(2):
                dve.wait_ge(S["bias_mm"], i + 1)
                v.tensor_copy(bias_sb[:, i * REVN // 2:(i + 1) * REVN // 2], bank[6 + i][0:HEADS, 0:REVN // 2]).then_inc(S["bias_rows"], 1)
            dve.wait_ge(S["cmp2_mm"], 1)
            dve.wait_ge(S["zeroed"], 4)
            for h in range(HPG):
                rows_h = slice(32 * h, 32 * h + NCMP)
                v.tensor_copy(vbd[rows_h, :, h, :], bank[5][rows_h, 0:KVG * DH].rearrange("p (g d) -> p g d", g=KVG)).then_inc(S["cmp_vc"], 1)
            for b in range(TB):
                dve.wait_ge(S["vd_mm"], b + 1)
                v.tensor_copy(vtok[:, b].rearrange("p r g d -> p (r g d)"), bank[2 + b][:, 0:2 * P])
                v.tensor_tensor(dtx[:, b, :], bank[2 + b][:, 2 * P:2 * P + SH], rowv[:, R_DTB:R_DTB + SH], ALU.add)
                v.tensor_copy(ngate[:, b].rearrange("p r h -> p (r h)"), bank[2 + b][:, 2 * P + SH:VD]).then_inc(S["vd_used"], 1)
            dve.wait_ge(S["vd_used"], TB)
            v.scalar_tensor_tensor(out=dtm, in0=dtx, scalar=-1.0, in1=dtx, op0=ALU.mult, op1=ALU.max).then_inc(S["soft_abs"], 1)
            dve.wait_ge(S["soft_ln"], 2)
            then(v.scalar_tensor_tensor(out=dt, in0=dtx, scalar=0.0, in1=dte, op0=ALU.max, op1=ALU.add))
            v.scalar_tensor_tensor(out=dta, in0=dt, scalar=-1.0, in1=expa.unsqueeze(1).broadcast_to([P, TB, SH]),
                                   op0=ALU.mult, op1=ALU.mult).then_inc(S["decay_a"], 1)
            dve.wait_ge(S["gates_e"], 1)
            then(v.tensor_scalar(ngate, ngate, 1.0, None, ALU.add))
            then(v.reciprocal(ngate, ngate))

            def cmp_scores(qb):
                nv = nvalid[qb]
                z0 = T - P - qb * P + CMP_LEN - 1
                if qb == 0:
                    dve.wait_ge(S["ld_strip"], 16)
                    dve.wait_ge(S["zeroed"], 5)
                dve.wait_ge(S["cs_mm"], qb + 1)
                s3 = pcs[:, qb, :, 0:nv]
                for g in range(KVG):
                    hs = slice(g * HPG, (g + 1) * HPG)
                    last = v.tensor_tensor(s3[:, hs, :], bank[2 + g][:, 0:256].rearrange("p (h n) -> p h n", h=HEADS)[:, hs, 0:nv],
                                           strips[:, hs, z0:z0 + CMP_STRIDE * (nv - 1) + 1:CMP_STRIDE], ALU.add)
                then(last)
                then(v.tensor_reduce(cmax[:, qb, :], s3, AX.X, ALU.max))
                v.tensor_tensor(s3, s3, cmax[:, qb, :].unsqueeze(2).broadcast_to([P, HEADS, nv]), ALU.subtract).then_inc(S["cs_sub"], 1)

            def cmp_turn(qb):
                dve.wait_ge(S["cs_exp"], qb + 1)
                then(v.tensor_reduce(csum[:, qb, :], pcs[:, qb, :, 0:nvalid[qb]], AX.X, ALU.add))
                then(v.reciprocal(csum[:, qb, :], csum[:, qb, :]))
                gate = ngate[:, qb, 0, :]
                if qb == 0:
                    then(v.tensor_scalar(gate, gate, rowok, None, ALU.mult))
                then(v.tensor_tensor(ogate[:, 0, qb, :], gate, csum[:, qb, :], ALU.mult))
                dve.wait_ge(S["cs_turned"], qb + 1)
                if qb >= 2:
                    dve.wait_ge(S["co_mm"], qb - 1)
                v.tensor_copy(pct[:, qb % 2].rearrange("p g n -> p (g n)"), bank[4][:, 0:256]).then_inc(S["cs_copied"], 1)

            def cmp_values(qb):
                dve.wait_ge(S["co_mm"], qb + 1)
                v.tensor_tensor(oacc[:, qb], bank[5][:, :].rearrange("p (h d) -> p h d", h=HEADS),
                                ogate[:, 0, qb, :].unsqueeze(2).broadcast_to([P, HEADS, DH]), ALU.mult).then_inc(S["co_read"], 1)

            for i in range(16):
                dst = xsT[:, i, :] if i < 8 else bcT[:, i - 8, :]
                dve.wait_ge(S["conv_first"], i + 1)
                for n, back in enumerate((1, 2, 3)):
                    tap = C_CW + (3 - back) * 16 + i
                    if n:
                        dve.wait_ge(S["conv_sum"], 3 * i + n)
                    v.scalar_tensor_tensor(out=dst[:, back:], in0=bank[i % 2][:, 0:T - back], scalar=colv[:, tap:tap + 1],
                                           in1=dst[:, back:], op0=ALU.mult, op1=ALU.add).then_inc(S["conv_sum"], 1)
                qb, part = divmod(12 + i - CMP_AT, 3)
                if 0 <= qb < TB:
                    (cmp_scores, cmp_turn, cmp_values)[part](qb)
            for g in range(4):
                dve.wait_ge(S["pool_mm"], g + 1)
                v.tensor_scalar(poolT[:, g, :], bank[2 + g][:, :], colv[:, C_PS + g:C_PS + g + 1], None, ALU.mult).then_inc(S["pool_scaled"], 1)

            NU = len(units)
            for u in range(NU + 3):
                if u < NU:
                    br, qb, h = units[u]
                    n = (qb + 1) * P
                    dve.wait_ge(S["sc_mm"], u + 1)
                    if u >= 3:
                        dve.wait_ge(S["p_done"], u - 2)
                    v.tensor_tensor_reduce(out=att_s[u % 3][:, 0:n], in0=bank[u % 3][:, 0:n], in1=strips[:, h, T - n:T],
                                           scale=-1.0, scalar=3e38, op0=ALU.add, op1=ALU.min,
                                           accum_out=nmax[:, br, qb, h:h + 1]).then_inc(S["sc_max"], 1)
                if 2 <= u < NU + 2:
                    w = u - 2
                    nb = units[w][1] + 1
                    dve.wait_ge(S["p_turned"], w + 1)
                    if w >= 3:
                        dve.wait_ge(S["o_mm"], w - 2)
                    v.tensor_copy(att_pt[w % 3][:, 0:nb, :].rearrange("p a b -> p (a b)"), bank[3 + w % 2][:, 0:nb * P]).then_inc(S["pt_copied"], 1)
                if u >= 3 and units[u - 3][2] == HEADS - 1:
                    br, qb, _h = units[u - 3]
                    n = br * TB + qb
                    dve.wait_ge(S["p_done"], u - 2)
                    then(v.reciprocal(psums[:, br, qb, :], psums[:, br, qb, :]))
                    then(v.tensor_tensor(ogate[:, 1 + br, qb, :], psums[:, br, qb, :], ngate[:, qb, 1 + br, :], ALU.mult))
                    dve.wait_ge(S["o_mm"], u - 2)
                    v.tensor_tensor(osc, bank[5 + n % 2][:, :].rearrange("p (h d) -> p h d", h=HEADS),
                                    ogate[:, 1 + br, qb, :].unsqueeze(2).broadcast_to([P, HEADS, DH]), ALU.mult).then_inc(S["o_read"], 1)
                    dve.wait_ge(S["o_read"], n + 1)
                    v.tensor_tensor(oacc[:, qb], oacc[:, qb], osc, ALU.add).then_inc(S["o_acc"], 1)

            for c in range(TB):
                dve.wait_ge(S["bt_turned"], c + 1)
                v.tensor_copy(btok[:, c].rearrange("p g n -> p (g n)"), bank[c % 2][:, :]).then_inc(S["bt_copied"], 1)
            dve.wait_ge(S["acs_mm"], 1)
            flat = lambda a: a.rearrange("p c h -> p (c h)")
            then(v.tensor_copy(flat(acs), bank[4][:, 0:64]))
            v.tensor_scalar(negacs, acs, -1.0, None, ALU.mult).then_inc(S["acs_neg"], 1)
            v.tensor_tensor(flat(decin), bank[4][:, 64:128], flat(acs), ALU.subtract).then_inc(S["acs_neg"], 1)
            v.tensor_copy(flat(cdec), bank[4][:, 64:128]).then_inc(S["acs_neg"], 1)

            def caps(n):
                c, g = groups[n]
                dve.wait_ge(S["seg_mm"], n + 1)
                for e in range(SE):
                    v.scalar_tensor_tensor(out=segd[n % 2][:, e, :], in0=bank[n % 2][:, e * P:(e + 1) * P],
                                           scalar=negacs[:, c, g * SE + e:g * SE + e + 1], in1=cap,
                                           op0=ALU.add, op1=ALU.min).then_inc(S["seg_cap"], 1)

            def weigh(n):
                dve.wait_ge(S["seg_exp"], n + 1)
                if n >= 2:
                    dve.wait_ge(S["y_mm"], n - 1)
                v.tensor_tensor(segm[n % 2], segd[n % 2], bank[2 + n % 2][:, 0:P].unsqueeze(1).broadcast_to([P, SE, P]),
                                ALU.mult).then_inc(S["seg_done"], 1)

            def heads_of(a, g):
                return a[:, g * SE:(g + 1) * SE].unsqueeze(2).broadcast_to([P, SE, SP])

            dve.wait_ge(S["o_turned"], TB)
            dve.wait_ge(S["acs_exp"], 3)
            dve.wait_ge(S["acs_neg"], 3)
            dve.wait_ge(S["z_silu"], 2 * TB)
            caps(0)
            weigh(0)
            for n, (c, g) in enumerate(groups):
                if g == 0:
                    dve.wait_ge(S["xt_copied"], 2 * (c + 1))
                    if c >= 2:
                        dve.wait_ge(S["xdd_done"], c - 1)
                    v.tensor_tensor(xdt[c % 2].rearrange("p (h d) -> p h d", h=SH), ytok[:, c, :].rearrange("p (h d) -> p h d", h=SH),
                                    dt[:, c, :].unsqueeze(2).broadcast_to([P, SH, SP]), ALU.mult).then_inc(S["xdt_done"], 1)
                if n + 1 < 16:
                    caps(n + 1)
                dve.wait_ge(S["y_mm"], n + 1)
                yb = bank[4 + n % 2]
                h4 = lambda a: a.rearrange("p (h d) -> p h d", h=SE)
                dve.wait_ge(S["xsd_done"], c + 1)
                dst = h4(ytok[:, c, g * 256:(g + 1) * 256])
                x4 = h4(xsd[:, g * 256:(g + 1) * 256])
                if c > 0:
                    then(v.tensor_tensor(yoff, h4(yb[:, 256:512]), heads_of(eacs[:, c, :], g), ALU.mult))
                    then(v.tensor_tensor(yoff, yoff, x4, ALU.add))
                    v.tensor_tensor(dst, h4(yb[:, 0:256]), yoff, ALU.add).then_inc(S["y_read"], 1)
                else:
                    v.tensor_tensor(dst, h4(yb[:, 0:256]), x4, ALU.add).then_inc(S["y_read"], 1)
                if c < TB - 1:
                    stb = bank[2 + n % 2][:, P:P + 256]
                    hg = h4(hst[:, g, :])
                    dve.wait_ge(S["st_mm"], n + 1)
                    if c == 0:
                        v.tensor_copy(hst[:, g, :], stb).then_inc(S["st_new"], 1)
                    else:
                        then(v.tensor_tensor(hg, hg, heads_of(cdec[:, c, :], g), ALU.mult))
                        v.tensor_tensor(hg, h4(stb), hg, ALU.add).then_inc(S["st_new"], 1)
                if n + 1 < 16:
                    weigh(n + 1)
                if g == SG - 1:
                    dve.wait_ge(S["y_read"], n + 1)
                    v.tensor_tensor(ytok[:, c, :], ytok[:, c, :], zs[:, c, :], ALU.mult).then_inc(S["y_gated"], 1)
            dve.wait_ge(S["y_sq"], 16)
            v.tensor_scalar(yrt, yss, 1.0 / 256, LN_EPS, ALU.mult, ALU.add).then_inc(S["y_ms"], 1)
            dve.wait_ge(S["y_sd"], 1)
            then(v.reciprocal(yrs, yrt))
            for c in range(TB):
                y4 = ytok[:, c, :].rearrange("p (g d) -> p g d", g=SG)
                v.tensor_tensor(y4, y4, yrs[:, c, :].unsqueeze(2).broadcast_to([P, SG, 256]), ALU.mult).then_inc(S["y_norm"], 1)

            def gated(j, first):
                if not first:
                    dve.wait_ge(S["mT_done"], j)
                for s in range(3):
                    dve.wait_ge(S["gate_sig"], j * 3 + (s + 1))
                    dve.wait_ge(S["br_mm"], j * 3 + (s + 1))
                    v.tensor_tensor(gm[s], gsb[s], bank[3 + s][:, :], ALU.mult).then_inc(S["br_used"], 1)
                dve.wait_ge(S["br_used"], j * 3 + 3)
                v.tensor_tensor(gm[0], gm[0], gm[1], ALU.add).then_inc(S["m_add"], 1)
                dve.wait_ge(S["m_add"], j + 1)
                dst = mT[:, 0, :] if first else mT[:, bass.ds(j, 1), :].rearrange("p a t -> p (a t)")
                v.tensor_tensor(dst, gm[0], gm[2], ALU.add).then_inc(S["mT_done"], 1)

            gated(0, True)
            with dve.Fori(1, KT) as j:
                gated(j, False)
            for b in range(TB):
                dve.wait_ge(S["mix_read"], b + 1)
                then(stats_of(b, [n1[:, b, 0:512], n1[:, b, 512:1024]]))
            add_eps()
            dve.wait_ge(S["ln_sd"], 2)
            then(v.reciprocal(rstd, sdev))
            for b in range(TB):
                v.tensor_scalar(n1[:, b, :], n1[:, b, :], mv[:, b, 0:1], rstd[:, b:b + 1], ALU.subtract, ALU.mult).then_inc(S["ln_norm"], 1)
            turned_to(h1T, KT, C_LN1G, C_LN1B)

            dve.wait_ge(S["ld_ln1"], 32)
            dve.wait_ge(S["ln_turned"], 2 * KT)
            for b in (0, 1):
                then(v.tensor_tensor(n1[:, b, :], n1[:, b, :], lnr[:, 0, :], ALU.mult))
                v.tensor_tensor(n1[:, b, :], n1[:, b, :], lnr[:, 1, :], ALU.add).then_inc(S["tok_dve"], 1)

            b16 = lambda a: a.unsqueeze(2).broadcast_to([P, TB, NE])
            dve.wait_ge(S["rt_mm"], 1)
            lg_in = bank[0][:, 0:TB * NE].rearrange("p (b e) -> p b e", b=TB)
            then(v.tensor_reduce(lmax, lg_in, AX.X, ALU.max))
            v.tensor_tensor(lg, lg_in, b16(lmax), ALU.subtract).then_inc(S["rt_max"], 1)
            dve.wait_ge(S["rt_exp"], 1)
            then(v.tensor_reduce(lsum, lg, AX.X, ALU.add))
            then(v.reciprocal(lsum, lsum))
            then(v.tensor_tensor(prob, lg, b16(lsum), ALU.mult))
            then(v.tensor_tensor(score, prob, rowv[:, R_RB:R_RB + NE].unsqueeze(1).broadcast_to([P, TB, NE]), ALU.add))

            def ranks(dst, vals, n):
                other = vals.unsqueeze(2).broadcast_to([P, n, 4, 4])
                own = vals.unsqueeze(3).broadcast_to([P, n, 4, 4])
                low = lower.unsqueeze(1).broadcast_to([P, n, 4, 4])
                a, b = gt[:, 0:n], ge[:, 0:n]
                then(v.tensor_tensor(a, other, own, ALU.is_gt))
                then(v.tensor_tensor(b, other, own, ALU.is_equal))
                then(v.tensor_tensor(b, b, low, ALU.mult))
                then(v.tensor_tensor(a, a, b, ALU.add))
                then(v.tensor_reduce(dst, a, AX.X, ALU.add))

            by4 = lambda a: a.rearrange("p b (g i) -> p (b g) i", g=4)
            ranks(rank, by4(score), 4 * TB)
            then(v.tensor_scalar(by4(sel), rank, 1.5, None, ALU.is_lt))
            then(v.tensor_tensor(ssel, sel, score, ALU.mult))
            then(v.tensor_reduce(gsc.rearrange("p b g -> p (b g)"), by4(ssel), AX.X, ALU.add))
            ranks(grank, gsc, TB)
            then(v.tensor_scalar(ing, grank, 0.5, None, ALU.is_lt))
            v.tensor_tensor(by4(sel), by4(sel), ing.rearrange("p b g -> p (b g)").unsqueeze(2).broadcast_to([P, 4 * TB, 4]),
                            ALU.mult).then_inc(S["sel_done"], 1)
            dve.wait_ge(S["sel_done"], 1)
            then(v.tensor_tensor(ssel, sel, prob, ALU.mult))
            then(v.tensor_reduce(wden, ssel, AX.X, ALU.add))
            then(v.reciprocal(wden, wden))
            then(v.tensor_tensor(comb, ssel, b16(wden), ALU.mult))
            dve.wait_ge(S["pos_mm"], 1)
            then(v.tensor_copy(cnt, bank[1][:, 64:64 + NE]))
            then(v.tensor_copy(pos.rearrange("p b e -> p (b e)"), bank[1][:, 0:64]))
            then(v.tensor_tensor(thr_gt, cnt.unsqueeze(2).broadcast_to([P, NE, 3]), thr.unsqueeze(1).broadcast_to([P, NE, 3]), ALU.is_gt))
            then(v.tensor_reduce(spn, thr_gt, AX.X, ALU.add))
            then(v.tensor_tensor(big16, spn.unsqueeze(1).broadcast_to([P, NE, NE]), lower16, ALU.mult))
            then(v.tensor_reduce(spx, big16, AX.X, ALU.add))
            be = lambda a: a.unsqueeze(1).broadcast_to([P, TB, NE])
            then(v.tensor_scalar(over, pos, float(P), None, ALU.is_gt))
            then(v.tensor_tensor(cnt, spx, eoff, ALU.add))
            then(v.tensor_tensor(slot1, over, be(cnt), ALU.mult))
            then(v.tensor_tensor(slot1, slot1, be(eid), ALU.add))
            then(v.scalar_tensor_tensor(out=slot1, in0=slot1, scalar=float(P), in1=pos, op0=ALU.mult, op1=ALU.add))
            then(v.tensor_tensor(slot1, slot1, sel, ALU.mult))
            then(v.tensor_reduce(slot_a, slot1, AX.X, ALU.max))
            then(v.tensor_reduce(slot_b, slot1, AX.X, ALU.add))
            then(v.tensor_tensor(slot_b, slot_b, slot_a, ALU.subtract))
            then(v.tensor_scalar(slotf[:, :, 0], slot_a, -1.0, None, ALU.add))
            then(v.tensor_scalar(slotf[:, :, 1], slot_b, -1.0, None, ALU.add))
            then(v.tensor_copy(slot_no, slotf))
            then(v.tensor_tensor(spn, spx, spn, ALU.add))
            then(v.tensor_tensor(sp_le, spn.unsqueeze(1).broadcast_to([P, SPARE, NE]), spare_i.unsqueeze(2).broadcast_to([P, SPARE, NE]), ALU.is_le))
            then(v.tensor_reduce(spf[:, 0:SPARE], sp_le, AX.X, ALU.add))
            then(v.tensor_copy(spf[:, SPARE:SPARE + 1], spn[:, NE - 1:NE]))
            v.tensor_copy(spare_info, spf).then_inc(S["slots_done"], 1)
            then(v.tensor_tensor(over, slot1, b16(slot_a), ALU.is_equal))
            then(v.tensor_tensor(ssel, over, comb, ALU.mult))
            then(v.tensor_reduce(slot_wt[:, :, 0], ssel, AX.X, ALU.add))
            then(v.tensor_tensor(comb, comb, ssel, ALU.subtract))
            then(v.tensor_reduce(slot_wt[:, :, 1], comb, AX.X, ALU.add))

            def tokens_out(k, first=False):
                dve.wait_ge(S["x_turned"], k * 2 + 2)
                if not first:
                    dve.wait_ge(S["up_mm"], k * 2)
                v.tensor_copy(xgT[:, 4:8, :].rearrange("p k t -> p (k t)"), bank[3][:, :]).then_inc(S["xT_dve"], 1)

            def hidden(k, first=False):
                dve.wait_ge(S["up_silu"], k + 1)
                dve.wait_ge(S["up_mm"], k * 2 + 2)
                if not first:
                    dve.wait_ge(S["h_turned"], k)
                v.tensor_tensor(hidv, upv, bank[1][:, :], ALU.mult).then_inc(S["hid_done"], 1)

            def hidden_out(k, first=False):
                dve.wait_ge(S["h_turned"], k + 1)
                if not first:
                    dve.wait_ge(S["dn_mm"], k * 2)
                v.tensor_copy(hidT.rearrange("p f t -> p (f t)"), bank[4][:, :]).then_inc(S["hidT_done"], 1)

            def out_half(k, first=False):
                dve.wait_ge(S["dn_mm"], k * 2 + 2)
                if not first:
                    dve.wait_ge(S["st_y"], k * 16)
                v.tensor_copy(eout[:, 512:D], bank[6][:, :]).then_inc(S["out_dve"], 1)

            tokens_out(0, first=True)
            hidden(0, first=True)
            tokens_out(1)
            hidden_out(0, first=True)
            hidden(1)
            tokens_out(2)
            out_half(0, first=True)
            with dve.Fori(2, NE - 1) as e:
                hidden_out(e - 1)
                hidden(e)
                tokens_out(e + 1)
                out_half(e - 1)
            hidden_out(NE - 2)
            hidden(NE - 1)
            out_half(NE - 2)
            hidden_out(NE - 1)
            out_half(NE - 1)
            n_spare = dve.value_load(spare_info[0:1, SPARE:SPARE + 1], min_val=0, max_val=SPARE)
            with dve.Fori(0, SPARE) as i:
                with dve.If(i < n_spare):
                    tokens_out(i + NE)
                    hidden(i + NE)
                    hidden_out(i + NE)
                    out_half(i + NE)

            for b in range(TB):
                dve.wait_ge(ld_back[b], 32)
                h, ya, yb = n1[:, b, :], by_token[:, b, 0, :], by_token[:, b, 1, :]
                then(v.tensor_scalar(h, h, ALPHA, None, ALU.mult))
                then(v.scalar_tensor_tensor(out=h, in0=ya, scalar=slot_wt[:, b, 0:1], in1=h, op0=ALU.mult, op1=ALU.add))
                then(v.scalar_tensor_tensor(out=h, in0=yb, scalar=slot_wt[:, b, 1:2], in1=h, op0=ALU.mult, op1=ALU.add))
                then(stats_of(b, [h[:, 0:512], h[:, 512:D]]))
            add_eps()
            dve.wait_ge(S["ln_sd"], 3)
            then(v.reciprocal(rstd, sdev))
            dve.wait_ge(S["ld_ln"], 32)
            for b in range(TB):
                h = n1[:, b, :]
                then(v.tensor_scalar(h, h, mv[:, b, 0:1], rstd[:, b:b + 1], ALU.subtract, ALU.mult))
                then(v.tensor_tensor(h, h, lnr[:, 0, :], ALU.mult))
                v.tensor_tensor(obuf[:, b, :], h, lnr[:, 1, :], ALU.add).then_inc(S["ln2_out"], 1)


def shape_constants():
    fixed = np.zeros((P, K_END), np.float32)
    fixed[:, K_ID:K_ID + P] = np.eye(P)
    s, l = np.arange(P)[:, None], np.arange(P)[None, :]
    fixed[:, K_TRI:K_TRI + P] = s <= l
    fixed[:, K_CAP:K_CAP + P] = np.where(s <= l, -NEG, NEG)
    fixed[:, K_AID:K_AID + P] = np.eye(P) * ALPHA
    fixed[:, K_ONE:K_ONE + P] = 1.0
    fixed[:, K_ROW] = np.arange(P) >= CMP_LEN - 1
    fixed[:, K_LOW:K_LOW + 16] = (np.arange(4)[None, :] < np.arange(4)[:, None]).reshape(-1)
    e = np.arange(NE)
    fixed[:, K_EID:K_EID + NE], fixed[:, K_EOFF:K_EOFF + NE] = e, NE - 1 - e
    fixed[:, K_THR:K_THR + 3], fixed[:, K_SPI:K_SPI + SPARE] = P * (np.arange(3) + 1), np.arange(SPARE)
    fixed[:, K_LOW16:K_LOW16 + NE * NE] = (e[None, :] < e[:, None]).reshape(-1)
    for g, w in enumerate(WINDOWS):
        fixed[:, K_INV + 16 * g:K_INV + 16 * (g + 1)] = 1.0 / np.minimum(np.arange(16) + 1, w)
    dist = T - 1 - np.arange(REVN)
    n = np.maximum(dist, 0)
    exact = BUCKETS // 2
    nf = np.maximum(n, 1).astype(np.float32)
    large = exact + (np.log(nf / np.float32(exact)) / np.float32(math.log(MAX_DIST / exact)) * np.float32(BUCKETS - exact)).astype(np.int32)
    bucket = np.where(n < exact, n, np.minimum(large, BUCKETS - 1))
    onehot = np.zeros((BUCKETS + 1, REVN), np.float32)
    onehot[np.where(dist < 0, BUCKETS, bucket), np.arange(REVN)] = 1.0
    return fixed, onehot


def kernel(**inputs):
    import concourse.bacc as bacc
    from concourse.bass_utils import run_bass_kernel_spmd

    a = {k: np.asarray(v) for k, v in inputs.items()}
    w_in = a["w_in"][0]
    c_pool, c_q, c_kv = 0, 512, 1024
    c_ng = c_kv + 768
    c_ssd = c_ng + 24
    c_gate = c_ssd + 3088

    def lhs(w):
        return w.reshape(KT, P, P).transpose(1, 0, 2).reshape(P, D)

    cols128 = lambda c: w_in[:, c:c + P]
    tiles = [cols128(c_kv), cols128(c_kv + P), cols128(c_kv + 2 * P), cols128(c_kv + 4 * P)]
    for i in range(HPG):
        tiles.append(np.concatenate([w_in[:, c_q + i * DH:c_q + (i + 1) * DH],
                                     w_in[:, c_q + (HPG + i) * DH:c_q + (HPG + i + 1) * DH]], axis=1))
    tiles += [cols128(c_pool + i * P) for i in range(4)]
    tiles += [cols128(c_ssd + D + i * P) for i in range(16)]
    assert len(tiles) == CM_PROJ

    def gates(j):
        return [cols128(c_gate + b * D + j * P) for b in range(3)]

    def branches(j):
        sl = slice(j * P, (j + 1) * P)
        return [np.concatenate([a["w_br_pool"][0][:, sl], a["w_br_nsa"][0][:, sl]], axis=0), a["w_br_ssd"][0][:, sl]]

    for j in range(EARLY):
        tiles += gates(j)
    for j in range(EARLY):
        tiles += branches(j)
    for j in range(EARLY, KT):
        tiles += gates(j) + branches(j)
    w_cm = np.stack([lhs(w) for w in tiles])

    def rhs(w):
        return w.reshape(-1, P, w.shape[1]).transpose(1, 0, 2)

    w_tm = np.stack([rhs(w_in[:, c_ssd + h * 512:c_ssd + (h + 1) * 512]) for h in range(2)])
    w_vd = rhs(np.concatenate([cols128(c_kv + 3 * P), cols128(c_kv + 5 * P), w_in[:, c_ssd + 3072:c_ssd + 3088],
                               w_in[:, c_ng:c_ng + 24]], axis=1))
    percol = lambda u: u.reshape(-1, P).T
    cols = np.concatenate([
        percol(a["ln0_g"]), percol(a["ln0_b"]), percol(a["ln1_g"][0]), percol(a["ln1_b"][0]), percol(a["pool_scale"][0]),
        percol(a["conv_w"][0].reshape(-1)), percol(a["conv_b"][0]), percol(a["ssd_norm_g"][0]),
        percol(a["cmp_k_pe"][0].reshape(-1)), percol(a["cmp_v_pe"][0].reshape(-1))], axis=1)
    rows = np.concatenate([a["dt_bias"][0], a["a_log"][0], a["d_skip"][0], a["router_b"]])[None]
    fixed, onehot = shape_constants()
    table = np.concatenate([a["rel_bias"], np.full((1, HEADS), NEG, np.float32)], axis=0)
    e13 = np.stack([a["exp_w1"][0], a["exp_w3"][0]], axis=1).reshape(NE, 2, KT, P, DE).transpose(0, 3, 1, 2, 4)
    arrays = {
        "x": a["x"][0], "w_cm": w_cm, "w_tm": w_tm, "w_vd": w_vd, "cols": cols, "rows": rows,
        "lnrows": np.stack([a["ln1_g"][0], a["ln1_b"][0], a["ln2_g"][0], a["ln2_b"][0]]), "fixed": fixed, "onehot": onehot, "table": table,
        "pool_w": a["pool_w"][0].transpose(1, 0, 2),
        "w1c_in": np.stack([rhs(a["cmp_k_w1"][0]), rhs(a["cmp_v_w1"][0])], axis=1),
        "w2kv": np.stack([a["cmp_k_w2"][0], a["cmp_v_w2"][0]], axis=1),
        "w_out": np.stack([rhs(a["w_out"][0][:, h * 512:(h + 1) * 512]) for h in range(2)]),
        "w_rt": rhs(a["router_w"]),
        "e13": e13, "e2": a["exp_w2"][0].reshape(NE, FT, P, D).transpose(0, 2, 1, 3),
    }
    nc = bacc.Bacc("TRN2", target_bir_lowering=False, num_devices=1)
    handles = {}
    for name in arrays:
        arrays[name] = np.ascontiguousarray(arrays[name])
        handles[name] = nc.dram_tensor(f"in_{name}", arrays[name].shape, F32, kind="ExternalInput").ap()
    out = nc.dram_tensor("out", (T, D), F32, kind="ExternalOutput").ap()
    bias_dram = nc.dram_tensor("bias_rows", (HEADS, P * (REVN + 1)), F32, kind="Internal").ap()
    xs_dram, ys_dram = (nc.dram_tensor(n, ((NE + SPARE) * P, D), F32, kind="Internal").ap() for n in ("slots_in", "slots_out"))
    build_program(nc, out=out, bias_dram=bias_dram, xs_dram=xs_dram, ys_dram=ys_dram, **handles)
    r = run_bass_kernel_spmd(nc, [{f"in_{k}": v for k, v in arrays.items()}], core_ids=[0])
    return r.results[0]["out"].reshape(1, T, D)
```

```python
import math
from contextlib import ExitStack

import numpy as np
import concourse.bass as bass
from concourse import mybir

F32 = mybir.dt.float32
F32R = mybir.dt.float32r
ALU = mybir.AluOpType
ACT = mybir.ActivationFunctionType
AX = mybir.AxisListType

P = 128
T = 512
D = 1024
TB = T // P
KT = D // P
ALPHA = 2.0 ** 0.25
LN_EPS = 1e-5
NEG = -1e30

HEADS, KVG, HPG, DH = 8, 2, 4, 64
BUCKETS = 32
MAX_DIST = 128
CMP_LEN, CMP_STRIDE = 32, 16
NCMP = (T - CMP_LEN) // CMP_STRIDE + 1
WINDOWS = (2, 4, 8, 16)

SG, SE, SP, SN = 4, 4, 64, 128
SH = SG * SE
NE, DE = 16, 512
FT = DE // P
SPARE = (2 * T - NE) // P

CM_PROJ = 28
EARLY = 3
CM_EARLY = CM_PROJ + 3 * EARLY
CM_LOOP = CM_EARLY + 2 * EARLY
BR_TILES = 5
SLOTS = 5
VD = 2 * P + SH + 3 * HEADS
REVN = T + P

C_LN0G, C_LN0B, C_LN1G, C_LN1B, C_PS, C_CW, C_CB, C_NG, C_PEK, C_PEV, C_END = (
    0, 8, 16, 24, 32, 36, 100, 116, 124, 140, 156)
K_ID, K_TRI, K_CAP, K_AID, K_ONE, K_ROW, K_LOW, K_INV, K_EID, K_EOFF, K_THR, K_SPI, K_LOW16, K_END = (
    0, 128, 256, 384, 512, 640, 641, 657, 721, 737, 753, 756, 763, 1019)
R_DTB, R_ALOG, R_DSK, R_RB = 0, 16, 32, 48


def build_program(nc, x, w_cm, w_tm, w_vd, cols, rows, lnrows, fixed, onehot, table, pool_w, w1c_in, w2kv,
                  w_out, w_rt, e13, e2, out, bias_dram, xs_dram, ys_dram):
    with ExitStack() as ctx:
        def sb(name, shape, dtype=F32):
            return ctx.enter_context(nc.sbuf_tensor(name, shape, dtype))

        def sem(name):
            return ctx.enter_context(nc.semaphore(name))

        bank = [ctx.enter_context(nc.psum_tensor(f"bank{i}", [P, 512], F32)) for i in range(8)]

        widths = (("r_mid", 4096 + SLOTS * D + 4096), ("r_big", 6 * 4096), ("r_tmp", 5632), ("r_late", 6144),
                  ("r_vbd", KVG * HPG * DH), ("fix", K_END))
        with ExitStack() as plain:
            r_mid, r_big, r_tmp, r_late, r_vbd, fix = (plain.enter_context(nc.sbuf_tensor(n, [P, w], F32)) for n, w in widths)
        s_mid, s_big, s_tmp, s_late, s_vbd, s_fix = (sb(n + "_split", [P, w], F32R) for n, w in widths)
        r_h, r_ring, r_qkv = (r_mid[:, a:b] for a, b in ((0, 4096), (4096, 9216), (9216, 13312)))
        r_o, r_oT, r_pool = (r_late[:, i * 2048:(i + 1) * 2048] for i in range(3))
        colv = sb("colv", [P, C_END])
        rowv = sb("rowv", [P, 4 * SH])
        small = sb("small", [P, 1280])
        kcT = sb("kcT", [P, NCMP])

        def view(region, off, *dims):
            v = region[:, off:off + int(np.prod(dims))]
            names = "abcde"[:len(dims)]
            if len(dims) == 1:
                return v
            return v.rearrange(f"p ({' '.join(names)}) -> p {' '.join(names)}",
                               **{n: d for n, d in zip(names[1:], dims[1:])})

        vbd = view(r_vbd, 0, KVG, HPG, DH)
        hT = view(r_h, 0, KT, T)
        ring = view(r_ring, 0, SLOTS, KT, P)
        h1T = view(r_ring, 0, KT, T)
        zs = view(r_big, 0, TB, D)
        ytok = view(r_big, 4096, TB, D)
        xsT = view(r_big, 8192, 8, T)
        bcT = view(r_big, 16384, 8, T)
        strips = view(r_big, 20480, HEADS, T)
        btok = view(r_big, 20480, TB, SG, SN)
        xin = view(r_big, 0, TB, D)
        xnorm = view(r_big, 4096, TB, D)
        wz = [view(r_big, 4096, KT, 512), view(r_big, 12288, KT, 512)]
        wvd = view(r_big, 8192, KT, VD)
        w1c = view(r_big, 16384, 2, 16, P)
        wo = view(r_big, 16384, 2, KT, 512)
        qT = view(r_qkv, 0, 4, T)
        kT = [view(r_qkv, 2048, T), view(r_qkv, 2560, T)]
        vtok = view(r_qkv, 3072, TB, 2, KVG, DH)
        mT = view(r_qkv, 0, KT, T)
        early = [view(r_big, 22528 + 512 * m, T) for m in range(4)] + [view(r_qkv, 512 * m, T) for m in range(EARLY, KT)]
        tok2 = view(r_o, 0, 2, KVG, T)
        oacc = view(r_o, 0, TB, HEADS, DH)
        oT = view(r_oT, 0, 4, T)
        pcs = view(r_oT, 0, TB, HEADS, 32)
        pct = view(r_oT, 1024, 2, 2, P)
        poolT = view(r_pool, 0, 4, T)
        blocks = view(r_pool, 0, 2, CMP_LEN // 2, KVG, NCMP)

        ring_lo = view(s_mid, 4096, SLOTS, KT, P)
        ring_hi = [view(r, o, KT, P) for r, o in ((s_big, 20480), (s_late, 0), (s_late, D), (s_tmp, 3072), (s_tmp, 4096))]
        h_hi, h_lo = view(s_big, 4096, KT, T), view(s_mid, 0, KT, T)
        proj_h_lo = view(s_big, 12288, KT, T)
        proj_hi = [view(s_big, i * D, KT, P) for i in range(4)]
        y_hi, y_lo = view(s_big, 0, KT, T), view(s_big, 12288, KT, T)
        o_hi, o_lo = view(s_big, 8192, 4, T), view(s_late, 2048, 4, T)
        pool_hi, pool_lo = view(s_big, 10240, 4, T), view(s_late, 4096, 4, T)

        ident, tri, cap, aident, ones = (fix[:, k:k + P] for k in (K_ID, K_TRI, K_CAP, K_AID, K_ONE))
        rowok = fix[:, K_ROW:K_ROW + 1]
        eid = fix[:, K_EID:K_EID + NE]
        eoff = fix[:, K_EOFF:K_EOFF + NE]
        thr = fix[:, K_THR:K_THR + 3]
        spare_i = fix[:, K_SPI:K_SPI + SPARE]
        lower16 = fix[:, K_LOW16:K_LOW16 + NE * NE].rearrange("p (i j) -> p i j", i=NE)
        lower = fix[:, K_LOW:K_LOW + 16].rearrange("p (i j) -> p i j", i=4)
        invc = fix[:, K_INV:K_INV + 64].rearrange("p (g w) -> p g w", g=4)

        used = [0]

        def sm(*dims):
            n = int(np.prod(dims))
            used[0] += n
            assert used[0] <= 1280
            return view(small, used[0] - n, *dims)

        stats, mv, sdev, rstd = sm(TB, 2, 6), sm(TB, 2), sm(TB), sm(TB)
        dtx, dtm, dte, dt, dta = sm(TB, SH), sm(TB, SH), sm(TB, SH), sm(TB, SH), sm(TB, SH)
        acs, negacs, eacs, decin, cdec = sm(TB, SH), sm(TB, SH), sm(TB, SH), sm(TB, SH), sm(TB, SH)
        expa = sm(SH)
        shift = sm(TB)
        ngate = sm(TB, 3, HEADS)
        nmax, psums = sm(2, TB, HEADS), sm(2, TB, HEADS)
        ogate = sm(3, TB, HEADS)
        cmax, csum = sm(TB, HEADS), sm(TB, HEADS)
        yss, yrt, yrs = sm(TB, SG), sm(TB, SG), sm(TB, SG)
        slot_wt = sm(TB, 2)
        slot_no = sm(TB, 2).bitcast(mybir.dt.uint32)
        spare_info = sm(SPARE + 1).bitcast(mybir.dt.int32)

        onehot_sb, table_sb = r_tmp[0:BUCKETS + 1, 0:REVN], r_tmp[0:BUCKETS + 1, REVN:REVN + HEADS]
        bias_sb = r_tmp[0:HEADS, 700:700 + REVN]
        w2c = view(r_tmp, 1400, 2, DH)
        hidc = view(r_tmp, 1600, 2, KVG, NCMP)
        poolw = view(r_tmp, 1800, 4, P)
        praw = view(r_tmp, 2320, T + 16)
        pw = [view(r_tmp, 2320 + 528 * (i + 1), T + 16) for i in range(2)]
        pr = view(r_tmp, 3904, T)
        att_s = [view(r_tmp, 512 * i, 512) for i in range(3)]
        att_p = [view(r_tmp, 1536 + 512 * i, 512) for i in range(3)]
        att_pt = [view(r_tmp, 3072 + 512 * i, 4, P) for i in range(3)]
        osc = view(r_tmp, 4608, HEADS, DH)
        xdt = [view(r_tmp, 0, D), view(r_o, 0, D)]
        xdd = view(r_tmp, 1024, D)
        xsd = view(r_tmp, 2048, D)
        segd = [view(r_tmp, 3072 + 512 * i, SE, P) for i in range(2)]
        segm = [view(r_tmp, 4096 + 512 * i, SE, P) for i in range(2)]
        yoff = view(r_tmp, 5120, SE, SP)
        hst = view(r_o, 1024, SG, SE * SP)
        gsb = [view(r_tmp, 512 * i, 512) for i in range(3)]
        gm = [view(r_tmp, 1536 + 512 * i, 512) for i in range(3)]
        n1 = view(r_tmp, 0, TB, D)
        wrt = view(r_pool, 0, KT, NE)
        lnr = view(r_late, 0, 2, D)
        lnr2 = view(r_late, D, 2, D)
        ew13 = [view(r, o, 2, KT, DE) for r, o in ((r_big, 0), (r_big, 12288), (r_mid, 0))]
        ew2 = [view(r, o + 8192, FT, D) for r, o in ((r_big, 0), (r_big, 12288), (r_mid, 0))]
        w2_lo = [view(r, o + 8192, FT, D) for r, o in ((s_big, 0), (s_big, 12288), (s_mid, 0))]
        w2_hi = [view(s_late, 5120, 512), view(s_late, 5632, 512), view(s_vbd, 0, 512)]
        hidT_hi, hidT_lo = view(s_fix, P, FT, P), view(s_tmp, 5120, FT, P)
        xg = [view(r_late, i * D, D) for i in range(3)]
        xgT = view(r_late, 3 * D, KT, P)
        eout = view(r_late, 4 * D, D)
        upv, hidv = view(r_tmp, 4096, DE), view(r_tmp, 4608, DE)
        by_token = view(r_big, 0, TB, 2, D)
        obuf = view(r_mid, 0, TB, D)
        zeros = view(r_oT, 1536, 512)
        zrow = zeros.unsqueeze(1).broadcast_to([P, 2, 512])

        def rv(k, *dims):
            return view(r_pool, 128 + k * 64, *(dims or (TB, NE)))

        prob, score, lg, ssel, comb, pos, over, slot1 = (rv(k) for k in (0, 1, 2, 4, 5, 6, 7, 8))
        sel_zeros = view(r_pool, 1600, 2 * TB - 1, NE)
        sel = sel_zeros[:, TB - 1:, :]
        gt, ge = view(r_pool, 704, TB * 4, 4, 4), view(r_pool, 960, TB * 4, 4, 4)
        big16 = view(r_pool, 704, NE, NE)
        rank, gsc, grank, ing = (view(r_pool, 1216, TB * 4, 4), view(r_pool, 1280, TB, 4),
                                 view(r_pool, 1296, TB, 4), view(r_pool, 1312, TB, 4))
        lmax, lsum, wden = view(r_pool, 1328, TB), view(r_pool, 1332, TB), view(r_pool, 1336, TB)
        slot_a, slot_b = view(r_pool, 1340, TB), view(r_pool, 1344, TB)
        cnt, spn, spx = view(r_pool, 1348, NE), view(r_pool, 1364, NE), view(r_pool, 1380, NE)
        slotf, spf = view(r_pool, 1396, TB, 2), view(r_pool, 1404, SPARE + 1)
        thr_gt = view(r_pool, 1412, NE, 3)
        sp_le = view(r_pool, 1460, SPARE, NE)

        names = """ld_const ld_cmp ld_vd ld_strip ld_poolw st_bias ld_wo ld_ln st_out
            ln_stat ln_sd ln_rstd ln_norm ln_turned hT_act hT_dve
            proj_done act_freed dve_freed cmp_in cmp_mm cmp_hid cmp2_mm cmp_kc cmp_vc bias_mm bias_rows zeroed
            vd_mm vd_used z_mm z_out z_silu pool_out pool_mm pool_scaled conv_first conv_sum conv_done dv gp
            soft_abs soft_ln decay_a gates_e sc_mm sc_max p_done p_turned pt_copied o_mm o_read o_acc o_turned oT_copied
            cs_mm cs_sub cs_exp cs_turned cs_copied co_mm co_read
            acs_mm acs_neg acs_exp bt_turned bt_copied xt_turned xt_copied xdt_done xdd_done xsd_done
            seg_mm seg_cap seg_exp seg_done y_mm y_read early_out st_mm st_new y_gated y_sq y_ms y_sd y_norm y_turned yT_done yT_low hi_done gp_lo tile_lo
            gate_mm gate_sig br_mm br_used m_add mT_done mix_mm rt_mm rt_max rt_exp
            zero_tile zeroed_x sel_done pos_mm slots_done ld_ln1 st_h x_turned xT_act xT_dve
            up_mm up_silu hid_done h_turned hidT_done dn_mm out_act out_dve st_y h1_half h1_norm h1_turned h1T_act h1T_dve h_scaled ya_scaled ya_added ln2_norm ln2_g ln2_out ln2_last""".split()
        S = {n: sem(n) for n in names}
        ld_x = [sem(f"ld_x{i}") for i in range(TB)]
        ld_z = [sem(f"ld_z{i}") for i in range(2)]
        ld_ring = [sem(f"ld_ring{i}") for i in range(SLOTS)]
        ld_w13 = [sem(f"ld_w13_{i}") for i in range(3)]
        ld_w2 = [sem(f"ld_w2_{i}") for i in range(3)]
        ld_xg = [sem(f"ld_xg{i}") for i in range(3)]
        ld_back = [sem(f"ld_back{i}") for i in range(TB)]

        NCONST = 3
        CMP_AT = 15

        def release(i):
            if i < 2:
                return S["dve_freed"], i + 1
            if i < 12:
                return S["act_freed"], i - 1
            return S["conv_sum"], 3 * (i - 11)

        loads = [len([i for i in range(CM_EARLY) if i % SLOTS == s]) for s in range(SLOTS)]
        def proj_bank(i):
            return bank[i % 2] if i < 12 else bank[(0, 1, 6, 7)[i % 4]]

        NU, Z_AT = 2 * TB * HEADS, 4
        SPLIT_AT = 2
        HI0 = CM_PROJ - SPLIT_AT + KT
        PEELED = [(3, 1, HI0 + 9, HI0 + 1), (4, 1, HI0 + 10, HI0 + 2), (0, 1, HI0 + 11, HI0 + 3),
                  (1, 1, HI0 + 12, HI0 + 4), (2, 1, HI0 + 13, HI0 + 5), (3, 2, HI0 + 14 + KT, HI0 + 6)]
        LOOP_HI, LOOP_LO = HI0 + 15 + KT, HI0 + 2 * EARLY + 1
        HI_EXP, LO_EXP = LOOP_HI - 1 + BR_TILES * (KT - EARLY), LOOP_LO - 1 + BR_TILES * (KT - EARLY)
        AGAIN = [1, 1, 1, 2, 1]
        EARLY_IN_SSD = 7

        def early_bank(i):
            return bank[6] if i < EARLY_IN_SSD else bank[i - EARLY_IN_SSD]

        state_bank = bank[7][:, 0:256]

        Y_TURNS = [(0, 0), (1, 0), (2, 0), (0, 1), (1, 1), (2, 1), (3, 0), (3, 1)]
        units = [(br, qb, h) for br in range(2) for qb in range(TB) for h in range(HEADS)]
        nvalid = [7 + 8 * qb for qb in range(TB)]
        groups = [(c, g) for c in range(TB) for g in range(SG)]
        block = ctx.enter_context(nc.Block())

        @block.sync
        def _(sp):
            for b in range(TB):
                sp.dma_start(xin[:, b, :], x[b * P:(b + 1) * P, :]).then_inc(ld_x[b], 16)
            sp.dma_start(fix[:, :], fixed).then_inc(S["ld_const"], 16)
            sp.dma_start(colv[:, :], cols).then_inc(S["ld_const"], 16)
            sp.dma_start(rowv[:, :], rows.partition_broadcast(P)).then_inc(S["ld_const"], 16)

            def load_tile(i):
                if i >= SLOTS:
                    sp.wait_ge(S["proj_done"], i - SLOTS + 1)
                sp.dma_start(ring[:, i % SLOTS, :, :], w_cm[i].rearrange("p (k n) -> p k n", k=KT)
                             ).then_inc(ld_ring[i % SLOTS], 16)

            for i in range(4):
                load_tile(i)
            sp.dma_start(w1c, w1c_in).then_inc(S["ld_cmp"], 16)
            sp.dma_start(w2c, w2kv).then_inc(S["ld_cmp"], 16)
            sp.dma_start(onehot_sb, onehot).then_inc(S["ld_cmp"], 16)
            sp.dma_start(table_sb, table).then_inc(S["ld_cmp"], 16)
            load_tile(4)
            sp.dma_start(wvd, w_vd).then_inc(S["ld_vd"], 16)
            for i in range(5, 9):
                load_tile(i)
            sp.dma_start(poolw, pool_w).then_inc(S["ld_poolw"], 16)
            for i in range(9, 12):
                load_tile(i)
            sp.wait_ge(S["bias_rows"], 2)
            skewed = bass.AP(bias_dram.tensor, 0, [[P * (REVN + 1), HEADS], [REVN + 1, P], [1, REVN]])
            sp.dma_start(skewed, bias_sb.unsqueeze(1).broadcast_to([HEADS, P, REVN])).then_inc(S["st_bias"], 16)
            sp.wait_ge(S["st_bias"], 16)
            strip_src = bass.AP(bias_dram.tensor, P - 1, [[REVN, P], [P * (REVN + 1), HEADS], [1, T]])
            sp.dma_start(strips, strip_src).then_inc(S["ld_strip"], 16)
            for i in range(12, CM_PROJ):
                load_tile(i)
                if i == 12:
                    sp.wait_ge(S["zero_tile"], 1)
                for n in range(2 * (i - 12), 2 * (i - 11)):
                    if n < NE + SPARE:
                        sp.dma_start(xs_dram[n * P:(n + 1) * P, :].rearrange("p (a n) -> p a n", a=2), zrow).then_inc(S["zeroed_x"], 16)
                    elif n < NE + 2 * SPARE:
                        m = n - SPARE
                        sp.dma_start(ys_dram[m * P:(m + 1) * P, :].rearrange("p (a n) -> p a n", a=2), zrow).then_inc(S["zeroed_x"], 16)

            for i in range(CM_PROJ, CM_PROJ + 2):
                load_tile(i)
            sp.wait_ge(S["proj_done"], CM_PROJ)
            for half in range(2):
                sp.dma_start(wz[half], w_tm[half]).then_inc(ld_z[half], 16)
            for i in range(CM_PROJ + 2, CM_EARLY):
                load_tile(i)

            def load_slot(s, tile):
                src = w_cm[bass.ds(tile, 1), :, :].rearrange("a p (k n) -> (a p) k n", k=KT)
                sp.dma_start(ring[:, s, :, :], src).then_inc(ld_ring[s], 16)

            for q in range(BR_TILES):
                s = PEELED[q][0]
                sp.wait_ge(S["proj_done"], max(i for i in range(CM_EARLY) if i % SLOTS == s) + 1)
                load_slot(s, CM_EARLY + q)
            sp.wait_ge(S["y_mm"], 16)
            sp.dma_start(wo[:, 0], w_out[0]).then_inc(S["ld_wo"], 16)
            sp.wait_ge(S["br_mm"], 2)
            load_slot(3, CM_EARLY + 5)
            for s, used in ((4, 3), (0, 5), (1, 6), (2, 8), (3, 9)):
                sp.wait_ge(S["br_mm"], used)
                load_slot(s, CM_LOOP + s)
            with sp.Fori(EARLY + 1, KT) as j:
                for s in range(BR_TILES):
                    if s < 3:
                        sp.wait_ge(S["gate_mm"], j * 3 + (s - 2 - 3 * EARLY))
                    else:
                        sp.wait_ge(S["br_mm"], j * 3 + (s - 4))
                    load_slot(s, CM_LOOP + s - BR_TILES * EARLY + j * BR_TILES)

            def load_w13(e, slot, m):
                src = e13[bass.ds(e, 1), :, m].rearrange("a p k f -> (a p) k f")
                sp.dma_start(ew13[slot][:, m], src).then_inc(ld_w13[slot], 16)

            def load_w2(e, slot):
                sp.dma_start(ew2[slot], e2[bass.ds(e, 1)].rearrange("a p k n -> (a p) k n")).then_inc(ld_w2[slot], 16)

            def load_expert(e, slot):
                for m in range(2):
                    load_w13(e, slot, m)
                load_w2(e, slot)

            def load_tokens(tile, buf):
                sp.dma_start(xg[buf], xs_dram[bass.ds(tile * P, P), :]).then_inc(ld_xg[buf], 16)

            sp.wait_ge(S["gate_mm"], 3 * (KT - EARLY))
            sp.dma_start(wo[:, 1], w_out[1]).then_inc(S["ld_wo"], 16)
            for i in range(2):
                sp.dma_start(lnr[:, i, :], lnrows[i:i + 1, :].partition_broadcast(P)).then_inc(S["ld_ln1"], 16)
            sp.wait_ge(S["gp_lo"], 8 + 2 * KT)
            sp.wait_ge(S["br_mm"], 3 * KT)
            load_expert(0, 0)
            sp.wait_ge(S["mT_done"], KT)
            sp.dma_start(wrt, w_rt).then_inc(S["ld_ln1"], 16)
            sp.wait_ge(S["mix_mm"], TB)
            load_expert(1, 1)
            sp.wait_ge(S["rt_mm"], 1)
            for m in range(2):
                load_w13(2, 2, m)
            sp.wait_ge(S["st_h"], 16 * 2 * TB)
            for e in range(3):
                load_tokens(e, e)
            load_w2(2, 2)

            def refill(e, slot, first=False):
                sp.wait_ge(S["x_turned"], e * 2 - 4)
                load_tokens(e, slot)
                for m in range(2):
                    sp.wait_ge(S["up_mm"], e * 2 - (5 - m))
                    load_w13(e, slot, m)
                if not first:
                    sp.wait_ge(S["dn_mm"], e * 8 - 24)
                    load_w2(e - 1, (slot + 2) % 3)

            refill(3, 0, first=True)
            with sp.Fori(1, (NE - 1) // 3) as i:
                for d in (1, 2, 3):
                    refill(i * 3 + d, d % 3)
            sp.wait_ge(S["dn_mm"], NE * 8 - 24)
            load_w2(NE - 1, 0)
            sp.wait_ge(S["x_turned"], 2 * (NE - 1))
            for i in range(2):
                sp.dma_start(lnr2[:, i, :], lnrows[2 + i:3 + i, :].partition_broadcast(P)).then_inc(S["ld_ln"], 16)
            n_spare = sp.value_load(spare_info[0:1, SPARE:SPARE + 1], min_val=0, max_val=SPARE)
            with sp.Fori(0, SPARE) as i:
                with sp.If(i < n_spare):
                    e = sp.value_load(spare_info[0:1, bass.ds(i, 1)], min_val=0, max_val=NE - 1)
                    sp.wait_ge(S["dn_mm"], (i + NE) * 8)
                    load_tokens(i + NE, 0)
                    load_expert(e, 0)
            for b in range(TB):
                if b < TB - 1:
                    sp.wait_ge(S["ln2_out"], b + 1)
                else:
                    sp.wait_ge(S["ln2_last"], 1)
                sp.dma_start(out[b * P:(b + 1) * P, :], obuf[:, b, :]).then_inc(S["st_out"], 16)
            sp.wait_ge(S["st_out"], 16 * TB)

        @block.tensor
        def _(pe):
            mm = nc.tensor.matmul
            tr = nc.tensor.transpose
            pe.wait_ge(S["ld_const"], 16 * NCONST)
            pe.wait_ge(S["ln_norm"], TB)
            for k in range(KT):
                for b in range(TB):
                    last = tr(bank[k][:, b * P:(b + 1) * P], xnorm[:, b, k * P:(k + 1) * P], ident)
                last.then_inc(S["ln_turned"], 1)

            def split_mm(acc, w_hi, w_lo, x_hi, x_lo, start, stop):
                mm(acc, w_hi, x_hi, start=start, stop=False)
                mm(acc, w_hi, x_lo, start=False, stop=False)
                return mm(acc, w_lo, x_hi, start=False, stop=stop)

            def proj(i):
                if i < SPLIT_AT:
                    pe.wait_ge(ld_ring[i % SLOTS], 16 * (i // SLOTS + 1))
                else:
                    pe.wait_ge(S["hi_done"], KT + i - SPLIT_AT + 1)
                    pe.wait_ge(S["tile_lo"], KT + i - SPLIT_AT + 1)
                if i in (14, 15):
                    pe.wait_ge(S["bias_rows"], 2)
                elif i >= 2:
                    pe.wait_ge(*release(i - (4 if i >= 16 else 2)))
                for k in range(KT):
                    if i < SPLIT_AT:
                        last = mm(proj_bank(i)[:, :], ring[:, i % SLOTS, k, :], hT[:, k, :], start=(k == 0), stop=(k == KT - 1))
                    else:
                        last = split_mm(proj_bank(i)[:, :], proj_hi[i % 4][:, k, :], ring_lo[:, i % SLOTS, k, :], h_hi[:, k, :], proj_h_lo[:, k, :],
                                        start=(k == 0), stop=(k == KT - 1))
                last.then_inc(S["proj_done"], 1)

            pe.wait_ge(S["hT_act"], KT // 2)
            pe.wait_ge(S["hT_dve"], KT // 2)
            for i in range(8):
                proj(i)

            pe.wait_ge(S["ld_cmp"], 64)
            for kv in range(2):
                pe.wait_ge(S["cmp_in"], 2 * kv + 2)
                for l in range(CMP_LEN // 2):
                    last = mm(bank[2 + kv][:, 0:KVG * NCMP], w1c[:, kv, l, :], blocks[:, kv, l, :, :].rearrange("p g n -> p (g n)"),
                              start=(l == 0), stop=(l == CMP_LEN // 2 - 1))
                last.then_inc(S["cmp_mm"], 1)
            for i in range(2):
                mm(bank[6 + i][0:HEADS, 0:REVN // 2], table_sb, onehot_sb[:, i * REVN // 2:(i + 1) * REVN // 2],
                   start=True, stop=True).then_inc(S["bias_mm"], 1)
            pe.wait_ge(S["cmp_hid"], 2)
            for g in range(KVG):
                mm(bank[4][g * DH:(g + 1) * DH, 0:NCMP], w2c[:, 0, :], hidc[:, 0, g, :], start=True, stop=True)
            for g in range(KVG):
                for h in range(HPG):
                    last = mm(bank[5][32 * h:32 * h + NCMP, g * DH:(g + 1) * DH], hidc[:, 1, g, :], w2c[:, 1, :],
                              start=True, stop=True)
            last.then_inc(S["cmp2_mm"], 1)
            pe.wait_ge(S["ld_vd"], 16)
            pe.wait_ge(S["cmp_kc"], 1)
            pe.wait_ge(S["cmp_vc"], HPG)
            for b in range(TB):
                for k in range(KT):
                    last = mm(bank[2 + b][:, 0:VD], hT[:, k, b * P:(b + 1) * P], wvd[:, k, :], start=(k == 0), stop=(k == KT - 1))
                last.then_inc(S["vd_mm"], 1)

            def cmp_scores(qb):
                if qb == 0:
                    pe.wait_ge(S["act_freed"], 6)
                    pe.wait_ge(S["cmp_kc"], 1)
                    pe.wait_ge(S["vd_used"], TB)
                else:
                    pe.wait_ge(S["cs_sub"], qb)
                nv = nvalid[qb]
                for h in range(HEADS):
                    g, i = divmod(h, HPG)
                    last = mm(bank[2 + g][:, 32 * h:32 * h + nv], qT[g * DH:(g + 1) * DH, i, qb * P:(qb + 1) * P],
                              kcT[g * DH:(g + 1) * DH, 0:nv], start=True, stop=True)
                last.then_inc(S["cs_mm"], 1)

            def cmp_turn(qb):
                pe.wait_ge(S["cs_exp"], qb + 1)
                if qb >= 1:
                    pe.wait_ge(S["cs_copied"], qb)
                for g in range(KVG):
                    last = tr(bank[4][:, g * P:(g + 1) * P], pcs[:, qb, g * HPG:(g + 1) * HPG, :].rearrange("p h n -> p (h n)"), ident)
                last.then_inc(S["cs_turned"], 1)

            def cmp_values(qb):
                pe.wait_ge(S["cs_copied"], qb + 1)
                pe.wait_ge(S["cmp_vc"], HPG)
                if qb >= 1:
                    pe.wait_ge(S["co_read"], qb)
                for g in range(KVG):
                    last = mm(bank[5][:, g * 256:(g + 1) * 256], pct[:, qb % 2, g, :], vbd[:, g, :, :].rearrange("p h d -> p (h d)"),
                              start=True, stop=True)
                last.then_inc(S["co_mm"], 1)

            for i in range(8, CM_PROJ):
                proj(i)
                qb, part = divmod(i - CMP_AT, 3)
                if 0 <= qb < TB:
                    (cmp_scores, cmp_turn, cmp_values)[part](qb)
            pe.wait_ge(S["ld_poolw"], 16)
            pe.wait_ge(S["co_read"], TB)
            for g in range(4):
                pe.wait_ge(S["pool_out"], g + 1)
                mm(bank[2 + g][:, :], poolw[:, g, :], poolT[:, g, :], start=True, stop=True).then_inc(S["pool_mm"], 1)

            def scores(u):
                br, qb, h = units[u]
                g, i = divmod(h, HPG)
                n = (qb + 1) * P
                if u >= 3:
                    pe.wait_ge(S["sc_max"], u - 2)
                mm(bank[u % 3][:, 0:n], qT[g * DH:(g + 1) * DH, i, qb * P:(qb + 1) * P], kT[br][g * DH:(g + 1) * DH, 0:n],
                   start=True, stop=True).then_inc(S["sc_mm"], 1)

            def turn(u):
                br, qb, h = units[u]
                pe.wait_ge(S["p_done"], u + 1)
                if u >= 2:
                    pe.wait_ge(S["pt_copied"], u - 1)
                for kb in range(qb + 1):
                    last = tr(bank[3 + u % 2][:, kb * P:(kb + 1) * P], att_p[u % 3][:, kb * P:(kb + 1) * P], ident)
                last.then_inc(S["p_turned"], 1)

            def values(u):
                br, qb, h = units[u]
                n = br * TB + qb
                pe.wait_ge(S["pt_copied"], u + 1)
                if h == 0 and n >= 2:
                    pe.wait_ge(S["o_read"], n - 1)
                for kb in range(qb + 1):
                    last = mm(bank[5 + n % 2][:, h * DH:(h + 1) * DH], att_pt[u % 3][:, kb, :], vtok[:, kb, br, h // HPG, :],
                              start=(kb == 0), stop=(kb == qb))
                last.then_inc(S["o_mm"], 1)

            def turn_o(qb):
                pe.wait_ge(S["o_acc"], TB + qb + 1)
                if qb >= 2:
                    pe.wait_ge(S["oT_copied"], qb - 1)
                elif qb == 1:
                    pe.wait_ge(S["o_read"], 2 * TB)
                for ct in range(4):
                    last = tr(bank[7 - qb % 2][:, ct * P:(ct + 1) * P], oacc[:, qb, 2 * ct:2 * ct + 2, :].rearrange("p h d -> p (h d)"), ident)
                last.then_inc(S["o_turned"], 1)

            def z_product(m):
                n, k = divmod(m, KT)
                half, b = divmod(n, TB)
                if k == 0:
                    if b == 0:
                        pe.wait_ge(ld_z[half], 16)
                    if n == 0:
                        pe.wait_ge(S["bias_rows"], 2)
                    else:
                        pe.wait_ge(S["z_out"], n)
                last = mm(bank[7][:, :], hT[:, k, b * P:(b + 1) * P], wz[half][:, k, :], start=(k == 0), stop=(k == KT - 1))
                if k == KT - 1:
                    last.then_inc(S["z_mm"], 1)

            pe.wait_ge(S["conv_sum"], 48)
            pe.wait_ge(S["pool_scaled"], 4)

            for u in range(NU + 3):
                if u < NU:
                    scores(u)
                if 2 <= u < NU + 2:
                    turn(u - 2)
                if u >= 3:
                    values(u - 3)
                if Z_AT <= u < NU:
                    for m in range((u - Z_AT) * 8 * KT // (NU - Z_AT), (u - Z_AT + 1) * 8 * KT // (NU - Z_AT)):
                        z_product(m)
            pe.wait_ge(S["z_out"], 2 * TB)
            for qb in range(TB):
                turn_o(qb)

            for c in range(TB):
                if c >= 2:
                    pe.wait_ge(S["bt_copied"], c - 1)
                if c == 0:
                    pe.wait_ge(S["conv_done"], 16)
                for g in range(SG):
                    last = tr(bank[c % 2][:, g * P:(g + 1) * P], bcT[:, g, c * P:(c + 1) * P], ident)
                last.then_inc(S["bt_turned"], 1)
            for n in range(2 * TB):
                c, half = divmod(n, 2)
                if n >= 2:
                    pe.wait_ge(S["xt_copied"], n - 1)
                else:
                    pe.wait_ge(S["sc_max"], NU)
                for i in range(4):
                    last = tr(bank[2 + n % 2][:, i * P:(i + 1) * P], xsT[:, half * 4 + i, c * P:(c + 1) * P], ident)
                last.then_inc(S["xt_turned"], 1)
            pe.wait_ge(S["decay_a"], 1)
            a_all = dta.rearrange("p c h -> p (c h)")
            mm(bank[4][:, 0:64], tri, a_all, start=True, stop=True)
            mm(bank[4][:, 64:128], ones, a_all, start=True, stop=True).then_inc(S["acs_mm"], 1)

            def seg(n):
                c, g = groups[n]
                if n >= 2:
                    pe.wait_ge(S["seg_cap"], 4 * (n - 1))
                    pe.wait_ge(S["seg_done"], n - 1)
                for e in range(SE):
                    h = g * SE + e
                    mm(bank[n % 2][:, e * P:(e + 1) * P], dta[:, c, h:h + 1].to_broadcast([P, P]), tri, start=True, stop=True)
                mm(bank[2 + n % 2][:, 0:P], bcT[:, g, c * P:(c + 1) * P], bcT[:, 4 + g, c * P:(c + 1) * P],
                   start=True, stop=True).then_inc(S["seg_mm"], 1)

            def y_and_state(n):
                c, g = groups[n]
                yb, stb = bank[4 + n % 2], state_bank
                pe.wait_ge(S["seg_done"], n + 1)
                pe.wait_ge(S["xdt_done"], c + 1)
                if n >= 2:
                    pe.wait_ge(S["y_read"], n - 1)
                for e in range(SE):
                    h = g * SE + e
                    last = mm(yb[:, e * SP:(e + 1) * SP], segm[n % 2][:, e, :], xdt[c % 2][:, h * SP:(h + 1) * SP],
                              start=True, stop=True)
                if c > 0:
                    pe.wait_ge(S["st_new"], n - SG + 1)
                    last = mm(yb[:, 256:512], bcT[:, 4 + g, c * P:(c + 1) * P], hst[:, g, :], start=True, stop=True)
                last.then_inc(S["y_mm"], 1)
                if c < TB - 1:
                    pe.wait_ge(S["xdd_done"], c + 1)
                    if n >= 1:
                        pe.wait_ge(S["st_new"], n)
                    mm(stb, btok[:, c, g, :], xdd[:, g * 256:(g + 1) * 256], start=True, stop=True).then_inc(S["st_mm"], 1)

            pe.wait_ge(S["bt_copied"], TB)
            pe.wait_ge(S["xt_copied"], 2 * TB)
            pe.wait_ge(S["acs_neg"], 1)
            pe.wait_ge(S["oT_copied"], TB)

            def early_gates(first, last):
                for m in range(first, min(last, 3 * EARLY * KT)):
                    i, k = divmod(m, KT)
                    if k == 0:
                        t = CM_PROJ + i
                        pe.wait_ge(ld_ring[t % SLOTS], 16 * (t // SLOTS + 1))
                        if 0 < i < EARLY_IN_SSD:
                            pe.wait_ge(S["early_out"], i)
                        if i >= EARLY_IN_SSD:
                            pe.wait_ge(S["seg_cap"], 64)
                    last_mm = mm(early_bank(i)[:, :], ring[:, (CM_PROJ + i) % SLOTS, k, :], hT[:, k, :], start=(k == 0), stop=(k == KT - 1))
                    if k == KT - 1:
                        last_mm.then_inc(S["proj_done"], 1)

            seg(0)
            for n in range(16):
                if n + 1 < 16:
                    seg(n + 1)
                if n < 2 * EARLY_IN_SSD:
                    early_gates(4 * n, 4 * n + 4)
                y_and_state(n)

            def turn_y(n):
                c, half = Y_TURNS[n]
                pe.wait_ge(S["y_norm"], c + 1)
                if n >= 2:
                    pe.wait_ge(S["yT_low"], n - 1)
                else:
                    pe.wait_ge(S["early_out"], EARLY_IN_SSD)
                for i in range(4):
                    k = half * 4 + i
                    last = tr(bank[6 + n % 2][:, i * P:(i + 1) * P], ytok[:, c, k * P:(k + 1) * P], ident)
                last.then_inc(S["y_turned"], 1)

            def product(out_bank, s, first_k, hi, lo, n, sem):
                for k in range(n):
                    last = split_mm(out_bank[:, :], ring_hi[s][:, first_k + k, :], ring_lo[:, s, first_k + k, :], hi[:, k, :], lo[:, k, :],
                                    start=(k == 0), stop=(k == n - 1))
                last.then_inc(S[sem], 1)

            m = EARLY_IN_SSD * KT
            for n, count in ((0, 6), (1, 0), (2, 5), (3, 0), (4, 5)):
                early_gates(m, m + count)
                m += count
                turn_y(n)
            pe.wait_ge(S["y_read"], 16)
            pe.wait_ge(S["gp_lo"], 8)
            pe.wait_ge(S["hi_done"], PEELED[0][2])
            pe.wait_ge(S["tile_lo"], PEELED[0][3])
            product(bank[3], PEELED[0][0], 0, pool_hi, pool_lo, 4, "br_mm")
            turn_y(5)
            product(bank[4], PEELED[0][0], 4, o_hi, o_lo, 4, "br_mm")
            turn_y(6)
            turn_y(7)

            def tile_split(j, t, gates):
                if gates:
                    pe.wait_ge(S["hi_done"], j * BR_TILES + (LOOP_HI - BR_TILES * EARLY + t))
                    pe.wait_ge(S["tile_lo"], j * BR_TILES + (LOOP_LO - BR_TILES * EARLY + t))
                    return t
                slot, _, hi, lo = PEELED[2 * j + t - 3]
                pe.wait_ge(S["hi_done"], hi)
                pe.wait_ge(S["tile_lo"], lo)
                return slot

            def branch(j, first, gates):
                if gates:
                    for s in range(3):
                        tile_split(j, s, gates)
                        pe.wait_ge(S["gate_sig"], j * 3)
                        product(bank[s], s, 0, h_hi, h_lo, KT, "gate_mm")
                if not first:
                    s = tile_split(j, 3, gates)
                    pe.wait_ge(S["br_used"], j * 3)
                    product(bank[3], s, 0, pool_hi, pool_lo, 4, "br_mm")
                    product(bank[4], s, 4, o_hi, o_lo, 4, "br_mm")
                s = tile_split(j, 4, gates)
                product(bank[5], s, 0, y_hi, y_lo, KT, "br_mm")

            pe.wait_ge(S["yT_done"], 2 * TB)
            pe.wait_ge(S["yT_low"], 2 * TB)
            for j in range(EARLY):
                branch(j, j == 0, False)
            pe.wait_ge(S["gp_lo"], 8 + KT)
            with pe.Fori(EARLY, KT) as j:
                branch(j, False, True)

            pe.wait_ge(S["gp_lo"], 8 + 2 * KT)
            pe.wait_ge(S["ld_wo"], 32)
            pe.wait_ge(S["mT_done"], KT)
            def turn_h1(b):
                for half in range(2):
                    pe.wait_ge(S["h1_half"], 2 * b + half + 1)
                    if b > 0:
                        pe.wait_ge(S[("h1T_act", "h1T_dve")[half]], b)
                    for k in range(4):
                        c = half * 512 + k * P
                        last = tr(bank[2 + half][:, k * P:(k + 1) * P], n1[:, b, c:c + P], ident)
                    last.then_inc(S["h1_turned"], 1)

            def route(b):
                pe.wait_ge(S["h1T_act"], b + 1)
                pe.wait_ge(S["h1T_dve"], b + 1)
                if b == 0:
                    pe.wait_ge(S["ld_ln1"], 48)
                for k in range(KT):
                    last = mm(bank[4][:, b * NE:(b + 1) * NE], h1T[:, k, b * P:(b + 1) * P], wrt[:, k, :], start=(k == 0), stop=(k == KT - 1))
                if b == TB - 1:
                    last.then_inc(S["rt_mm"], 1)

            for b in range(TB):
                if b >= 2:
                    pe.wait_ge(S["h1_norm"], 2 * b - 2)
                for half in range(2):
                    acc = bank[(6, 0)[b % 2] + half]
                    for k in range(KT):
                        last = mm(acc[:, :], mT[:, k, b * P:(b + 1) * P], wo[:, half, k, :], start=(k == 0), stop=(k == KT - 1))
                        if k < 4:
                            mm(acc[:, k * P:(k + 1) * P], hT[:, half * 4 + k, b * P:(b + 1) * P], aident, start=False, stop=False)
                last.then_inc(S["mix_mm"], 1)
                if b >= 1:
                    turn_h1(b - 1)
                if b >= 2:
                    route(b - 2)
            route(TB - 2)
            turn_h1(TB - 1)
            route(TB - 1)

            pe.wait_ge(S["sel_done"], 1)
            flat_sel = sel_zeros.rearrange("p b e -> p (b e)")
            for back in range(1, TB):
                mm(bank[1][:, 0:TB * NE], ones, flat_sel[:, (TB - 1 - back) * NE:(2 * TB - 1 - back) * NE], start=(back == 1), stop=False)
            mm(bank[1][:, 0:TB * NE], tri, flat_sel[:, (TB - 1) * NE:], start=False, stop=True)
            mm(bank[1][:, 64:128], ones, flat_sel[:, (TB - 1) * NE:], start=True, stop=True).then_inc(S["pos_mm"], 1)

            def turn_tokens(k, buf, load, first=False):
                pe.wait_ge(ld_xg[buf], load * 16)
                if not first:
                    pe.wait_ge(S["xT_act"], k)
                    pe.wait_ge(S["xT_dve"], k)
                for c in range(KT):
                    last = tr(bank[2 + c // 4][:, (c % 4) * P:(c % 4 + 1) * P], xg[buf][:, c * P:(c + 1) * P], ident)
                    if c % 4 == 3:
                        last.then_inc(S["x_turned"], 1)

            def up_products(k, slot, load, first=False):
                pe.wait_ge(S["xT_act"], k + 1)
                pe.wait_ge(S["xT_dve"], k + 1)
                pe.wait_ge(ld_w13[slot], load * 32)
                if not first:
                    pe.wait_ge(S["hid_done"], k)
                for m in range(2):
                    for c in range(KT):
                        last = mm(bank[m][:, :], xgT[:, c, :], ew13[slot][:, m, c, :], start=(c == 0), stop=(c == KT - 1))
                    last.then_inc(S["up_mm"], 1)

            def turn_hidden(k, first=False):
                pe.wait_ge(S["hid_done"], k + 1)
                if not first:
                    pe.wait_ge(S["hidT_done"], k * 2)
                for f in range(FT):
                    last = tr(bank[4][:, f * P:(f + 1) * P], hidv[:, f * P:(f + 1) * P], ident)
                last.then_inc(S["h_turned"], 1)

            def down_products(k, slot, load, first=False):
                pe.wait_ge(S["hidT_done"], k * 2 + 2)
                if not first:
                    pe.wait_ge(S["out_act"], k)
                    pe.wait_ge(S["out_dve"], k)
                for u in range(2 * FT):
                    f, half = divmod(u, 2)
                    pe.wait_ge(S["hi_done"], k * 8 + (HI_EXP + u + 1))
                    pe.wait_ge(S["tile_lo"], k * 8 + (LO_EXP + u + 1))
                    split_mm(bank[5 + half][:, :], hidT_hi[:, f, :], hidT_lo[:, f, :], w2_hi[(8 * slot + u) % 3],
                             w2_lo[slot][:, f, half * 512:(half + 1) * 512], start=(f == 0), stop=(f == FT - 1)).then_inc(S["dn_mm"], 1)

            def step(e, slot, load, load_next, load_prev, first=False, second=False, last=False):
                if not first:
                    turn_hidden(e - 1, first=second)
                up_products(e, slot, load, first=first)
                if not last:
                    turn_tokens(e + 1, (slot + 1) % 3, load_next)
                if not first:
                    down_products(e - 1, (slot + 2) % 3, load_prev, first=second)

            turn_tokens(0, 0, 1, first=True)
            step(0, 0, 1, 1, 0, first=True)
            step(1, 1, 1, 1, 1, second=True)
            step(2, 2, 1, 2, 1)
            step(3, 0, 2, 2, 1)
            with pe.Fori(1, (NE - 1) // 3 - 1) as i:
                step(i * 3 + 1, 1, i + 1, i + 1, i + 1)
                step(i * 3 + 2, 2, i + 1, i + 2, i + 1)
                step(i * 3 + 3, 0, i + 2, i + 2, i + 1)
            n = (NE - 1) // 3 - 1
            step(n * 3 + 1, 1, n + 1, n + 1, n + 1)
            step(n * 3 + 2, 2, n + 1, n + 2, n + 1)
            step(n * 3 + 3, 0, n + 2, n + 2, n + 1, last=True)
            turn_hidden(NE - 1)
            down_products(NE - 1, 0, n + 2)
            n_spare = pe.value_load(spare_info[0:1, SPARE:SPARE + 1], min_val=0, max_val=SPARE)
            with pe.Fori(0, SPARE) as i:
                with pe.If(i < n_spare):
                    turn_tokens(i + NE, 0, i + n + 3)
                    up_products(i + NE, 0, i + n + 3)
                    turn_hidden(i + NE)
                    down_products(i + NE, 0, i + n + 3)

        @block.scalar
        def _(act):
            ac = nc.scalar.activation
            act.wait_ge(S["ln_stat"], 1)
            ac(sdev, mv[:, :, 1], ACT.Sqrt).then_inc(S["ln_sd"], 1)

            def turned_to(dst, base, g0, b0):
                for k in range(0, KT, 2):
                    act.wait_ge(S["ln_turned"], base + k + 1)
                    ac(dst[:, k, :], bank[k][:, :], ACT.Identity, scale=colv[:, g0 + k:g0 + k + 1],
                       bias=colv[:, b0 + k:b0 + k + 1]).then_inc(S["hT_act"], 1)

            act.wait_ge(S["ld_const"], 16 * NCONST)
            turned_to(hT, 0, C_LN0G, C_LN0B)
            act.wait_ge(S["ln_turned"], KT)
            for k in range(KT):
                if k % 2:
                    act.wait_ge(S["hT_dve"], k // 2 + 1)
                else:
                    act.wait_ge(S["hT_act"], k // 2 + 1)
                ac(h_hi[:, k, :], hT[:, k, :], ACT.Copy).then_inc(S["hi_done"], 1)

            def proj_high(i):
                act.wait_ge(ld_ring[i % SLOTS], 16 * (i // SLOTS + 1))
                if i >= SPLIT_AT + 4:
                    act.wait_ge(S["proj_done"], i - 3)
                ac(proj_hi[i % 4], ring[:, i % SLOTS, :, :], ACT.Copy).then_inc(S["hi_done"], 1)

            proj_high(2)
            proj_high(3)
            for i in (2, 3):
                act.wait_ge(S["proj_done"], i + 1)
                ac(kT[i - 2], bank[i % 2][:, :], ACT.Copy).then_inc(S["act_freed"], 1)
                proj_high(i + 2)
            for i in range(4, 8):
                act.wait_ge(S["proj_done"], i + 1)
                ac(qT[:, i - 4, :], bank[i % 2][:, :], ACT.Copy, scale=DH ** -0.5).then_inc(S["act_freed"], 1)
                proj_high(i + 2)
            for kv in range(2):
                act.wait_ge(S["cmp_mm"], kv + 1)
                ac(hidc[:, kv], bank[2 + kv][:, 0:KVG * NCMP].rearrange("p (g n) -> p g n", g=KVG),
                   ACT.Gelu_apprx_tanh).then_inc(S["cmp_hid"], 1)
            act.wait_ge(S["cmp2_mm"], 1)
            ac(kcT[:, :], bank[4][:, 0:NCMP], ACT.Copy).then_inc(S["cmp_kc"], 1)
            proj_high(10)
            for g in range(4):
                i = 8 + g
                act.wait_ge(S["proj_done"], i + 1)
                if g >= 1:
                    act.wait_ge(S["pool_out"], g)
                else:
                    act.wait_ge(S["zeroed"], 3)
                ac(praw[:, 16:], bank[i % 2][:, :], ACT.Copy).then_inc(S["act_freed"], 1)
                proj_high(i + 3)

            def conv_out(i):
                act.wait_ge(S["conv_sum"], 3 * (i + 1))
                dst = xsT[:, i, :] if i < 8 else bcT[:, i - 8, :]
                ac(dst, dst, ACT.Silu).then_inc(S["conv_done"], 1)

            act.wait_ge(S["soft_abs"], 1)
            ac(dte, dtm, ACT.Exp, scale=-1.0).then_inc(S["soft_ln"], 1)
            act.wait_ge(S["soft_ln"], 1)
            ac(dte, dte, ACT.Ln, bias=1.0).then_inc(S["soft_ln"], 1)
            ac(expa, rowv[:, R_ALOG:R_ALOG + SH], ACT.Exp).then_inc(S["soft_ln"], 1)
            ac(ngate, ngate, ACT.Exp, scale=-1.0).then_inc(S["gates_e"], 1)

            for i in range(16):
                dst = xsT[:, i, :] if i < 8 else bcT[:, i - 8, :]
                qb, part = divmod(12 + i - CMP_AT, 3)
                if 0 <= qb < TB and part == 1:
                    act.wait_ge(S["cs_sub"], qb + 1)
                    v = pcs[:, qb, :, 0:nvalid[qb]]
                    ac(v, v, ACT.Exp).then_inc(S["cs_exp"], 1)
                if i == 0:
                    act.wait_ge(S["vd_mm"], TB)
                if i == 8:
                    act.wait_ge(S["cmp_mm"], 2)
                act.wait_ge(S["proj_done"], 12 + i + 1)
                ac(dst, proj_bank(12 + i)[:, :], ACT.Identity, scale=colv[:, C_CW + 48 + i:C_CW + 49 + i],
                   bias=colv[:, C_CB + i:C_CB + i + 1]).then_inc(S["conv_first"], 1)
                if 12 + i + 3 < CM_PROJ:
                    proj_high(12 + i + 3)
                if i >= 1:
                    conv_out(i - 1)
            conv_out(15)
            for u, (br, qb, h) in enumerate(units):
                n = (qb + 1) * P
                act.wait_ge(S["sc_max"], u + 1)
                if u >= 3:
                    act.wait_ge(S["p_turned"], u - 2)
                ac(att_p[u % 3][:, 0:n], att_s[u % 3][:, 0:n], ACT.Exp, scale=-1.0, bias=nmax[:, br, qb, h:h + 1],
                   accum_out=psums[:, br, qb, h:h + 1]).then_inc(S["p_done"], 1)
                done = (u - Z_AT + 1) * 8 // (NU - Z_AT)
                if u >= Z_AT and done > (u - Z_AT) * 8 // (NU - Z_AT):
                    half, b = divmod(done - 1, TB)
                    act.wait_ge(S["z_mm"], done)
                    ac(zs[:, b, half * 512:(half + 1) * 512], bank[7][:, :], ACT.Copy).then_inc(S["z_out"], 1)
            act.wait_ge(S["zeroed_x"], 16 * (NE + 2 * SPARE))
            for qb in range(TB):
                act.wait_ge(S["o_turned"], qb + 1)
                ac(oT[:, :, qb * P:(qb + 1) * P], bank[7 - qb % 2][:, :].rearrange("p (a b) -> p a b", a=4), ACT.Copy).then_inc(S["oT_copied"], 1)
            for n in range(2 * TB):
                c, half = divmod(n, 2)
                act.wait_ge(S["xt_turned"], n + 1)
                ac(ytok[:, c, half * 512:(half + 1) * 512], bank[2 + n % 2][:, :], ACT.Copy).then_inc(S["xt_copied"], 1)
            act.wait_ge(S["acs_neg"], 3)
            for dst, src in ((eacs, acs), (decin, decin), (cdec, cdec)):
                ac(dst, src, ACT.Exp).then_inc(S["acs_exp"], 1)
            def squares(c):
                act.wait_ge(S["y_gated"], c + 1)
                for g in range(SG):
                    if c + g > 0:
                        act.wait_ge(S["y_sq"], c * SG + g)
                    ac(r_qkv[:, 0:256], ytok[:, c, g * 256:(g + 1) * 256], ACT.Square, accum_out=yss[:, c, g:g + 1]).then_inc(S["y_sq"], 1)

            def y_out(n):
                c, half = Y_TURNS[n]
                act.wait_ge(S["y_turned"], n + 1)
                for i in range(4):
                    k = half * 4 + i
                    last = ac(y_hi[:, k, c * P:(c + 1) * P], bank[6 + n % 2][:, i * P:(i + 1) * P], ACT.Copy, scale=colv[:, C_NG + k:C_NG + k + 1])
                last.then_inc(S["yT_done"], 1)

            def early_out(i):
                act.wait_ge(S["proj_done"], CM_PROJ + i + 1)
                ac(early[i], early_bank(i)[:, :], ACT.Copy).then_inc(S["early_out"], 1)

            for n in range(16):
                act.wait_ge(S["seg_cap"], 4 * (n + 1))
                ac(segd[n % 2], segd[n % 2], ACT.Exp).then_inc(S["seg_exp"], 1)
                if n % 2 == 0 and n >= 2:
                    early_out(n // 2 - 1)
                if n == 1:
                    act.wait_ge(S["z_out"], 2 * TB)
                    for b in range(TB):
                        ac(zs[:, b, :], zs[:, b, :], ACT.Silu).then_inc(S["z_silu"], 1)
                if n in (5, 9, 13):
                    squares((n - 5) // 4)
                if 4 <= n < 12:
                    dst, src = ((pool_hi, poolT), (o_hi, oT))[(n - 4) // 4]
                    ac(dst[:, n % 4, :], src[:, n % 4, :], ACT.Copy).then_inc(S["hi_done"], 1)

            def tile_high(s, load):
                act.wait_ge(ld_ring[s], load * 16)
                ac(ring_hi[s], ring[:, s, :, :], ACT.Copy).then_inc(S["hi_done"], 1)

            def peeled_high(q):
                slot, load, hi, lo = PEELED[q]
                tile_high(slot, loads[slot] + load)

            act.wait_ge(S["y_ms"], 1)
            ac(yrt[:, 0:3], yrt[:, 0:3], ACT.Sqrt).then_inc(S["y_sd"], 1)
            act.wait_ge(S["y_mm"], 16)
            peeled_high(0)
            peeled_high(1)
            for n in range(3):
                y_out(n)
            squares(3)
            y_out(3)
            early_out(7)
            y_out(4)
            early_out(8)
            y_out(5)
            act.wait_ge(S["y_ms"], 2)
            ac(yrt[:, 3], yrt[:, 3], ACT.Sqrt).then_inc(S["y_sd"], 1)
            for n in range(6, 8):
                y_out(n)
            for q in (2, 3, 4):
                peeled_high(q)

            act.wait_ge(S["early_out"], 3 * EARLY)
            for j in range(EARLY):
                for s in range(3):
                    if j > 0:
                        act.wait_ge(S["br_used"], j * 3)
                    else:
                        act.wait_ge(S["y_norm"], TB)
                    ac(gsb[s], early[j * 3 + s], ACT.Sigmoid).then_inc(S["gate_sig"], 1)
                if j == 0:
                    for k in range(KT):
                        ac(h_hi[:, k, :], hT[:, k, :], ACT.Copy).then_inc(S["hi_done"], 1)
                    peeled_high(5)
                elif j == 1:
                    tile_high(0, loads[0] + AGAIN[0] + 1)
            for s in range(1, BR_TILES):
                tile_high(s, loads[s] + AGAIN[s] + 1)

            def gate(j, s):
                act.wait_ge(S["gate_mm"], j * 3 + (s + 1 - 3 * EARLY))
                act.wait_ge(S["br_used"], j * 3)
                ac(gsb[s], bank[s][:, :], ACT.Sigmoid).then_inc(S["gate_sig"], 1)

            with act.Fori(EARLY, KT - 1) as j:
                gate(j, 0)
                gate(j, 1)
                tile_high(0, j + (loads[0] + AGAIN[0] + 2 - EARLY))
                gate(j, 2)
                for s in range(1, BR_TILES):
                    tile_high(s, j + (loads[s] + AGAIN[s] + 2 - EARLY))
            for s in range(3):
                gate(KT - 1, s)
            act.wait_ge(S["mT_done"], KT)
            for b in range(TB):
                act.wait_ge(S["ln_stat"], b + 2)
                ac(sdev[:, b:b + 1], sdev[:, b:b + 1], ACT.Sqrt).then_inc(S["ln_sd"], 1)
                act.wait_ge(S["ln_rstd"], b + 1)
                for half in range(2):
                    ac(n1[:, b, half * 512:(half + 1) * 512], bank[(6, 0)[b % 2] + half][:, :], ACT.Identity,
                              scale=rstd[:, b:b + 1], bias=shift[:, b:b + 1]).then_inc(S["h1_norm"], 1)
                act.wait_ge(S["h1_turned"], 2 * b + 1)
                ac(h1T[:, 0:4, b * P:(b + 1) * P], bank[2][:, :].rearrange("p (k t) -> p k t", k=4), ACT.Copy).then_inc(S["h1T_act"], 1)
            act.wait_ge(S["rt_max"], 1)
            ac(lg, lg, ACT.Exp).then_inc(S["rt_exp"], 1)

            def tokens_out(k, first=False):
                act.wait_ge(S["x_turned"], k * 2 + 1)
                if not first:
                    act.wait_ge(S["up_mm"], k * 2)
                ac(xgT[:, 0:4, :].rearrange("p k t -> p (k t)"), bank[2][:, :], ACT.Copy).then_inc(S["xT_act"], 1)

            def silu(k, first=False):
                act.wait_ge(S["up_mm"], k * 2 + 1)
                if not first:
                    act.wait_ge(S["hid_done"], k)
                ac(upv, bank[0][:, :], ACT.Silu).then_inc(S["up_silu"], 1)

            def out_half(k, first=False):
                act.wait_ge(S["dn_mm"], k * 8 + 7)
                if not first:
                    act.wait_ge(S["st_y"], k * 16)
                ac(eout[:, 0:512], bank[5][:, :], ACT.Copy).then_inc(S["out_act"], 1)

            def w2_high(k, slot, load, units):
                act.wait_ge(ld_w2[slot], load * 16)
                for u in units:
                    if not (isinstance(k, int) and k == 0 and u < 3):
                        act.wait_ge(S["dn_mm"], k * 8 + (u - 2))
                    f, half = divmod(u, 2)
                    ac(w2_hi[(8 * slot + u) % 3], ew2[slot][:, f, half * 512:(half + 1) * 512], ACT.Copy).then_inc(S["hi_done"], 1)

            def step(e, slot, load, last=False):
                w2_high(e - 1, slot, load, range(3))
                silu(e)
                if not last:
                    tokens_out(e + 1)
                w2_high(e - 1, slot, load, range(3, 8))
                out_half(e - 1, first=isinstance(e, int) and e == 1)

            tokens_out(0, first=True)
            silu(0, first=True)
            tokens_out(1)
            act.wait_ge(S["slots_done"], 3)
            for d in (1, 2, 3):
                step(d, d - 1, 1)
            with act.Fori(1, (NE - 1) // 3 - 1) as i:
                for d in (1, 2, 3):
                    step(i * 3 + d, d - 1, i + 1)
            n = (NE - 1) // 3 - 1
            for d in (1, 2, 3):
                step(n * 3 + d, d - 1, n + 1, last=(d == 3))
            w2_high(NE - 1, 0, n + 2, range(8))
            out_half(NE - 1)
            n_spare = act.value_load(spare_info[0:1, SPARE:SPARE + 1], min_val=0, max_val=SPARE)
            with act.Fori(0, SPARE) as i:
                with act.If(i < n_spare):
                    tokens_out(i + NE)
                    silu(i + NE)
                    act.wait_ge(S["dn_mm"], (i + NE) * 8)
                    w2_high(i + NE, 0, i + n + 3, range(8))
                    out_half(i + NE)

            def normalise(b):
                act.wait_ge(S["ln_stat"], TB + 2 + b)
                ac(sdev[:, b:b + 1], sdev[:, b:b + 1], ACT.Sqrt).then_inc(S["ln_sd"], 1)
                act.wait_ge(S["ln_rstd"], TB + 1 + b)
                ac(n1[:, b, :], n1[:, b, :], ACT.Identity, scale=rstd[:, b:b + 1], bias=shift[:, b:b + 1]).then_inc(S["ln2_norm"], 1)

            act.wait_ge(S["slots_done"], 3)
            for b in range(TB):
                if b < TB - 1:
                    act.wait_ge(ld_back[b], 32)
                    ac(by_token[:, b, 0, :], by_token[:, b, 0, :], ACT.Copy, scale=slot_wt[:, b, 0:1]).then_inc(S["ya_scaled"], 1)
                if b > 0:
                    normalise(b - 1)
            act.wait_ge(S["ln_stat"], 2 * TB + 1)
            ac(sdev[:, TB - 1:], sdev[:, TB - 1:], ACT.Sqrt).then_inc(S["ln_sd"], 1)

        @block.gpsimd
        def _(gp):
            g_ = nc.gpsimd
            g_.memset(praw[:, 0:16], 0.0).then_inc(S["zeroed"], 1)
            g_.memset(pw[0][:, 0:16], 0.0).then_inc(S["zeroed"], 1)
            g_.memset(pw[1][:, 0:16], 0.0).then_inc(S["zeroed"], 1)
            g_.memset(vbd[:, :, :, :], 0.0).then_inc(S["zeroed"], 1)
            g_.memset(zeros, 0.0).then_inc(S["zero_tile"], 1)
            g_.memset(pcs, 0.0).then_inc(S["zeroed"], 1)
            step = 0
            gp.wait_ge(S["zeroed"], 3)
            gp.wait_ge(S["ld_const"], 16 * NCONST)
            for g, w in enumerate(WINDOWS):
                gp.wait_ge(S["act_freed"], 6 + g + 1)
                src, span, flip = praw, 1, 0
                while span < w:
                    dst = pw[flip]
                    g_.tensor_tensor(dst[:, 16:], src[:, 16:], src[:, 16 - span:16 - span + T], ALU.add).then_inc(S["gp"], 1)
                    step += 1
                    gp.wait_ge(S["gp"], step)
                    src, span, flip = dst, span * 2, 1 - flip
                g_.tensor_scalar(pr[:, 16:], src[:, 32:], 1.0 / w, None, ALU.mult).then_inc(S["gp"], 1)
                g_.tensor_tensor(pr[:, 0:16], src[:, 16:32], invc[:, g, :], ALU.mult).then_inc(S["gp"], 1)
                step += 2
                gp.wait_ge(S["gp"], step)
                g_.tensor_tensor(poolT[:, g, :], pr, praw[:, 16:], ALU.subtract).then_inc(S["pool_out"], 1)
                gp.wait_ge(S["pool_out"], g + 1)
            for c in range(TB):
                gp.wait_ge(S["xdt_done"], c + 1)
                if c < TB - 1:
                    if c >= 1:
                        gp.wait_ge(S["st_mm"], SG * c)
                    g_.tensor_tensor(xdd.rearrange("p (h d) -> p h d", h=SH), xdt[c % 2].rearrange("p (h d) -> p h d", h=SH),
                                     decin[:, c, :].unsqueeze(2).broadcast_to([P, SH, SP]), ALU.mult).then_inc(S["xdd_done"], 1)
                if c >= 1:
                    gp.wait_ge(S["y_gated"], c)
                g_.tensor_tensor(xsd.rearrange("p (h d) -> p h d", h=SH), ytok[:, c, :].rearrange("p (h d) -> p h d", h=SH),
                                 rowv[:, R_DSK:R_DSK + SH].unsqueeze(2).broadcast_to([P, SH, SP]), ALU.mult).then_inc(S["xsd_done"], 1)

            for i in range(8):
                hi, lo, src = ((pool_hi, pool_lo, poolT), (o_hi, o_lo, oT))[i // 4]
                gp.wait_ge(S["hi_done"], HI0 + i + 1)
                g_.tensor_tensor(lo[:, i % 4, :], src[:, i % 4, :], hi[:, i % 4, :], ALU.subtract).then_inc(S["gp_lo"], 1)
            for k in range(KT):
                gp.wait_ge(S["hi_done"], HI0 + 14 + k)
                g_.tensor_tensor(h_lo[:, k, :], hT[:, k, :], h_hi[:, k, :], ALU.subtract).then_inc(S["gp_lo"], 1)
            gp.wait_ge(S["gate_mm"], 3 * (KT - EARLY))
            for k in range(KT):
                gp.wait_ge(S["gp_lo"], 8 + KT)
                g_.tensor_tensor(hT[:, k, :], h_lo[:, k, :], h_hi[:, k, :], ALU.add).then_inc(S["gp_lo"], 1)

            gp.wait_ge(S["h1_half"], 2 * TB)
            gp.wait_ge(S["slots_done"], 1)
            gp.wait_ge(S["zeroed_x"], 16 * (NE + 2 * SPARE))
            for b in range(TB):
                for k in range(2):
                    g_.indirect_dma_start(xs_dram, bass.IndirectOffsetOnAxis(ap=slot_no[:, b, k:k + 1], axis=0),
                                          n1[:, b, :], None).then_inc(S["st_h"], 16)
            gp.wait_ge(S["slots_done"], 2)
            n_spare = gp.value_load(spare_info[0:1, SPARE:SPARE + 1], min_val=0, max_val=SPARE)
            gp.wait_ge(S["st_h"], 16 * 2 * TB)
            for b in range(TB):
                g_.tensor_scalar(n1[:, b, :], n1[:, b, :], ALPHA, None, ALU.mult).then_inc(S["h_scaled"], 1)

            def store(k):
                gp.wait_ge(S["out_act"], k + 1)
                gp.wait_ge(S["out_dve"], k + 1)
                g_.dma_start(ys_dram[bass.ds(k * P, P), :], eout).then_inc(S["st_y"], 16)
                gp.wait_ge(S["st_y"], k * 16 + 16)

            with gp.Fori(0, NE) as k:
                store(k)
            with gp.If(0 < n_spare):
                with gp.Fori(0, SPARE) as i:
                    with gp.If(i < n_spare):
                        store(i + NE)
            for b in range(TB):
                for k in range(2):
                    g_.indirect_dma_start(by_token[:, b, k, :], None, ys_dram,
                                          bass.IndirectOffsetOnAxis(ap=slot_no[:, b, k:k + 1], axis=0)).then_inc(ld_back[b], 16)

            def add_first(b):
                gp.wait_ge(S["h_scaled"], b + 1)
                gp.wait_ge(S["ya_scaled"], b + 1)
                g_.tensor_tensor(n1[:, b, :], n1[:, b, :], by_token[:, b, 0, :], ALU.add).then_inc(S["ya_added"], 1)

            def add_bias(b):
                gp.wait_ge(S["ln2_g"], b + 1)
                g_.tensor_tensor(obuf[:, b, :], n1[:, b, :], lnr2[:, 1, :], ALU.add).then_inc(S["ln2_out"], 1)

            for b in range(TB - 1):
                add_first(b)
            for b in range(TB - 1):
                add_bias(b)

        @block.vector
        def _(dve):
            v = nc.vector
            chain = [0]

            def then(ins):
                chain[0] += 1
                ins.then_inc(S["dv"], 1)
                dve.wait_ge(S["dv"], chain[0])

            def stats_of(b, halves):
                for i, half in enumerate(halves):
                    last = v.bn_stats(stats[:, b, i, :], half)
                then(last)
                return v.bn_aggr(mv[:, b, :], stats[:, b].rearrange("p a s -> p (a s)"))

            def add_eps():
                then(v.tensor_scalar(rstd, mv[:, :, 1], LN_EPS, None, ALU.add))
                v.tensor_copy(mv[:, :, 1], rstd).then_inc(S["ln_stat"], 1)

            for b in range(TB):
                dve.wait_ge(ld_x[b], 16)
                then(stats_of(b, [xin[:, b, 0:512], xin[:, b, 512:1024]]))
            add_eps()
            dve.wait_ge(S["ln_sd"], 1)
            then(v.reciprocal(rstd, sdev))
            for b in range(TB):
                v.tensor_scalar(xnorm[:, b, :], xin[:, b, :], mv[:, b, 0:1], rstd[:, b:b + 1], ALU.subtract, ALU.mult).then_inc(S["ln_norm"], 1)

            def turned_to(dst, base, g0, b0):
                for k in range(1, KT, 2):
                    dve.wait_ge(S["ln_turned"], base + k + 1)
                    v.tensor_scalar(dst[:, k, :], bank[k][:, :], colv[:, g0 + k:g0 + k + 1], colv[:, b0 + k:b0 + k + 1],
                                    ALU.mult, ALU.add).then_inc(S["hT_dve"], 1)

            dve.wait_ge(S["ld_const"], 16 * NCONST)
            turned_to(hT, 0, C_LN0G, C_LN0B)
            for k in range(KT):
                dve.wait_ge(S["hi_done"], k + 1)
                v.tensor_tensor(proj_h_lo[:, k, :], hT[:, k, :], h_hi[:, k, :], ALU.subtract).then_inc(S["tile_lo"], 1)

            def proj_low(i):
                dve.wait_ge(S["hi_done"], KT + i - SPLIT_AT + 1)
                v.tensor_tensor(ring_lo[:, i % SLOTS, :, :], ring[:, i % SLOTS, :, :], proj_hi[i % 4], ALU.subtract).then_inc(S["tile_lo"], 1)

            proj_low(2)
            for kv in range(2):
                dve.wait_ge(S["proj_done"], kv + 1)
                for g in range(KVG):
                    rows_g = bank[kv][g * DH:(g + 1) * DH, :]
                    v.tensor_copy(tok2[0:DH, kv, g, :], rows_g)
                    last = v.tensor_copy(tok2[DH:P, kv, g, 0:T - 1], rows_g[:, 1:T])
                last.then_inc(S["dve_freed"], 1)
                dve.wait_ge(S["dve_freed"], kv + 1)
                rows16 = tok2[:, kv].rearrange("p g (n m) -> p g n m", m=CMP_STRIDE)
                for half in range(2):
                    c = (C_PEK, C_PEV)[kv] + half * 8
                    v.tensor_tensor(blocks[:, kv, half * 8:half * 8 + 8].rearrange("p l g n -> p g n l"),
                                    rows16[:, :, half:half + NCMP, 0:CMP_STRIDE:2],
                                    colv[:, c:c + 8].unsqueeze(1).unsqueeze(1).broadcast_to([P, KVG, NCMP, 8]),
                                    ALU.add).then_inc(S["cmp_in"], 1)
                proj_low(3 + kv)
            for i in range(5, 10):
                proj_low(i)
            for i in range(2):
                dve.wait_ge(S["bias_mm"], i + 1)
                v.tensor_copy(bias_sb[:, i * REVN // 2:(i + 1) * REVN // 2], bank[6 + i][0:HEADS, 0:REVN // 2]).then_inc(S["bias_rows"], 1)
            dve.wait_ge(S["cmp2_mm"], 1)
            dve.wait_ge(S["zeroed"], 4)
            for h in range(HPG):
                rows_h = slice(32 * h, 32 * h + NCMP)
                v.tensor_copy(vbd[rows_h, :, h, :], bank[5][rows_h, 0:KVG * DH].rearrange("p (g d) -> p g d", g=KVG)).then_inc(S["cmp_vc"], 1)

            proj_low(10)
            for b in range(TB):
                dve.wait_ge(S["vd_mm"], b + 1)
                v.tensor_copy(vtok[:, b].rearrange("p r g d -> p (r g d)"), bank[2 + b][:, 0:2 * P])
                v.tensor_tensor(dtx[:, b, :], bank[2 + b][:, 2 * P:2 * P + SH], rowv[:, R_DTB:R_DTB + SH], ALU.add)
                v.tensor_copy(ngate[:, b].rearrange("p r h -> p (r h)"), bank[2 + b][:, 2 * P + SH:VD]).then_inc(S["vd_used"], 1)
            for i in range(11, 15):
                proj_low(i)
            dve.wait_ge(S["vd_used"], TB)
            v.scalar_tensor_tensor(out=dtm, in0=dtx, scalar=-1.0, in1=dtx, op0=ALU.mult, op1=ALU.max).then_inc(S["soft_abs"], 1)
            dve.wait_ge(S["soft_ln"], 3)
            then(v.scalar_tensor_tensor(out=dt, in0=dtx, scalar=0.0, in1=dte, op0=ALU.max, op1=ALU.add))
            v.scalar_tensor_tensor(out=dta, in0=dt, scalar=-1.0, in1=expa.unsqueeze(1).broadcast_to([P, TB, SH]),
                                   op0=ALU.mult, op1=ALU.mult).then_inc(S["decay_a"], 1)
            dve.wait_ge(S["gates_e"], 1)
            then(v.tensor_scalar(ngate, ngate, 1.0, None, ALU.add))
            then(v.reciprocal(ngate, ngate))

            def cmp_scores(qb):
                nv = nvalid[qb]
                z0 = T - P - qb * P + CMP_LEN - 1
                if qb == 0:
                    dve.wait_ge(S["ld_strip"], 16)
                    dve.wait_ge(S["zeroed"], 5)
                dve.wait_ge(S["cs_mm"], qb + 1)
                s3 = pcs[:, qb, :, 0:nv]
                for g in range(KVG):
                    hs = slice(g * HPG, (g + 1) * HPG)
                    last = v.tensor_tensor(s3[:, hs, :], bank[2 + g][:, 0:256].rearrange("p (h n) -> p h n", h=HEADS)[:, hs, 0:nv],
                                           strips[:, hs, z0:z0 + CMP_STRIDE * (nv - 1) + 1:CMP_STRIDE], ALU.add)
                then(last)
                then(v.tensor_reduce(cmax[:, qb, :], s3, AX.X, ALU.max))
                v.tensor_tensor(s3, s3, cmax[:, qb, :].unsqueeze(2).broadcast_to([P, HEADS, nv]), ALU.subtract).then_inc(S["cs_sub"], 1)

            def cmp_turn(qb):
                dve.wait_ge(S["cs_exp"], qb + 1)
                then(v.tensor_reduce(csum[:, qb, :], pcs[:, qb, :, 0:nvalid[qb]], AX.X, ALU.add))
                then(v.reciprocal(csum[:, qb, :], csum[:, qb, :]))
                gate = ngate[:, qb, 0, :]
                if qb == 0:
                    then(v.tensor_scalar(gate, gate, rowok, None, ALU.mult))
                then(v.tensor_tensor(ogate[:, 0, qb, :], gate, csum[:, qb, :], ALU.mult))
                dve.wait_ge(S["cs_turned"], qb + 1)
                if qb >= 2:
                    dve.wait_ge(S["co_mm"], qb - 1)
                v.tensor_copy(pct[:, qb % 2].rearrange("p g n -> p (g n)"), bank[4][:, 0:256]).then_inc(S["cs_copied"], 1)

            def cmp_values(qb):
                dve.wait_ge(S["co_mm"], qb + 1)
                v.tensor_tensor(oacc[:, qb], bank[5][:, :].rearrange("p (h d) -> p h d", h=HEADS),
                                ogate[:, 0, qb, :].unsqueeze(2).broadcast_to([P, HEADS, DH]), ALU.mult).then_inc(S["co_read"], 1)

            for i in range(16):
                dst = xsT[:, i, :] if i < 8 else bcT[:, i - 8, :]
                dve.wait_ge(S["conv_first"], i + 1)
                for n, back in enumerate((1, 2, 3)):
                    tap = C_CW + (3 - back) * 16 + i
                    if n:
                        dve.wait_ge(S["conv_sum"], 3 * i + n)
                    v.scalar_tensor_tensor(out=dst[:, back:], in0=proj_bank(12 + i)[:, 0:T - back], scalar=colv[:, tap:tap + 1],
                                           in1=dst[:, back:], op0=ALU.mult, op1=ALU.add).then_inc(S["conv_sum"], 1)
                if 12 + i + 3 < CM_PROJ:
                    proj_low(12 + i + 3)
                qb, part = divmod(12 + i - CMP_AT, 3)
                if 0 <= qb < TB:
                    (cmp_scores, cmp_turn, cmp_values)[part](qb)
            for g in range(4):
                dve.wait_ge(S["pool_mm"], g + 1)
                v.tensor_scalar(poolT[:, g, :], bank[2 + g][:, :], colv[:, C_PS + g:C_PS + g + 1], None, ALU.mult).then_inc(S["pool_scaled"], 1)


            for u in range(NU + 3):
                if u < NU:
                    br, qb, h = units[u]
                    n = (qb + 1) * P
                    dve.wait_ge(S["sc_mm"], u + 1)
                    if u >= 3:
                        dve.wait_ge(S["p_done"], u - 2)
                    v.tensor_tensor_reduce(out=att_s[u % 3][:, 0:n], in0=bank[u % 3][:, 0:n], in1=strips[:, h, T - n:T],
                                           scale=-1.0, scalar=3e38, op0=ALU.add, op1=ALU.min,
                                           accum_out=nmax[:, br, qb, h:h + 1]).then_inc(S["sc_max"], 1)
                if 2 <= u < NU + 2:
                    w = u - 2
                    nb = units[w][1] + 1
                    dve.wait_ge(S["p_turned"], w + 1)
                    if w >= 3:
                        dve.wait_ge(S["o_mm"], w - 2)
                    v.tensor_copy(att_pt[w % 3][:, 0:nb, :].rearrange("p a b -> p (a b)"), bank[3 + w % 2][:, 0:nb * P]).then_inc(S["pt_copied"], 1)
                if u >= 3 and units[u - 3][2] == HEADS - 1:
                    br, qb, _h = units[u - 3]
                    n = br * TB + qb
                    dve.wait_ge(S["p_done"], u - 2)
                    then(v.reciprocal(psums[:, br, qb, :], psums[:, br, qb, :]))
                    then(v.tensor_tensor(ogate[:, 1 + br, qb, :], psums[:, br, qb, :], ngate[:, qb, 1 + br, :], ALU.mult))
                    dve.wait_ge(S["o_mm"], u - 2)
                    v.tensor_tensor(osc, bank[5 + n % 2][:, :].rearrange("p (h d) -> p h d", h=HEADS),
                                    ogate[:, 1 + br, qb, :].unsqueeze(2).broadcast_to([P, HEADS, DH]), ALU.mult).then_inc(S["o_read"], 1)
                    dve.wait_ge(S["o_read"], n + 1)
                    v.tensor_tensor(oacc[:, qb], oacc[:, qb], osc, ALU.add).then_inc(S["o_acc"], 1)

            for c in range(TB):
                dve.wait_ge(S["bt_turned"], c + 1)
                v.tensor_copy(btok[:, c].rearrange("p g n -> p (g n)"), bank[c % 2][:, :]).then_inc(S["bt_copied"], 1)
            dve.wait_ge(S["acs_mm"], 1)
            flat = lambda a: a.rearrange("p c h -> p (c h)")
            then(v.tensor_copy(flat(acs), bank[4][:, 0:64]))
            v.tensor_scalar(negacs, acs, -1.0, None, ALU.mult).then_inc(S["acs_neg"], 1)
            v.tensor_tensor(flat(decin), bank[4][:, 64:128], flat(acs), ALU.subtract).then_inc(S["acs_neg"], 1)
            v.tensor_copy(flat(cdec), bank[4][:, 64:128]).then_inc(S["acs_neg"], 1)

            def caps(n):
                c, g = groups[n]
                dve.wait_ge(S["seg_mm"], n + 1)
                for e in range(SE):
                    v.scalar_tensor_tensor(out=segd[n % 2][:, e, :], in0=bank[n % 2][:, e * P:(e + 1) * P],
                                           scalar=negacs[:, c, g * SE + e:g * SE + e + 1], in1=cap,
                                           op0=ALU.add, op1=ALU.min).then_inc(S["seg_cap"], 1)

            def weigh(n):
                dve.wait_ge(S["seg_exp"], n + 1)
                if n >= 2:
                    dve.wait_ge(S["y_mm"], n - 1)
                v.tensor_tensor(segm[n % 2], segd[n % 2], bank[2 + n % 2][:, 0:P].unsqueeze(1).broadcast_to([P, SE, P]),
                                ALU.mult).then_inc(S["seg_done"], 1)

            def heads_of(a, g):
                return a[:, g * SE:(g + 1) * SE].unsqueeze(2).broadcast_to([P, SE, SP])

            dve.wait_ge(S["o_turned"], TB)
            dve.wait_ge(S["acs_exp"], 3)
            dve.wait_ge(S["acs_neg"], 3)
            caps(0)
            weigh(0)

            def mean_square(part):
                v.tensor_scalar(yrt[:, part], yss[:, part], 1.0 / 256, LN_EPS, ALU.mult, ALU.add).then_inc(S["y_ms"], 1)

            def normalise(part):
                then(v.reciprocal(yrs[:, part], yrt[:, part]))
                for c in range(TB)[part]:
                    y4 = ytok[:, c, :].rearrange("p (g d) -> p g d", g=SG)
                    v.tensor_tensor(y4, y4, yrs[:, c, :].unsqueeze(2).broadcast_to([P, SG, 256]), ALU.mult).then_inc(S["y_norm"], 1)

            h4 = lambda a: a.rearrange("p (h d) -> p h d", h=SE)

            def x_dt(c):
                dve.wait_ge(S["xt_copied"], 2 * (c + 1))
                if c >= 2:
                    dve.wait_ge(S["xdd_done"], c - 1)
                v.tensor_tensor(xdt[c % 2].rearrange("p (h d) -> p h d", h=SH), ytok[:, c, :].rearrange("p (h d) -> p h d", h=SH),
                                dt[:, c, :].unsqueeze(2).broadcast_to([P, SH, SP]), ALU.mult).then_inc(S["xdt_done"], 1)

            def y_and_state(n):
                c, g = groups[n]
                dve.wait_ge(S["y_mm"], n + 1)
                yb = bank[4 + n % 2]
                dve.wait_ge(S["xsd_done"], c + 1)
                dst = h4(ytok[:, c, g * 256:(g + 1) * 256])
                x4 = h4(xsd[:, g * 256:(g + 1) * 256])
                if c > 0:
                    dve.wait_ge(S["y_read"], n)
                    then(v.tensor_tensor(yoff, h4(yb[:, 256:512]), heads_of(eacs[:, c, :], g), ALU.mult))
                    then(v.tensor_tensor(yoff, yoff, x4, ALU.add))
                    v.tensor_tensor(dst, h4(yb[:, 0:256]), yoff, ALU.add).then_inc(S["y_read"], 1)
                else:
                    v.tensor_tensor(dst, h4(yb[:, 0:256]), x4, ALU.add).then_inc(S["y_read"], 1)
                if c < TB - 1:
                    stb, hg = state_bank, h4(hst[:, g, :])
                    dve.wait_ge(S["st_mm"], n + 1)
                    if c == 0:
                        v.tensor_copy(hst[:, g, :], stb).then_inc(S["st_new"], 1)
                    else:
                        then(v.tensor_tensor(hg, hg, heads_of(cdec[:, c, :], g), ALU.mult))
                        v.tensor_tensor(hg, h4(stb), hg, ALU.add).then_inc(S["st_new"], 1)
                if g == SG - 1:
                    dve.wait_ge(S["y_read"], n + 1)
                    dve.wait_ge(S["z_silu"], c + 1)
                    v.tensor_tensor(ytok[:, c, :], ytok[:, c, :], zs[:, c, :], ALU.mult).then_inc(S["y_gated"], 1)

            x_dt(0)
            for n, (c, g) in enumerate(groups):
                if n + 1 < 16:
                    caps(n + 1)
                if n >= 1:
                    y_and_state(n - 1)
                if n == 14:
                    dve.wait_ge(S["y_sq"], 12)
                    mean_square(slice(0, 3))
                if n + 1 < 16:
                    weigh(n + 1)
                if n == 15:
                    dve.wait_ge(S["y_sd"], 1)
                    normalise(slice(0, 3))
                if g == 2 and c + 1 < TB:
                    x_dt(c + 1)
            y_and_state(15)

            def tile_low(s, hi):
                dve.wait_ge(S["hi_done"], hi)
                v.tensor_tensor(ring_lo[:, s, :, :], ring[:, s, :, :], ring_hi[s], ALU.subtract).then_inc(S["tile_lo"], 1)

            def peeled_low(q):
                slot, load, hi, lo = PEELED[q]
                tile_low(slot, hi)

            def y_out(n):
                c, half = Y_TURNS[n]
                dve.wait_ge(S["yT_done"], n + 1)
                for i in range(4):
                    k = half * 4 + i
                    ts = slice(c * P, (c + 1) * P)
                    last = v.scalar_tensor_tensor(out=y_lo[:, k, ts], in0=bank[6 + n % 2][:, i * P:(i + 1) * P], scalar=colv[:, C_NG + k:C_NG + k + 1],
                                                  in1=y_hi[:, k, ts], op0=ALU.mult, op1=ALU.subtract)
                last.then_inc(S["yT_low"], 1)

            peeled_low(0)
            peeled_low(1)
            for n in range(3):
                y_out(n)
            dve.wait_ge(S["y_sq"], 16)
            mean_square(slice(3, 4))
            for n in range(3, 6):
                y_out(n)
            dve.wait_ge(S["y_sd"], 2)
            normalise(slice(3, 4))
            for n in range(6, 8):
                y_out(n)
            for q in (2, 3, 4):
                peeled_low(q)

            def gated(j, first):
                if not first:
                    dve.wait_ge(S["mT_done"], j)
                for s in range(3):
                    dve.wait_ge(S["gate_sig"], j * 3 + (s + 1))
                    dve.wait_ge(S["br_mm"], j * 3 + (s + 1))
                    v.tensor_tensor(gm[s], gsb[s], bank[3 + s][:, :], ALU.mult).then_inc(S["br_used"], 1)
                dve.wait_ge(S["br_used"], j * 3 + 3)
                v.tensor_tensor(gm[0], gm[0], gm[1], ALU.add).then_inc(S["m_add"], 1)
                dve.wait_ge(S["m_add"], j + 1)
                dst = mT[:, j, :] if isinstance(j, int) else mT[:, bass.ds(j, 1), :].rearrange("p a t -> p (a t)")
                v.tensor_tensor(dst, gm[0], gm[2], ALU.add).then_inc(S["mT_done"], 1)

            for j in range(EARLY):
                gated(j, j == 0)
                if j == 0:
                    peeled_low(5)
                elif j == 1:
                    tile_low(0, LOOP_HI)
            for s in range(1, BR_TILES):
                tile_low(s, LOOP_HI + s)
            with dve.Fori(EARLY, KT - 1) as j:
                for s in range(3):
                    tile_low(s, j * BR_TILES + (LOOP_HI + s - BR_TILES * (EARLY - 1)))
                gated(j, False)
                for s in (3, 4):
                    tile_low(s, j * BR_TILES + (LOOP_HI + s - BR_TILES * (EARLY - 1)))
            gated(KT - 1, False)
            def block_norm(n, b, halves):
                then(stats_of(b, halves))
                v.tensor_scalar(sdev[:, b:b + 1], mv[:, b, 1:2], LN_EPS, None, ALU.add).then_inc(S["ln_stat"], 1)
                dve.wait_ge(S["ln_sd"], n + 2)
                then(v.reciprocal(rstd[:, b:b + 1], sdev[:, b:b + 1]))
                v.scalar_tensor_tensor(out=shift[:, b:b + 1], in0=mv[:, b, 0:1], scalar=-1.0, in1=rstd[:, b:b + 1],
                                       op0=ALU.mult, op1=ALU.mult).then_inc(S["ln_rstd"], 1)

            dve.wait_ge(S["ld_ln1"], 48)
            for b in range(TB):
                dve.wait_ge(S["mix_mm"], b + 1)
                block_norm(b, b, [bank[(6, 0)[b % 2] + half][:, :] for half in range(2)])
                for half in range(2):
                    cs = slice(half * 512, (half + 1) * 512)
                    dve.wait_ge(S["h1_norm"], 2 * b + half + 1)
                    then(v.tensor_tensor(n1[:, b, cs], n1[:, b, cs], lnr[:, 0, cs], ALU.mult))
                    v.tensor_tensor(n1[:, b, cs], n1[:, b, cs], lnr[:, 1, cs], ALU.add).then_inc(S["h1_half"], 1)
                dve.wait_ge(S["h1_turned"], 2 * b + 2)
                v.tensor_copy(h1T[:, 4:8, b * P:(b + 1) * P], bank[3][:, :].rearrange("p (k t) -> p k t", k=4)).then_inc(S["h1T_dve"], 1)
            then(v.memset(sel_zeros[:, 0:TB - 1, :], 0.0))

            b16 = lambda a: a.unsqueeze(2).broadcast_to([P, TB, NE])
            dve.wait_ge(S["rt_mm"], 1)
            lg_in = bank[4][:, 0:TB * NE].rearrange("p (b e) -> p b e", b=TB)
            then(v.tensor_reduce(lmax, lg_in, AX.X, ALU.max))
            v.tensor_tensor(lg, lg_in, b16(lmax), ALU.subtract).then_inc(S["rt_max"], 1)
            dve.wait_ge(S["rt_exp"], 1)
            then(v.tensor_reduce(lsum, lg, AX.X, ALU.add))
            then(v.reciprocal(lsum, lsum))
            then(v.tensor_tensor(prob, lg, b16(lsum), ALU.mult))
            then(v.tensor_tensor(score, prob, rowv[:, R_RB:R_RB + NE].unsqueeze(1).broadcast_to([P, TB, NE]), ALU.add))

            def ranks(dst, vals, n):
                other = vals.unsqueeze(2).broadcast_to([P, n, 4, 4])
                own = vals.unsqueeze(3).broadcast_to([P, n, 4, 4])
                low = lower.unsqueeze(1).broadcast_to([P, n, 4, 4])
                a, b = gt[:, 0:n], ge[:, 0:n]
                then(v.tensor_tensor(a, other, own, ALU.is_gt))
                then(v.tensor_tensor(b, other, own, ALU.is_equal))
                then(v.tensor_tensor(b, b, low, ALU.mult))
                then(v.tensor_tensor(a, a, b, ALU.add))
                then(v.tensor_reduce(dst, a, AX.X, ALU.add))

            by4 = lambda a: a.rearrange("p b (g i) -> p (b g) i", g=4)
            ranks(rank, by4(score), 4 * TB)
            then(v.tensor_scalar(by4(sel), rank, 1.5, None, ALU.is_lt))
            then(v.tensor_tensor(ssel, sel, score, ALU.mult))
            then(v.tensor_reduce(gsc.rearrange("p b g -> p (b g)"), by4(ssel), AX.X, ALU.add))
            ranks(grank, gsc, TB)
            then(v.tensor_scalar(ing, grank, 0.5, None, ALU.is_lt))
            v.tensor_tensor(by4(sel), by4(sel), ing.rearrange("p b g -> p (b g)").unsqueeze(2).broadcast_to([P, 4 * TB, 4]),
                            ALU.mult).then_inc(S["sel_done"], 1)
            dve.wait_ge(S["sel_done"], 1)
            then(v.tensor_tensor(ssel, sel, prob, ALU.mult))
            then(v.tensor_reduce(wden, ssel, AX.X, ALU.add))
            then(v.reciprocal(wden, wden))
            then(v.tensor_tensor(comb, ssel, b16(wden), ALU.mult))
            dve.wait_ge(S["pos_mm"], 1)
            then(v.tensor_reduce(cnt, bank[1][:, 64:128].rearrange("p (b e) -> p e b", b=TB), AX.X, ALU.add))
            then(v.tensor_copy(pos.rearrange("p b e -> p (b e)"), bank[1][:, 0:64]))
            then(v.tensor_tensor(thr_gt, cnt.unsqueeze(2).broadcast_to([P, NE, 3]), thr.unsqueeze(1).broadcast_to([P, NE, 3]), ALU.is_gt))
            then(v.tensor_reduce(spn, thr_gt, AX.X, ALU.add))
            then(v.tensor_tensor(big16, spn.unsqueeze(1).broadcast_to([P, NE, NE]), lower16, ALU.mult))
            then(v.tensor_reduce(spx, big16, AX.X, ALU.add))
            be = lambda a: a.unsqueeze(1).broadcast_to([P, TB, NE])
            then(v.tensor_scalar(over, pos, float(P), None, ALU.is_gt))
            then(v.tensor_tensor(cnt, spx, eoff, ALU.add))
            then(v.tensor_tensor(slot1, over, be(cnt), ALU.mult))
            then(v.tensor_tensor(slot1, slot1, be(eid), ALU.add))
            then(v.scalar_tensor_tensor(out=slot1, in0=slot1, scalar=float(P), in1=pos, op0=ALU.mult, op1=ALU.add))
            then(v.tensor_tensor(slot1, slot1, sel, ALU.mult))
            then(v.tensor_reduce(slot_a, slot1, AX.X, ALU.max))
            then(v.tensor_reduce(slot_b, slot1, AX.X, ALU.add))
            then(v.tensor_tensor(slot_b, slot_b, slot_a, ALU.subtract))
            then(v.tensor_scalar(slotf[:, :, 0], slot_a, -1.0, None, ALU.add))
            then(v.tensor_scalar(slotf[:, :, 1], slot_b, -1.0, None, ALU.add))
            v.tensor_copy(slot_no, slotf).then_inc(S["slots_done"], 1)
            then(v.tensor_tensor(spn, spx, spn, ALU.add))
            then(v.tensor_tensor(sp_le, spn.unsqueeze(1).broadcast_to([P, SPARE, NE]), spare_i.unsqueeze(2).broadcast_to([P, SPARE, NE]), ALU.is_le))
            then(v.tensor_reduce(spf[:, 0:SPARE], sp_le, AX.X, ALU.add))
            then(v.tensor_copy(spf[:, SPARE:SPARE + 1], spn[:, NE - 1:NE]))
            v.tensor_copy(spare_info, spf).then_inc(S["slots_done"], 1)
            then(v.tensor_tensor(over, slot1, b16(slot_a), ALU.is_equal))
            then(v.tensor_tensor(ssel, over, comb, ALU.mult))
            then(v.tensor_reduce(slot_wt[:, :, 0], ssel, AX.X, ALU.add))
            then(v.tensor_tensor(comb, comb, ssel, ALU.subtract))
            v.tensor_reduce(slot_wt[:, :, 1], comb, AX.X, ALU.add).then_inc(S["slots_done"], 1)
            dve.wait_ge(S["slots_done"], 3)

            def tokens_out(k, first=False):
                dve.wait_ge(S["x_turned"], k * 2 + 2)
                if not first:
                    dve.wait_ge(S["up_mm"], k * 2)
                v.tensor_copy(xgT[:, 4:8, :].rearrange("p k t -> p (k t)"), bank[3][:, :]).then_inc(S["xT_dve"], 1)

            def hidden(k, first=False):
                dve.wait_ge(S["up_silu"], k + 1)
                dve.wait_ge(S["up_mm"], k * 2 + 2)
                if not first:
                    dve.wait_ge(S["h_turned"], k)
                v.tensor_tensor(hidv, upv, bank[1][:, :], ALU.mult).then_inc(S["hid_done"], 1)

            def hidden_out(k, first=False):
                dve.wait_ge(S["h_turned"], k + 1)
                if not first:
                    dve.wait_ge(S["dn_mm"], k * 8)
                flat_hi = hidT_hi.rearrange("p f t -> p (f t)")
                v.tensor_copy(flat_hi, bank[4][:, :]).then_inc(S["hidT_done"], 1)
                dve.wait_ge(S["hidT_done"], k * 2 + 1)
                v.tensor_tensor(hidT_lo.rearrange("p f t -> p (f t)"), bank[4][:, :], flat_hi, ALU.subtract).then_inc(S["hidT_done"], 1)

            def w2_low(k, slot, units):
                for u in units:
                    dve.wait_ge(S["hi_done"], k * 8 + (HI_EXP + u + 1))
                    f, half = divmod(u, 2)
                    cs = slice(half * 512, (half + 1) * 512)
                    v.tensor_tensor(w2_lo[slot][:, f, cs], ew2[slot][:, f, cs], w2_hi[(8 * slot + u) % 3], ALU.subtract).then_inc(S["tile_lo"], 1)

            def out_half(k, first=False):
                dve.wait_ge(S["dn_mm"], k * 8 + 8)
                if not first:
                    dve.wait_ge(S["st_y"], k * 16)
                v.tensor_copy(eout[:, 512:D], bank[6][:, :]).then_inc(S["out_dve"], 1)

            def step(e, slot, last=False):
                first = isinstance(e, int) and e == 1
                hidden_out(e - 1, first=first)
                w2_low(e - 1, slot, range(3))
                hidden(e)
                if not last:
                    tokens_out(e + 1)
                w2_low(e - 1, slot, range(3, 8))
                out_half(e - 1, first=first)

            tokens_out(0, first=True)
            hidden(0, first=True)
            tokens_out(1)
            for d in (1, 2, 3):
                step(d, d - 1)
            with dve.Fori(1, (NE - 1) // 3 - 1) as i:
                for d in (1, 2, 3):
                    step(i * 3 + d, d - 1)
            for e in range(NE - 3, NE):
                step(e, (e - 1) % 3, last=(e == NE - 1))
            hidden_out(NE - 1)
            w2_low(NE - 1, 0, range(8))
            out_half(NE - 1)
            n_spare = dve.value_load(spare_info[0:1, SPARE:SPARE + 1], min_val=0, max_val=SPARE)
            with dve.Fori(0, SPARE) as i:
                with dve.If(i < n_spare):
                    tokens_out(i + NE)
                    hidden(i + NE)
                    hidden_out(i + NE)
                    w2_low(i + NE, 0, range(8))
                    out_half(i + NE)

            dve.wait_ge(S["h_scaled"], TB)

            def sum_up(b):
                dve.wait_ge(ld_back[b], 32)
                h, ya, yb = n1[:, b, :], by_token[:, b, 0, :], by_token[:, b, 1, :]
                if b < TB - 1:
                    dve.wait_ge(S["ya_added"], b + 1)
                else:
                    then(v.scalar_tensor_tensor(out=h, in0=ya, scalar=slot_wt[:, b, 0:1], in1=h, op0=ALU.mult, op1=ALU.add))
                then(v.scalar_tensor_tensor(out=h, in0=yb, scalar=slot_wt[:, b, 1:2], in1=h, op0=ALU.mult, op1=ALU.add))
                if b < TB - 1:
                    block_norm(TB + b, b, [h[:, 0:512], h[:, 512:D]])

            def times_g(b):
                dve.wait_ge(S["ln2_norm"], b + 1)
                v.tensor_tensor(n1[:, b, :], n1[:, b, :], lnr2[:, 0, :], ALU.mult).then_inc(S["ln2_g"], 1)

            dve.wait_ge(S["ld_ln"], 32)
            sum_up(0)
            for b in range(1, TB):
                sum_up(b)
                times_g(b - 1)
            b, h = TB - 1, n1[:, TB - 1, :]
            then(stats_of(b, [h[:, 0:512], h[:, 512:D]]))
            v.tensor_scalar(sdev[:, b:b + 1], mv[:, b, 1:2], LN_EPS, None, ALU.add).then_inc(S["ln_stat"], 1)
            then(v.scalar_tensor_tensor(out=h, in0=h, scalar=mv[:, b, 0:1], in1=lnr2[:, 0, :], op0=ALU.subtract, op1=ALU.mult))
            dve.wait_ge(S["ln_sd"], 2 * TB + 1)
            then(v.reciprocal(rstd[:, b:b + 1], sdev[:, b:b + 1]))
            v.scalar_tensor_tensor(out=obuf[:, b, :], in0=h, scalar=rstd[:, b:b + 1], in1=lnr2[:, 1, :],
                                   op0=ALU.mult, op1=ALU.add).then_inc(S["ln2_last"], 1)


def shape_constants():
    fixed = np.zeros((P, K_END), np.float32)
    fixed[:, K_ID:K_ID + P] = np.eye(P)
    s, l = np.arange(P)[:, None], np.arange(P)[None, :]
    fixed[:, K_TRI:K_TRI + P] = s <= l
    fixed[:, K_CAP:K_CAP + P] = np.where(s <= l, -NEG, NEG)
    fixed[:, K_AID:K_AID + P] = np.eye(P) * ALPHA
    fixed[:, K_ONE:K_ONE + P] = 1.0
    fixed[:, K_ROW] = np.arange(P) >= CMP_LEN - 1
    fixed[:, K_LOW:K_LOW + 16] = (np.arange(4)[None, :] < np.arange(4)[:, None]).reshape(-1)
    e = np.arange(NE)
    fixed[:, K_EID:K_EID + NE], fixed[:, K_EOFF:K_EOFF + NE] = e, NE - 1 - e
    fixed[:, K_THR:K_THR + 3], fixed[:, K_SPI:K_SPI + SPARE] = P * (np.arange(3) + 1), np.arange(SPARE)
    fixed[:, K_LOW16:K_LOW16 + NE * NE] = (e[None, :] < e[:, None]).reshape(-1)
    for g, w in enumerate(WINDOWS):
        fixed[:, K_INV + 16 * g:K_INV + 16 * (g + 1)] = 1.0 / np.minimum(np.arange(16) + 1, w)
    dist = T - 1 - np.arange(REVN)
    n = np.maximum(dist, 0)
    exact = BUCKETS // 2
    nf = np.maximum(n, 1).astype(np.float32)
    large = exact + (np.log(nf / np.float32(exact)) / np.float32(math.log(MAX_DIST / exact)) * np.float32(BUCKETS - exact)).astype(np.int32)
    bucket = np.where(n < exact, n, np.minimum(large, BUCKETS - 1))
    onehot = np.zeros((BUCKETS + 1, REVN), np.float32)
    onehot[np.where(dist < 0, BUCKETS, bucket), np.arange(REVN)] = 1.0
    return fixed, onehot


def kernel(**inputs):
    import concourse.bacc as bacc
    from concourse.bass_utils import run_bass_kernel_spmd

    a = {k: np.asarray(v) for k, v in inputs.items()}
    w_in = a["w_in"][0]
    c_pool, c_q, c_kv = 0, 512, 1024
    c_ng = c_kv + 768
    c_ssd = c_ng + 24
    c_gate = c_ssd + 3088

    def lhs(w):
        return w.reshape(KT, P, P).transpose(1, 0, 2).reshape(P, D)

    cols128 = lambda c: w_in[:, c:c + P]
    tiles = [cols128(c_kv), cols128(c_kv + P), cols128(c_kv + 2 * P), cols128(c_kv + 4 * P)]
    for i in range(HPG):
        tiles.append(np.concatenate([w_in[:, c_q + i * DH:c_q + (i + 1) * DH],
                                     w_in[:, c_q + (HPG + i) * DH:c_q + (HPG + i + 1) * DH]], axis=1))
    tiles += [cols128(c_pool + i * P) for i in range(4)]
    tiles += [cols128(c_ssd + D + i * P) for i in range(16)]
    assert len(tiles) == CM_PROJ

    def gates(j):
        return [cols128(c_gate + b * D + j * P) for b in range(3)]

    def branches(j):
        sl = slice(j * P, (j + 1) * P)
        return [np.concatenate([a["w_br_pool"][0][:, sl], a["w_br_nsa"][0][:, sl]], axis=0), a["w_br_ssd"][0][:, sl]]

    for j in range(EARLY):
        tiles += gates(j)
    for j in range(EARLY):
        tiles += branches(j)
    for j in range(EARLY, KT):
        tiles += gates(j) + branches(j)
    w_cm = np.stack([lhs(w) for w in tiles])

    def rhs(w):
        return w.reshape(-1, P, w.shape[1]).transpose(1, 0, 2)

    w_tm = np.stack([rhs(w_in[:, c_ssd + h * 512:c_ssd + (h + 1) * 512]) for h in range(2)])
    w_vd = rhs(np.concatenate([cols128(c_kv + 3 * P), cols128(c_kv + 5 * P), w_in[:, c_ssd + 3072:c_ssd + 3088],
                               w_in[:, c_ng:c_ng + 24]], axis=1))
    percol = lambda u: u.reshape(-1, P).T
    cols = np.concatenate([
        percol(a["ln0_g"]), percol(a["ln0_b"]), percol(a["ln1_g"][0]), percol(a["ln1_b"][0]), percol(a["pool_scale"][0]),
        percol(a["conv_w"][0].reshape(-1)), percol(a["conv_b"][0]), percol(a["ssd_norm_g"][0]),
        percol(a["cmp_k_pe"][0].reshape(-1)), percol(a["cmp_v_pe"][0].reshape(-1))], axis=1)
    rows = np.concatenate([a["dt_bias"][0], a["a_log"][0], a["d_skip"][0], a["router_b"]])[None]
    fixed, onehot = shape_constants()
    table = np.concatenate([a["rel_bias"], np.full((1, HEADS), NEG, np.float32)], axis=0)
    e13 = np.stack([a["exp_w1"][0], a["exp_w3"][0]], axis=1).reshape(NE, 2, KT, P, DE).transpose(0, 3, 1, 2, 4)
    arrays = {
        "x": a["x"][0], "w_cm": w_cm, "w_tm": w_tm, "w_vd": w_vd, "cols": cols, "rows": rows,
        "lnrows": np.stack([a["ln1_g"][0], a["ln1_b"][0], a["ln2_g"][0], a["ln2_b"][0]]), "fixed": fixed, "onehot": onehot, "table": table,
        "pool_w": a["pool_w"][0].transpose(1, 0, 2),
        "w1c_in": np.stack([rhs(a["cmp_k_w1"][0]), rhs(a["cmp_v_w1"][0])], axis=1),
        "w2kv": np.stack([a["cmp_k_w2"][0], a["cmp_v_w2"][0]], axis=1),
        "w_out": np.stack([rhs(a["w_out"][0][:, h * 512:(h + 1) * 512]) for h in range(2)]),
        "w_rt": rhs(a["router_w"]),
        "e13": e13, "e2": a["exp_w2"][0].reshape(NE, FT, P, D).transpose(0, 2, 1, 3),
    }
    nc = bacc.Bacc("TRN2", target_bir_lowering=False, num_devices=1)
    handles = {}
    for name in arrays:
        arrays[name] = np.ascontiguousarray(arrays[name])
        handles[name] = nc.dram_tensor(f"in_{name}", arrays[name].shape, F32, kind="ExternalInput").ap()
    out = nc.dram_tensor("out", (T, D), F32, kind="ExternalOutput").ap()
    bias_dram = nc.dram_tensor("bias_rows", (HEADS, P * (REVN + 1)), F32, kind="Internal").ap()
    xs_dram, ys_dram = (nc.dram_tensor(n, ((NE + SPARE) * P, D), F32, kind="Internal").ap() for n in ("slots_in", "slots_out"))
    build_program(nc, out=out, bias_dram=bias_dram, xs_dram=xs_dram, ys_dram=ys_dram, **handles)
    r = run_bass_kernel_spmd(nc, [{f"in_{k}": v for k, v in arrays.items()}], core_ids=[0])
    return r.results[0]["out"].reshape(1, T, D)
```
